# Optimizing a Trainium2 kernel written in Bass

```python
import math
import jax, jax.numpy as jnp
from jax import lax
import numpy as np
import jax
import jax.numpy as jnp

D_MODEL = 1024
BATCH = 1
SEQ = 256
DEPTH = 4

N_MIXERS = 3
EPS = 1e-6
D_FF = -(-8 * D_MODEL // (3 * 256)) * 256
FOURIER_GROUP = 128
N_FOURIER_GROUPS = D_MODEL // FOURIER_GROUP
S5_GROUP = 16
S5_GROUPS = D_MODEL // S5_GROUP
S5_STATE = 64
S5_DT_MIN = 1e-3
S5_DT_MAX = 1e-1
HEAD_DIM = 64
HEADS_PER_GROUP = D_MODEL // HEAD_DIM
DILATED_GROUPS = ((128, 1), (512, 4), (2048, 16))
N_ATTN_GROUPS = len(DILATED_GROUPS)
N_ATTN_HEADS = N_ATTN_GROUPS * HEADS_PER_GROUP
QKV_WIDTH = N_ATTN_GROUPS * 3 * HEADS_PER_GROUP * HEAD_DIM
ATTN_OUT = HEADS_PER_GROUP * HEAD_DIM
NUM_BUCKETS = 32
MAX_DISTANCE = 1024
N_LAYERS_A = (DEPTH + 2) // 3
N_LAYERS_B = (DEPTH + 1) // 3
N_LAYERS_C = DEPTH // 3


def rms_norm(x, g):
    xf = x.astype(jnp.float32)
    y = xf * lax.rsqrt(jnp.mean(xf * xf, axis=-1, keepdims=True) + EPS)
    return (y * g.astype(jnp.float32)).astype(x.dtype)

def swiglu(h, w_gate_up, w_down):
    gate, up = jnp.split(h @ w_gate_up, 2, axis=-1)
    return (jax.nn.silu(gate) * up) @ w_down

def fourier_mixer(h, w_out):
    b, s, d = h.shape
    hg = h.astype(jnp.float32).reshape(b, s, N_FOURIER_GROUPS, FOURIER_GROUP)
    f = jnp.fft.fft2(hg, axes=(1, 3), norm="ortho").real
    return f.reshape(b, s, d).astype(h.dtype) @ w_out

def _s5_direction(u, lam_re, lam_im, log_dt, b_re, b_im, c_re, c_im, reverse):
    f32 = jnp.float32
    lam = lax.complex(lam_re.astype(f32), lam_im.astype(f32))
    dt = jnp.exp(log_dt.astype(f32))[:, None]
    lam_bar = jnp.exp(lam * dt)
    b_bar = ((lam_bar - 1.0) / lam)[..., None] * lax.complex(b_re.astype(f32), b_im.astype(f32))
    bu = lax.complex(jnp.einsum('bsgp,gnp->bsgn', u, b_bar.real),
                     jnp.einsum('bsgp,gnp->bsgn', u, b_bar.imag))
    a = jnp.broadcast_to(lam_bar, bu.shape)

    def combine(e1, e2):
        a1, x1 = e1
        a2, x2 = e2
        return a1 * a2, a2 * x1 + x2

    _, hs = lax.associative_scan(combine, (a, bu), axis=1, reverse=reverse)
    c = lax.complex(c_re.astype(f32), c_im.astype(f32))
    return jnp.einsum('gpn,bsgn->bsgp', c, hs).real

def s5_mixer(h, lam_re, lam_im, log_dt, b_re, b_im, c_re, c_im, d_skip, w_glu):
    b, s, d = h.shape
    hf = h.astype(jnp.float32)
    u = hf.reshape(b, s, S5_GROUPS, S5_GROUP)
    y_fwd = _s5_direction(u, lam_re[0], lam_im[0], log_dt[0], b_re[0], b_im[0], c_re[0], c_im[0], False)
    y_bwd = _s5_direction(u, lam_re[1], lam_im[1], log_dt[1], b_re[1], b_im[1], c_re[1], c_im[1], True)
    y = (y_fwd + y_bwd).reshape(b, s, d) + d_skip.astype(jnp.float32) * hf
    g = jax.nn.gelu(y).astype(h.dtype)
    val, gate = jnp.split(g @ w_glu, 2, axis=-1)
    return val * jax.nn.sigmoid(gate)

def t5_bucket(rel):
    half = NUM_BUCKETS // 2
    max_exact = half // 2
    n = np.abs(rel)
    sign = (rel > 0).astype(np.int32) * half
    large = max_exact + (np.log(np.maximum(n, 1) / max_exact) / math.log(MAX_DISTANCE / max_exact)
                         * (half - max_exact)).astype(np.int32)
    large = np.minimum(large, half - 1)
    return (sign + np.where(n < max_exact, n, large)).astype(np.int32)

def head_rms_norm(t, g):
    tf = t.astype(jnp.float32)
    y = tf * lax.rsqrt(jnp.mean(tf * tf, axis=-1, keepdims=True) + EPS)
    return (y * g.astype(jnp.float32)).astype(t.dtype)

def dilated_group_attention(q, k, v, bias_g, dil, n_side):
    bsz, s, nh, e = q.shape
    seg = s // dil
    blk = n_side
    nb = -(-seg // blk)
    segp = nb * blk

    def res(t):
        return t.reshape(bsz, seg, dil, nh, e).transpose(0, 2, 1, 3, 4)

    qb = jnp.pad(res(q), ((0, 0), (0, 0), (0, segp - seg), (0, 0), (0, 0))).reshape(bsz, dil, nb, blk, nh, e)

    def kv_blocks(t):
        tp = jnp.pad(res(t), ((0, 0), (0, 0), (blk, segp - seg + blk), (0, 0), (0, 0)))
        tp = tp.reshape(bsz, dil, nb + 2, blk, nh, e)
        return jnp.concatenate([tp[:, :, :-2], tp[:, :, 1:-1], tp[:, :, 2:]], axis=3)

    kb = kv_blocks(k)
    vb = kv_blocks(v)
    qi = np.arange(blk)[:, None]
    ki = np.arange(3 * blk)[None, :]
    off = ki - blk - qi
    band = np.abs(off) <= n_side
    key_idx = np.arange(nb)[:, None] * blk + np.arange(3 * blk)[None, :] - blk
    in_range = (key_idx >= 0) & (key_idx < seg)
    allowed = band[None] & in_range[:, None, :]
    buckets = t5_bucket(off * dil)
    bias = jnp.transpose(bias_g.astype(jnp.float32)[buckets], (2, 0, 1))

    sc = jnp.einsum('brnqhe,brnkhe->brnhqk', qb, kb, preferred_element_type=jnp.float32) * (e ** -0.5)
    sc = jnp.where(allowed[None, None, :, None], sc + bias, -1e30)
    m = jnp.max(sc, axis=-1, keepdims=True)
    p = jnp.exp(sc - m)
    den = jnp.sum(p, axis=-1, keepdims=True)
    o = jnp.einsum('brnhqk,brnkhe->brnqhe', (p / den).astype(v.dtype), vb)
    lse = (m + jnp.log(den))[..., 0]
    o = o.reshape(bsz, dil, segp, nh, e)[:, :, :seg].transpose(0, 2, 1, 3, 4).reshape(bsz, s, nh, e)
    lse = lse.transpose(0, 1, 2, 4, 3).reshape(bsz, dil, segp, nh)[:, :, :seg]
    lse = lse.transpose(0, 2, 1, 3).reshape(bsz, s, nh)
    return o, lse

def dilated_attention_mixer(h, w_qkv, q_gain, k_gain, w_o, rel_bias):
    b, s, d = h.shape
    qkv = (h @ w_qkv).reshape(b, s, N_ATTN_GROUPS, 3, HEADS_PER_GROUP, HEAD_DIM)
    outs = []
    lses = []
    for g, (window, dil) in enumerate(DILATED_GROUPS):
        q = head_rms_norm(qkv[:, :, g, 0], q_gain[g])
        k = head_rms_norm(qkv[:, :, g, 1], k_gain[g])
        v = qkv[:, :, g, 2]
        bias_g = rel_bias[:, g * HEADS_PER_GROUP:(g + 1) * HEADS_PER_GROUP]
        o, l = dilated_group_attention(q, k, v, bias_g, dil, (window // 2) // dil)
        outs.append(o)
        lses.append(l)
    wts = jax.nn.softmax(jnp.stack(lses, axis=0), axis=0)
    o = jnp.einsum('gbsh,gbshe->bshe', wts, jnp.stack(outs, axis=0).astype(jnp.float32))
    return o.reshape(b, s, ATTN_OUT).astype(h.dtype) @ w_o

def first_inputs(seed: int = 0) -> dict:
    key = jax.random.key(seed)
    ks = jax.random.split(key, 24)
    f32 = jnp.float32
    d = D_MODEL

    def nrm(k, shape, scale):
        return jax.random.normal(k, shape, f32) * scale

    s5_shape = (N_LAYERS_B, 2, S5_GROUPS, S5_STATE)
    n_idx = jnp.arange(S5_STATE, dtype=f32)
    return {
        "x": nrm(ks[0], (BATCH, SEQ, d), 1.0),
        "norm_mix_g": 1.0 + nrm(ks[1], (DEPTH, d), 0.1),
        "norm_ffn_g": 1.0 + nrm(ks[2], (DEPTH, d), 0.1),
        "fnet_w_out": nrm(ks[3], (N_LAYERS_A, d, d), d ** -0.5),
        "s5_lambda_re": -0.5 + nrm(ks[4], s5_shape, 0.01),
        "s5_lambda_im": math.pi * n_idx + nrm(ks[5], s5_shape, 0.01),
        "s5_log_dt": jax.random.uniform(ks[6], (N_LAYERS_B, 2, S5_GROUPS), f32,
                                        math.log(S5_DT_MIN), math.log(S5_DT_MAX)),
        "s5_b_re": nrm(ks[7], (N_LAYERS_B, 2, S5_GROUPS, S5_STATE, S5_GROUP), (2 * S5_GROUP) ** -0.5),
        "s5_b_im": nrm(ks[8], (N_LAYERS_B, 2, S5_GROUPS, S5_STATE, S5_GROUP), (2 * S5_GROUP) ** -0.5),
        "s5_c_re": nrm(ks[9], (N_LAYERS_B, 2, S5_GROUPS, S5_GROUP, S5_STATE), S5_STATE ** -0.5),
        "s5_c_im": nrm(ks[10], (N_LAYERS_B, 2, S5_GROUPS, S5_GROUP, S5_STATE), S5_STATE ** -0.5),
        "s5_d": nrm(ks[11], (N_LAYERS_B, d), 1.0),
        "s5_w_glu": nrm(ks[12], (N_LAYERS_B, d, 2 * d), d ** -0.5),
        "attn_w_qkv": nrm(ks[13], (N_LAYERS_C, d, QKV_WIDTH), d ** -0.5),
        "attn_q_gain": 1.0 + nrm(ks[14], (N_LAYERS_C, N_ATTN_GROUPS, HEAD_DIM), 0.1),
        "attn_k_gain": 1.0 + nrm(ks[15], (N_LAYERS_C, N_ATTN_GROUPS, HEAD_DIM), 0.1),
        "attn_w_o": nrm(ks[16], (N_LAYERS_C, ATTN_OUT, d), ATTN_OUT ** -0.5),
        "rel_bias": nrm(ks[17], (NUM_BUCKETS, N_ATTN_HEADS), 0.5),
        "ffn_w_gate_up": nrm(ks[18], (DEPTH, d, 2 * D_FF), d ** -0.5),
        "ffn_w_down": nrm(ks[19], (DEPTH, D_FF, d), D_FF ** -0.5),
    }

def first_block(x, norm_mix_g, norm_ffn_g, fnet_w_out, s5_lambda_re, s5_lambda_im, s5_log_dt,
              s5_b_re, s5_b_im, s5_c_re, s5_c_im, s5_d, s5_w_glu, attn_w_qkv, attn_q_gain,
              attn_k_gain, attn_w_o, rel_bias, ffn_w_gate_up, ffn_w_down):
    counts = [0, 0, 0]
    for i in range(DEPTH):
        kind = i % N_MIXERS
        j = counts[kind]
        counts[kind] += 1
        h = rms_norm(x, norm_mix_g[i])
        if kind == 0:
            mix = fourier_mixer(h, fnet_w_out[j])
        elif kind == 1:
            mix = s5_mixer(h, s5_lambda_re[j], s5_lambda_im[j], s5_log_dt[j], s5_b_re[j], s5_b_im[j],
                           s5_c_re[j], s5_c_im[j], s5_d[j], s5_w_glu[j])
        else:
            mix = dilated_attention_mixer(h, attn_w_qkv[j], attn_q_gain[j], attn_k_gain[j],
                                          attn_w_o[j], rel_bias)
        x = x + mix.astype(x.dtype)
        h = rms_norm(x, norm_ffn_g[i])
        x = x + swiglu(h, ffn_w_gate_up[i], ffn_w_down[i]).astype(x.dtype)
    return x


DEPTH_2 = 2

SSD_HEADS = 16
SSD_HEAD_DIM = 64
D_SSD = SSD_HEADS * SSD_HEAD_DIM
SSD_GROUPS = 2
SSD_STATE = 128
SSD_CONV = 4
SSD_CHUNK = 256
CONV_DIM = D_SSD + 2 * SSD_GROUPS * SSD_STATE
ATT_HEADS = 8
ATT_HEAD_DIM = 128
D_ATT = ATT_HEADS * ATT_HEAD_DIM
IDX_HEADS = 8
IDX_HEAD_DIM = 64
TOPK_MAX = 256
Q_BLOCK = 128
ROPE_THETA = 500000.0
ATT_ROPE_DIM = ATT_HEAD_DIM // 4
IDX_ROPE_DIM = IDX_HEAD_DIM // 4
D_MIX = D_SSD + D_ATT
D_FF_2 = 2816
MIX_SPLITS = (D_SSD, CONV_DIM, SSD_HEADS, D_ATT, D_ATT, D_ATT,
              IDX_HEADS * IDX_HEAD_DIM, IDX_HEAD_DIM, IDX_HEADS)
SPLIT_POINTS = tuple(int(p) for p in np.cumsum(MIX_SPLITS)[:-1])
D_IN_PROJ = sum(MIX_SPLITS)


def rmsnorm(x, g):
    xf = x.astype(jnp.float32)
    y = xf * lax.rsqrt(jnp.mean(xf * xf, axis=-1, keepdims=True) + EPS)
    return (y * g.astype(jnp.float32)).astype(x.dtype)

def swiglu_ffn(x, w_in, w_out):
    gate, up = jnp.split(x @ w_in, 2, axis=-1)
    return (jax.nn.silu(gate) * up) @ w_out

def partial_rope(x, positions, rot_dim):
    inv_freq = ROPE_THETA ** (-jnp.arange(0, rot_dim, 2, dtype=jnp.float32) / rot_dim)
    ang = positions.astype(jnp.float32)[..., None] * inv_freq
    cos = jnp.cos(ang)[:, :, None, :]
    sin = jnp.sin(ang)[:, :, None, :]
    xr = x[..., :rot_dim].astype(jnp.float32)
    x1, x2 = jnp.split(xr, 2, axis=-1)
    rot = jnp.concatenate([x1 * cos - x2 * sin, x2 * cos + x1 * sin], axis=-1)
    return jnp.concatenate([rot.astype(x.dtype), x[..., rot_dim:]], axis=-1)

def causal_dwconv(x, w, b):
    k = w.shape[0]
    y = lax.conv_general_dilated(x, w[:, None, :].astype(x.dtype), window_strides=(1,),
                                 padding=[(k - 1, 0)],
                                 dimension_numbers=('NWC', 'WIO', 'NWC'),
                                 feature_group_count=x.shape[-1])
    return y + b.astype(x.dtype)

def segsum_exp(a):
    l = a.shape[-1]
    cs = jnp.cumsum(a, axis=-1)
    seg = cs[..., :, None] - cs[..., None, :]
    mask = jnp.tril(jnp.ones((l, l), dtype=bool))
    return jnp.exp(jnp.where(mask, seg, -jnp.inf))

def ssd_chunked(xh, dt, a, bmat, cmat, chunk):
    bsz, L, H, P = xh.shape
    G, N = bmat.shape[-2:]
    E = H // G
    nc = L // chunk
    x = (xh.astype(jnp.float32) * dt[..., None]).reshape(bsz, nc, chunk, G, E, P)
    adt = jnp.moveaxis((dt * a).reshape(bsz, nc, chunk, G, E), 2, -1)
    a_cs = jnp.cumsum(adt, axis=-1)
    bc = bmat.astype(jnp.float32).reshape(bsz, nc, chunk, G, N)
    cc = cmat.astype(jnp.float32).reshape(bsz, nc, chunk, G, N)
    decay = segsum_exp(adt)
    cb = jnp.einsum('bclgn,bcsgn->bcgls', cc, bc)
    y_diag = jnp.einsum('bcgls,bcgels,bcsgep->bclgep', cb, decay, x)
    decay_states = jnp.exp(a_cs[..., -1:] - a_cs)
    states = jnp.einsum('bclgn,bcgel,bclgep->bcgepn', bc, decay_states, x)
    chunk_decay = jnp.exp(a_cs[..., -1])

    def step(h, inp):
        st, dec = inp
        return h * dec[..., None, None] + st, h

    h0 = jnp.zeros((bsz, G, E, P, N), jnp.float32)
    _, h_in = lax.scan(step, h0, (jnp.moveaxis(states, 1, 0), jnp.moveaxis(chunk_decay, 1, 0)))
    h_in = jnp.moveaxis(h_in, 0, 1)
    y_off = jnp.einsum('bclgn,bcgepn,bcgel->bclgep', cc, h_in, jnp.exp(a_cs))
    return (y_diag + y_off).reshape(bsz, L, H, P)

def ssd_mixer(z, xbc, dt_raw, conv_w, conv_b, dt_bias, a_log, d_skip, norm_g):
    bsz, L, _ = z.shape
    xbc = jax.nn.silu(causal_dwconv(xbc, conv_w, conv_b))
    xs, bm, cm = jnp.split(xbc, [D_SSD, D_SSD + SSD_GROUPS * SSD_STATE], axis=-1)
    xh = xs.reshape(bsz, L, SSD_HEADS, SSD_HEAD_DIM)
    bm = bm.reshape(bsz, L, SSD_GROUPS, SSD_STATE)
    cm = cm.reshape(bsz, L, SSD_GROUPS, SSD_STATE)
    dt = jax.nn.softplus(dt_raw.astype(jnp.float32) + dt_bias.astype(jnp.float32))
    a = -jnp.exp(a_log.astype(jnp.float32))
    chunk = math.gcd(SSD_CHUNK, L)
    y = ssd_chunked(xh, dt, a, bm, cm, chunk)
    y = y + xh.astype(jnp.float32) * d_skip.astype(jnp.float32)[:, None]
    y = y.reshape(bsz, L, D_SSD) * jax.nn.silu(z.astype(jnp.float32))
    yg = y.reshape(bsz, L, SSD_GROUPS, D_SSD // SSD_GROUPS)
    yg = yg * lax.rsqrt(jnp.mean(yg * yg, axis=-1, keepdims=True) + EPS)
    return (yg.reshape(bsz, L, D_SSD) * norm_g.astype(jnp.float32)).astype(z.dtype)

def dsa_mixer(q, k, v, q_idx, k_idx, w_idx, positions):
    bsz, L, _ = q.shape
    q = partial_rope(q.reshape(bsz, L, ATT_HEADS, ATT_HEAD_DIM), positions, ATT_ROPE_DIM)
    k = partial_rope(k.reshape(bsz, L, ATT_HEADS, ATT_HEAD_DIM), positions, ATT_ROPE_DIM)
    v = v.reshape(bsz, L, ATT_HEADS, ATT_HEAD_DIM)
    qi = partial_rope(q_idx.reshape(bsz, L, IDX_HEADS, IDX_HEAD_DIM), positions, IDX_ROPE_DIM)
    ki = partial_rope(k_idx[:, :, None, :], positions, IDX_ROPE_DIM)[:, :, 0].astype(jnp.float32)
    wi = w_idx.astype(jnp.float32) * IDX_HEADS ** -0.5
    topk = min(TOPK_MAX, L // 4)
    n_blocks = L // Q_BLOCK
    key_pos = jnp.arange(L)
    att_scale = ATT_HEAD_DIM ** -0.5
    idx_scale = IDX_HEAD_DIM ** -0.5

    def block(i):
        start = i * Q_BLOCK
        qb = lax.dynamic_slice_in_dim(q, start, Q_BLOCK, axis=1)
        qib = lax.dynamic_slice_in_dim(qi, start, Q_BLOCK, axis=1)
        wb = lax.dynamic_slice_in_dim(wi, start, Q_BLOCK, axis=1)
        t = start + jnp.arange(Q_BLOCK)
        causal = key_pos[None, :] <= t[:, None]
        logit_idx = jnp.einsum('bthd,bsd->bths', qib.astype(jnp.float32), ki) * idx_scale
        score = jnp.einsum('bth,bths->bts', wb, jax.nn.relu(logit_idx))
        score = jnp.where(causal[None], score, -jnp.inf)
        _, sel = lax.top_k(score, topk)
        k_sel = jax.vmap(lambda kb, ib: kb[ib])(k, sel)
        v_sel = jax.vmap(lambda vb, ib: vb[ib])(v, sel)
        valid = sel <= t[None, :, None]
        s = jnp.einsum('bthd,btkhd->bhtk', qb.astype(jnp.float32),
                       k_sel.astype(jnp.float32)) * att_scale
        s = jnp.where(valid[:, None], s, -jnp.inf)
        p = jax.nn.softmax(s, axis=-1)
        o = jnp.einsum('bhtk,btkhd->bthd', p, v_sel.astype(jnp.float32))
        return o.astype(q.dtype)

    out = lax.map(block, jnp.arange(n_blocks))
    return jnp.moveaxis(out, 0, 1).reshape(bsz, L, D_ATT)

def second_inputs(seed: int = 0) -> dict:
    key = jax.random.key(seed)
    ks = jax.random.split(key, 20)
    f32 = jnp.float32

    def dense(k, shape, fan_in):
        return jax.random.normal(k, shape, f32) * fan_in ** -0.5

    def gain(k, shape):
        return 1.0 + 0.02 * jax.random.normal(k, shape, f32)

    x = jax.random.normal(ks[0], (BATCH, SEQ, D_MODEL), f32)
    offset = jax.random.randint(ks[1], (BATCH, 1), 0, 1024, dtype=jnp.int32)
    positions = (offset + jnp.arange(SEQ, dtype=jnp.int32)[None, :]).astype(jnp.int32)
    dt0 = jnp.exp(jax.random.uniform(ks[10], (DEPTH_2, SSD_HEADS), f32,
                                     minval=math.log(1e-3), maxval=math.log(1e-1)))
    dt_bias = dt0 + jnp.log(-jnp.expm1(-dt0))
    a_log = jnp.log(jax.random.uniform(ks[11], (DEPTH_2, SSD_HEADS), f32, minval=1.0, maxval=16.0))
    return {
        'x': x,
        'positions': positions,
        'norm_ffn1': gain(ks[2], (DEPTH_2, D_MODEL)),
        'w_ffn1_in': dense(ks[3], (DEPTH_2, D_MODEL, 2 * D_FF_2), D_MODEL),
        'w_ffn1_out': dense(ks[4], (DEPTH_2, D_FF_2, D_MODEL), D_FF_2),
        'norm_mix': gain(ks[5], (DEPTH_2, D_MODEL)),
        'w_mix_in': dense(ks[6], (DEPTH_2, D_MODEL, D_IN_PROJ), D_MODEL),
        'conv_w': dense(ks[7], (DEPTH_2, SSD_CONV, CONV_DIM), SSD_CONV),
        'conv_b': 0.02 * jax.random.normal(ks[8], (DEPTH_2, CONV_DIM), f32),
        'dt_bias': dt_bias,
        'a_log': a_log,
        'd_skip': 1.0 + 0.1 * jax.random.normal(ks[9], (DEPTH_2, SSD_HEADS), f32),
        'ssd_norm': gain(ks[12], (DEPTH_2, D_SSD)),
        'w_mix_out': dense(ks[13], (DEPTH_2, D_MIX, D_MODEL), D_MIX),
        'norm_ffn2': gain(ks[14], (DEPTH_2, D_MODEL)),
        'w_ffn2_in': dense(ks[15], (DEPTH_2, D_MODEL, 2 * D_FF_2), D_MODEL),
        'w_ffn2_out': dense(ks[16], (DEPTH_2, D_FF_2, D_MODEL), D_FF_2),
        'final_norm': gain(ks[17], (D_MODEL,)),
    }

def second_block(x, positions, norm_ffn1, w_ffn1_in, w_ffn1_out, norm_mix, w_mix_in,
              conv_w, conv_b, dt_bias, a_log, d_skip, ssd_norm, w_mix_out,
              norm_ffn2, w_ffn2_in, w_ffn2_out, final_norm):
    h = x
    for i in range(DEPTH_2):
        h = h + 0.5 * swiglu_ffn(rmsnorm(h, norm_ffn1[i]), w_ffn1_in[i], w_ffn1_out[i])
        u = rmsnorm(h, norm_mix[i]) @ w_mix_in[i]
        z, xbc, dt_raw, q, k, v, q_idx, k_idx, w_idx = jnp.split(u, SPLIT_POINTS, axis=-1)
        y_ssd = ssd_mixer(z, xbc, dt_raw, conv_w[i], conv_b[i], dt_bias[i], a_log[i],
                          d_skip[i], ssd_norm[i])
        y_att = dsa_mixer(q, k, v, q_idx, k_idx, w_idx, positions)
        h = h + jnp.concatenate([y_ssd, y_att], axis=-1) @ w_mix_out[i]
        h = h + 0.5 * swiglu_ffn(rmsnorm(h, norm_ffn2[i]), w_ffn2_in[i], w_ffn2_out[i])
    return rmsnorm(h, final_norm)


def setup_inputs(seed=0):
    out = dict(first_inputs(seed))
    for name, value in second_inputs(seed + 1).items():
        if name != "x":
            out[name + "_2"] = value
    return out


def reference(
    x, norm_mix_g, norm_ffn_g, fnet_w_out, s5_lambda_re, s5_lambda_im, s5_log_dt, s5_b_re,
    s5_b_im, s5_c_re, s5_c_im, s5_d, s5_w_glu, attn_w_qkv, attn_q_gain, attn_k_gain, attn_w_o,
    rel_bias, ffn_w_gate_up, ffn_w_down, positions_2, norm_ffn1_2, w_ffn1_in_2, w_ffn1_out_2,
    norm_mix_2, w_mix_in_2, conv_w_2, conv_b_2, dt_bias_2, a_log_2, d_skip_2, ssd_norm_2,
    w_mix_out_2, norm_ffn2_2, w_ffn2_in_2, w_ffn2_out_2, final_norm_2,
):
    x = first_block(
        x, norm_mix_g, norm_ffn_g, fnet_w_out, s5_lambda_re, s5_lambda_im, s5_log_dt, s5_b_re,
        s5_b_im, s5_c_re, s5_c_im, s5_d, s5_w_glu, attn_w_qkv, attn_q_gain, attn_k_gain,
        attn_w_o, rel_bias, ffn_w_gate_up, ffn_w_down,
    )
    return second_block(
        x, positions_2, norm_ffn1_2, w_ffn1_in_2, w_ffn1_out_2, norm_mix_2, w_mix_in_2,
        conv_w_2, conv_b_2, dt_bias_2, a_log_2, d_skip_2, ssd_norm_2, w_mix_out_2, norm_ffn2_2,
        w_ffn2_in_2, w_ffn2_out_2, final_norm_2,
    )


_drawn_inputs = setup_inputs


def setup_inputs(seed=0):
    import zlib

    import numpy as np

    out = dict(_drawn_inputs(seed))
    spreads = {}
    factors = {'s5_lambda_re': 34.821,
     'attn_q_gain': 4.033,
     'attn_k_gain': 4.183,
     'norm_ffn1_2': 5.644,
     'norm_mix_2': 2.824,
     'conv_b_2': 11.276,
     'ssd_norm_2': 19.682,
     'norm_ffn2_2': 7.997,
     'final_norm_2': 8.055,
     'd_skip_2': 8.0}
    for name, (base, spread) in spreads.items():
        noise = np.random.default_rng([zlib.crc32(name.encode()), seed]).standard_normal(out[name].shape)
        drawn = base * np.exp(spread * noise) if base else spread * noise
        out[name] = jnp.asarray(drawn.astype(out[name].dtype))
    for name, factor in factors.items():
        out[name] = (out[name] * factor).astype(out[name].dtype)
    return out
```

```python
from contextlib import ExitStack

import numpy as np
import concourse.bass as bass
from concourse import mybir
from concourse.alu_op_type import AluOpType as ALU

F32 = mybir.dt.float32
F32R = mybir.dt.float32r
ACT = mybir.ActivationFunctionType
AX = mybir.AxisListType

P = 128
D = 1024
S = 256
KT = D // P
FF = 2816
COLS = 256
PANEL = KT * COLS
FFC = FF // COLS
SLOTS = 3
PROJ_BANKS = 4
EPS = 1e-6
TWO_PI = 2 * np.pi
TWO_PI_1 = 6.28125
TWO_PI_2 = float(np.float32(1.93500518798828125e-3))
TWO_PI_3 = TWO_PI - TWO_PI_1 - TWO_PI_2
ROUND = 1.5 * 2.0 ** 23
PI_BELOW = float(np.nextafter(np.float32(np.pi), np.float32(0)))
MASKED = -1e30
HEADS = 16
E = 64
GROUPS = ((128, 1), (512, 4), (2048, 16))
NG = len(GROUPS)
BUCKETS = 32
MAX_DISTANCE = 1024
HB = 4
SSD_H = 16
SSD_P = 64
SSD_G = 2
SSD_N = 128
CONV = 4
CONV_T = (SSD_H * SSD_P + 2 * SSD_G * SSD_N) // P
ATT_H = 8
IDX_H = 8
TOPK = min(256, S // 4)
ROPE_THETA = 500000.0
ROPE_D = P // 4
ROPE_I = E // 4
TAKEN = -3e38
LOG_TERMS = 8
S5_T = 8
S5_C = S // S5_T
S5_P = 16
S5_N = 64
S5_G = D // S5_P
BLOCK1 = 4
BLOCK2 = 2


def plan_stages():
    stages = []
    panel = xr = norm = ffn = 0
    mixers = ["fourier", "s5", "dilated", "fourier"]
    todo = []
    for i in range(BLOCK1):
        todo += [("norm", i), (mixers[i], i), ("norm", BLOCK1 + i), ("ffn", i)]
    for i in range(BLOCK2):
        b = 2 * BLOCK1 + 3 * i
        todo += [("norm", b), ("ffn", BLOCK1 + 2 * i), ("norm", b + 1), ("mix", i),
                 ("norm", b + 2), ("ffn", BLOCK1 + 2 * i + 1)]
    todo.append(("final", 2 * BLOCK1 + 3 * BLOCK2))
    panels_of = {"fourier": 4, "s5": 8, "dilated": 40, "ffn": 3 * FFC, "mix": 25 + 8}
    for kind, i in todo:
        st = {"kind": kind, "i": i, "n0": panel, "xr": xr}
        if kind in ("norm", "final"):
            st["norm"] = norm
            norm += 1
        else:
            xr += 4
            panel += panels_of[kind]
        st["hn"] = norm - 1
        if kind == "ffn":
            st["ffn"] = ffn
            ffn += 1
        stages.append(st)
    return stages, panel


def build(nc, A, out, stop=None):
    stages, n_panels = plan_stages()
    if stop is not None:
        stages = stages[:stop]
    final = stages[-1]["kind"] == "final"

    with ExitStack() as ctx:
        def sb(name, shape, dt=F32):
            return ctx.enter_context(nc.sbuf_tensor(name, shape, dt))

        def sem(name):
            return ctx.enter_context(nc.semaphore(name))

        raw = sb("raw", [P, SLOTS, PANEL])
        w_hi = sb("w_hi", [P, SLOTS, PANEL], F32R)
        w_lo = sb("w_lo", [P, SLOTS, PANEL], F32R)
        x = sb("x", [P, KT, S])
        h = sb("h", [P, KT, S])
        h_hi = sb("h_hi", [P, KT, S], F32R)
        h_lo = sb("h_lo", [P, KT, S], F32R)
        rstd = sb("rstd", [P, S])
        gains = sb("gains", [P, A["gains"].shape[1]])
        ones = sb("ones", [P, P])
        zeros = sb("zeros", [P, P], F32R)
        eps = sb("eps", [P, 1])
        hidden = sb("hidden", [P, 2, 2, 2, S])
        gate, act = hidden[:, 0], hidden[:, 1]
        act_hi = sb("act_hi", [P, 2, 2, S], F32R)
        act_lo = sb("act_lo", [P, 2, 2, S], F32R)
        ident = sb("ident", [P, P])
        rope = sb("rope", [P, 4, S])
        arena = sb("arena", [P, 20688])

        psum = ctx.enter_context(nc.psum_tensor("psum", [P, 8, 512], F32))
        bank = [psum[:, i, :] for i in range(8)]

        panel_loaded = [sem(f"panel_loaded{i}") for i in range(SLOTS)]
        hi_ready = sem("hi_ready")
        lo_ready = sem("lo_ready")
        panel_done = sem("panel_done")
        x_loaded = sem("x_loaded")
        const_loaded = sem("const_loaded")
        const_set = sem("const_set")
        zeros_set = sem("zeros_set")
        x_ready = sem("x_ready")
        sq_ready = sem("sq_ready")
        ss_ready = sem("ss_ready")
        rms_ready = sem("rms_ready")
        rstd_ready = sem("rstd_ready")
        h_ready = sem("h_ready")
        h_hi_ready = sem("h_hi_ready")
        h_lo_ready = sem("h_lo_ready")
        gate_ready = sem("gate_ready")
        act_ready = sem("act_ready")
        act_hi_ready = sem("act_hi_ready")
        act_lo_ready = sem("act_lo_ready")
        dft_loaded = sem("dft_loaded")
        dft_tok_ready = sem("dft_tok_ready")
        dft_tok_copied = sem("dft_tok_copied")
        dft_ready = sem("dft_ready")
        dft_hi_ready = sem("dft_hi_ready")
        dft_lo_ready = sem("dft_lo_ready")
        s5_loaded = sem("s5_loaded")
        s5_dt_ready = sem("s5_dt_ready")
        s5_prep = sem("s5_prep")
        s5_trig_ready = sem("s5_trig_ready")
        s5_hperm_ready = sem("s5_hperm_ready")
        s5_u_stored = sem("s5_u_stored")
        s5_u_loaded = sem("s5_u_loaded")
        s5_v_part = sem("s5_v_part")
        s5_v_ready = sem("s5_v_ready")
        s5_vt_ready = sem("s5_vt_ready")
        s5_win_ready = sem("s5_win_ready")
        s5_k_ready = sem("s5_k_ready")
        s5_k_copied = sem("s5_k_copied")
        s5_t_ready = sem("s5_t_ready")
        s5_t_copied = sem("s5_t_copied")
        s5_intra_ready = sem("s5_intra_ready")
        s5_intra_copied = sem("s5_intra_copied")
        s5_in_ready = sem("s5_in_ready")
        s5_in_copied = sem("s5_in_copied")
        s5_step = sem("s5_step")
        s5_w_part = sem("s5_w_part")
        s5_w_ready = sem("s5_w_ready")
        s5_out_ready = sem("s5_out_ready")
        s5_y_ready = sem("s5_y_ready")
        s5_y_stored = sem("s5_y_stored")
        s5_y_loaded = sem("s5_y_loaded")
        s5_skip_ready = sem("s5_skip_ready")
        s5_gelu_ready = sem("s5_gelu_ready")
        s5_g_hi_ready = sem("s5_g_hi_ready")
        s5_g_lo_ready = sem("s5_g_lo_ready")
        glu_sig_ready = sem("glu_sig_ready")
        glu_mul_ready = sem("glu_mul_ready")
        e_loaded = sem("e_loaded")
        e_ready = sem("e_ready")
        e_masked = sem("e_masked")
        e_stored = sem("e_stored")
        qk_sq_ready = sem("qk_sq_ready")
        qk_ss_ready = sem("qk_ss_ready")
        qk_rms_ready = sem("qk_rms_ready")
        qk_rstd_ready = sem("qk_rstd_ready")
        qk_ready = sem("qk_ready")
        v_copied = sem("v_copied")
        bias_loaded = [sem(f"bias_loaded{i}") for i in range(3)]
        sc_ready = sem("sc_ready")
        sc_biased = sem("sc_biased")
        max_ready = sem("max_ready")
        neg_ready = sem("neg_ready")
        p_ready = sem("p_ready")
        rden_ready = sem("rden_ready")
        p_scaled = sem("p_scaled")
        pt_ready = sem("pt_ready")
        pt_copied = sem("pt_copied")
        o_ready = sem("o_ready")
        o_copied = sem("o_copied")
        o_hi_ready = sem("o_hi_ready")
        o_lo_ready = sem("o_lo_ready")
        pos_loaded = sem("pos_loaded")
        rope_step = sem("rope_step")
        rope_angle = sem("rope_angle")
        rope_sin = sem("rope_sin")
        rope_squared = sem("rope_squared")
        rope_ready = sem("rope_ready")
        mix_loaded = sem("mix_loaded")
        pad_set = sem("pad_set")
        mix_copied = sem("mix_copied")
        conv_ready = sem("conv_ready")
        conv_act = sem("conv_act")
        dt_exp_ready = sem("dt_exp_ready")
        dt_arg_ready = sem("dt_arg_ready")
        a_ready = sem("a_ready")
        small_set = sem("small_set")
        small_ready = sem("small_ready")
        tok_ready = sem("tok_ready")
        tok_copied = sem("tok_copied")
        xt_ready = sem("xt_ready")
        xt_copied = sem("xt_copied")
        cb_ready = sem("cb_ready")
        cb_copied = sem("cb_copied")
        cs_ready = sem("cs_ready")
        decay_arg = sem("decay_arg")
        decay_ready = sem("decay_ready")
        decay_used = sem("decay_used")
        yp_ready = sem("yp_ready")
        y_raw = sem("y_raw")
        y_gated = sem("y_gated")
        ysq_ready = sem("ysq_ready")
        yss_ready = sem("yss_ready")
        yrms_ready = sem("yrms_ready")
        y_normed = sem("y_normed")
        y_hi_ready = sem("y_hi_ready")
        y_lo_ready = sem("y_lo_ready")
        rot_ready = sem("rot_ready")
        rope_used = sem("rope_used")
        rope_done = sem("rope_done")
        idx_ready = sem("idx_ready")
        relu_ready = sem("relu_ready")
        idx_added = sem("idx_added")
        sel_ready = sem("sel_ready")
        att_sc_ready = sem("att_sc_ready")
        att_biased = sem("att_biased")
        att_neg = sem("att_neg")
        att_p_ready = sem("att_p_ready")
        att_scaled = sem("att_scaled")
        att_pt_ready = sem("att_pt_ready")
        att_pt_copied = sem("att_pt_copied")
        att_o_ready = sem("att_o_ready")
        att_o_copied = sem("att_o_copied")
        att_hi_ready = sem("att_hi_ready")
        att_lo_ready = sem("att_lo_ready")
        mix_step = sem("mix_step")
        stored = sem("stored")

        block = ctx.enter_context(nc.Block())

        y_of = [bank[4 + o // 2][:, (o % 2) * S:(o % 2 + 1) * S] for o in range(KT)]

        def hidden_panel(n0, c):
            return n0 if c == 0 else n0 + 2 + 3 * (c - 1)

        dft_ch = arena[:, 0:S]
        dft_sq = arena[:, S:S + 2 * 2 * S].rearrange("p (t f s) -> p t f s", t=2, f=2)
        dft_tok = arena[:, 5 * S:5 * S + 2 * 2 * S].rearrange("p (b t n) -> p b t n", b=2, t=2)

        NC = 8

        class s5:
            at = 0

            @classmethod
            def take(cls, n):
                cls.at += n
                return arena[:, cls.at - n:cls.at]

        s5.z = s5.take(2 * S5_G * S5_C).rearrange("p (r c k) -> p r c k", r=2, c=S5_G)
        s5.hperm = s5.z[:, 0].rearrange("p c k -> p (c k)").rearrange("p (f t c) -> p f t c", f=KT, t=S5_T)
        s5.skip = s5.z[:, 0].rearrange("p c k -> p (c k)").rearrange("p (f t) -> p f t", f=KT)
        s5.gelu = s5.z[:, 1].rearrange("p c k -> p (c k)").rearrange("p (f t) -> p f t", f=KT)
        u_flat = s5.take(S5_G * S5_C)
        s5.u = u_flat.rearrange("p (g c) -> p g c", g=S5_G)
        s5.yt = u_flat.rearrange("p (f t c) -> p f t c", f=KT, t=S5_T)
        s5.buf = [s5.take(2 * NC * P).rearrange("p (r c m) -> p r c m", r=2, c=NC) for _ in range(2)]
        win_flat = s5.take(2 * NC * P)
        s5.win = win_flat.rearrange("p (m q) -> p m q", m=2 * NC)
        s5.b = s5.take(2 * S5_G * S5_P).rearrange("p (r c m) -> p r c m", r=2, c=S5_G)
        s5.c = s5.take(2 * S5_G * S5_P).rearrange("p (r c m) -> p r c m", r=2, c=S5_G)
        s5.pow = s5.take(2 * (S5_T + 1) * S5_G).rearrange("p (r k c) -> p r k c", r=2, k=S5_T + 1)
        tmp_flat = s5.take(2 * NC * P)
        s5.tmp = tmp_flat.rearrange("p (r c m) -> p r c m", r=2, c=NC)
        s5.kc = s5.take(2 * P)
        s5.tc = rope[:, :, :].rearrange("p r s -> p (r s)").rearrange("p (g i m) -> p g i m", g=KT, i=S5_T)
        s5.wide = win_flat
        s5.rot = s5.take(2 * S5_G).rearrange("p (r c) -> p r c", r=2)
        s5.d = s5.take(KT)
        s5.wide = s5.take(352)
        s5.y = hidden[:, :, :, :, :].rearrange("p a b t s -> p (a b t s)").rearrange("p (g c) -> p g c", g=S5_G)
        s5.par = win_flat[:, 0:3 * S5_G].rearrange("p (r c) -> p r c", r=3)
        s5.t = [win_flat[:, (3 + i) * S5_G:(4 + i) * S5_G] for i in range(16)]
        assert s5.at <= arena.shape[1], s5.at
        u_dram = nc.dram_tensor("s5_u", (P, KT, S5_T, S5_C), F32, kind="Internal").ap()
        y_dram = nc.dram_tensor("s5_y", (P, S5_G, S5_C), F32, kind="Internal").ap()

        def s5_table(r, ahead, d, f):
            c0 = f * NC + d * NC // 2
            cols = slice(c0, c0 + NC // 2)
            if d == 0:
                tab = s5.pow[:, r, ahead:ahead + S5_T, cols]
            else:
                tab = s5.pow[:, r, S5_T - 1 + ahead:(ahead - 1 if ahead else None):-1, cols]
            return tab.rearrange("p k c -> p c k").unsqueeze(3).to_broadcast([P, NC // 2, S5_T, S5_P])

        def s5_over_rows(v, d, f):
            c0 = f * NC + d * NC // 2
            return v[:, c0:c0 + NC // 2, :].unsqueeze(2).to_broadcast([P, NC // 2, S5_T, S5_P])

        def s5_part(v, d):
            return v[:, d * NC // 2:(d + 1) * NC // 2, :].rearrange("p c (k m) -> p c k m", k=S5_T)

        class da:
            at = 0

            @classmethod
            def take(cls, n):
                cls.at += n
                return arena[:, cls.at - n:cls.at]

        da.q = da.take(NG * 2 * S).rearrange("p (g m s) -> p g m s", g=NG, m=2)
        da.k = da.take(NG * 2 * S).rearrange("p (g m s) -> p g m s", g=NG, m=2)
        da.v = da.take(NG * 2 * S).rearrange("p (g m s) -> p g m s", g=NG, m=2)
        da.sq = da.take(2 * 2 * S).rearrange("p (b n) -> p b n", b=2)
        da.rs = da.take(2 * 2 * S).rearrange("p (b n) -> p b n", b=2)
        da.sc = da.take(2 * NG * S).rearrange("p (b n) -> p b n", b=2)
        da.pt = da.take(2 * NG * S).rearrange("p (b n) -> p b n", b=2)
        da.bias = da.take(3 * NG * S).rearrange("p (b g k) -> p b g k", b=3, g=NG)
        da.pair_ones = da.take(P)
        da.gain = da.take(2 * NG)
        n_units = HEADS * 2
        da.stat = da.take(4 * n_units).rearrange("p (r u) -> p r u", r=4)
        e_at, e_w = 9 * S, 2 * S
        da.rel = arena[0:BUCKETS, e_at:e_at + NG * HEADS]
        e_at += NG * HEADS
        da.onehot = arena[0:BUCKETS, e_at:e_at + e_w]
        da.mask = arena[0:NG * HEADS, e_at + e_w:e_at + 2 * e_w]
        da.e = arena[0:NG * HEADS, e_at + 2 * e_w:e_at + 3 * e_w]
        assert e_at + 3 * e_w <= 4096
        e_dram = nc.dram_tensor("bias_by_distance", (NG * HEADS, 2 * S), F32, kind="Internal").ap()
        dilated = any(st["kind"] == "dilated" for st in stages)

        class mx:
            at = 0

            @classmethod
            def take(cls, n):
                cls.at += n
                assert cls.at <= arena.shape[1], cls.at
                return arena[:, cls.at - n:cls.at]

        mx.q = mx.take(ATT_H * S).rearrange("p (h s) -> p h s", h=ATT_H)
        mx.k = mx.take(ATT_H * S).rearrange("p (h s) -> p h s", h=ATT_H)
        v_flat = mx.take(2 * D)
        mx.v = v_flat.rearrange("p (t n) -> p t n", t=2)
        mx.dt = [v_flat[0:SSD_H, i * S:(i + 1) * S] for i in range(8)]
        mx.qi = mx.take(4 * S).rearrange("p (h s) -> p h s", h=4)
        mx.ki = mx.take(S)
        mx.small = mx.take(S)
        mx.tok = mx.take(2 * P).rearrange("p (t n) -> p t n", t=2)
        mx.tri = mx.take(2 * S).rearrange("p (t l) -> p t l", t=2)
        mx.causal = mx.take(2 * S).rearrange("p (t k) -> p t k", t=2)
        mx.turn_i = mx.take(P)
        mx.turn = mx.take(ROPE_D)
        mx.col = mx.take(CONV_T * (CONV + 1) + KT + KT + 3)
        mx.convw = mx.col[:, 0:CONV_T * CONV].rearrange("p (c k) -> p c k", c=CONV_T)
        mx.convb = mx.col[:, CONV_T * CONV:CONV_T * (CONV + 1)]
        mx.dskip = mx.col[:, CONV_T * (CONV + 1):CONV_T * (CONV + 1) + KT]
        mx.ygain = mx.col[:, CONV_T * (CONV + 1) + KT:CONV_T * (CONV + 1) + 2 * KT]
        mx.dtb = mx.col[0:SSD_H, CONV_T * (CONV + 1) + 2 * KT:][:, 0:1]
        mx.alog = mx.col[0:SSD_H, CONV_T * (CONV + 1) + 2 * KT:][:, 1:2]
        mx.wi = mx.take(2 * IDX_H).rearrange("p (t h) -> p t h", t=2)
        ssd_at = mx.at
        mx.z = mx.take(KT * S).rearrange("p (c s) -> p c s", c=KT)
        mx.raw = mx.take(CONV_T * (S + CONV - 1)).rearrange("p (c s) -> p c s", c=CONV_T)
        mx.conv = mx.take(CONV_T * S).rearrange("p (c s) -> p c s", c=CONV_T)
        mx.cb = mx.take(SSD_G * 2 * S).rearrange("p (g t l) -> p g t l", g=SSD_G, t=2)
        mx.dec = mx.take(2 * 2 * S).rearrange("p (b t l) -> p b t l", b=2, t=2)
        mx.m = mx.take(2 * 2 * S).rearrange("p (b t l) -> p b t l", b=2, t=2)
        mx.xt = hidden[:, :, :, :, :].rearrange("p a b t s -> p (a b t s)").rearrange("p (t n) -> p t n", t=2)
        mx.y = h
        mx.at = ssd_at + KT * S
        mx.yatt = mx.take(KT * S).rearrange("p (c s) -> p c s", c=KT)
        mx.relu = mx.take(4 * S).rearrange("p (b s) -> p b s", b=4)
        mx.score = mx.take(2 * S).rearrange("p (t s) -> p t s", t=2)
        mx.sel = mx.take(2 * S).rearrange("p (t s) -> p t s", t=2)
        mx.sc = mx.take(2 * S).rearrange("p (b s) -> p b s", b=2)
        mx.pt = mx.take(2 * S).rearrange("p (b s) -> p b s", b=2)
        mx.top8 = mx.take(2 * 8).rearrange("p (t s) -> p t s", t=2)
        mx.stat = mx.take(4 * 2 * ATT_H).rearrange("p (r u) -> p r u", r=4)
        mx.rot = hidden[:, :, :, :, :].rearrange("p a b t s -> p (a b t s)").rearrange("p (b n) -> p b n", b=4)
        mixes = any(st["kind"] == "mix" for st in stages)
        rp_flat = s5.c.rearrange("p r c m -> p (r c m)")
        rp_pos = rp_flat[:, 0:S].bitcast(mybir.dt.int32)
        rp_freq = rp_flat[:, S:S + 2]
        rp_f = rp_flat[:, 2 * S - 128:3 * S - 128]
        rp_ang = rp_flat[:, 3 * S:5 * S].rearrange("p (r s) -> p r s", r=2)
        rp_n = rp_flat[:, 5 * S:7 * S].rearrange("p (r s) -> p r s", r=2)

        @block.sync
        def _(sp):
            sp.dma_start(x[:, :, :], A["x"].rearrange("(c p) t -> p c t", p=P)).then_inc(x_loaded, 16)
            sp.dma_start(gains[:, :], A["gains"]).then_inc(const_loaded, 16)
            sp.dma_start(ident[:, :], A["ident"]).then_inc(const_loaded, 16)
            if any(st["kind"] == "s5" for st in stages):
                for dst, name in ((s5.par, "s5_lam"), (s5.b, "s5_b"), (s5.c, "s5_c")):
                    sp.dma_start(dst, A[name].rearrange("p (r c) -> p r c", r=dst.shape[1]) if dst is s5.par
                                 else A[name].rearrange("p (r c m) -> p r c m", r=2, c=S5_G)).then_inc(s5_loaded, 16)
                sp.dma_start(s5.d, A["s5_d"]).then_inc(s5_loaded, 16)
                sp.dma_start(s5.wide, A["s5_wide"]).then_inc(s5_loaded, 16)
            for n in range(SLOTS):
                sp.dma_start(raw[:, n, :], A["panels"][n]).then_inc(panel_loaded[n], 16)
            rounds = (n_panels + 1 - SLOTS) // SLOTS
            with sp.Fori(0, rounds) as i:
                for k in range(SLOTS):
                    sp.wait_ge(lo_ready, i * SLOTS + k + 1)
                    sp.dma_start(raw[:, k, :], A["panels"][bass.ds(i * SLOTS + (SLOTS + k), 1), :, :]
                                 .rearrange("o p n -> p (o n)")).then_inc(panel_loaded[k], 16)
            for n in range(SLOTS * (rounds + 1), n_panels + 1):
                sp.wait_ge(lo_ready, n - SLOTS + 1)
                sp.dma_start(raw[:, n % SLOTS, :], A["panels"][n]).then_inc(panel_loaded[n % SLOTS], 16)
            if final:
                sp.wait_ge(h_ready, 4 * (stages[-1]["norm"] + 1))
                sp.dma_start(out.rearrange("(c p) t -> p c t", p=P), h[:, :, :]).then_inc(stored, 16)
            else:
                sp.wait_ge(x_ready, stages[-1]["xr"] + 4)
                sp.dma_start(out.rearrange("(c p) t -> p c t", p=P), x[:, :, :]).then_inc(stored, 16)
            sp.wait_ge(stored, 16)

        S5_ANGLE, S5_DEN, S5_PREP = 11, 71, 80

        @block.gpsimd
        def _(pool):
            pool.memset(ones[:, :], 1.0).then_inc(const_set, 1)
            pool.memset(eps[:, :], EPS).then_inc(const_set, 1)
            if dilated:
                pool.dma_start(da.rel, A["rel_bias"]).then_inc(e_loaded, 16)
                pool.dma_start(da.onehot, A["bucket_onehot"]).then_inc(e_loaded, 16)
                pool.dma_start(da.mask, A["group_mask"]).then_inc(e_loaded, 16)

            def dilated_mixer(st):
                pool.wait_ge(x_ready, st["xr"])
                pool.dma_start(da.pair_ones, A["pair_ones"]).then_inc(e_loaded, 16)
                pool.dma_start(da.gain, A["qk_gain"]).then_inc(e_loaded, 16)
                if mixes:
                    rope_angles()
                pool.wait_ge(e_stored, 16)
                for u in range(n_units):
                    head, qt = u // 2, u % 2
                    if u >= 3:
                        pool.wait_ge(sc_biased, u - 2)
                    src = bass.AP(e_dram.tensor, head * 2 * S + qt * P, [[1, P], [HEADS * 2 * S, NG], [1, S]])
                    pool.dma_start(da.bias[:, u % 3], src).then_inc(bias_loaded[u % 3], 16)
                if mixes:
                    rope_cosines()

            n_prep = 0

            def then(*ins):
                nonlocal n_prep
                for q in ins:
                    q.then_inc(s5_prep, 1)
                    n_prep += 1
                pool.wait_ge(s5_prep, n_prep)

            def s5_prepare():
                tt, ts = pool.tensor_tensor, pool.tensor_scalar
                lre, lim = s5.par[:, 0], s5.par[:, 1]
                dt, are, ang, turns, mag, sn, sh, t0, t1, t2, t3, nre, nim = s5.t[:13]
                pool.wait_ge(s5_loaded, 5 * 16)
                pool.wait_ge(s5_dt_ready, 1)
                then(tt(are, lre, dt, ALU.mult), tt(ang, lim, dt, ALU.mult))
                then(ts(turns, ang, 1 / TWO_PI, ROUND, ALU.mult, ALU.add))
                then(ts(turns, turns, ROUND, None, ALU.subtract))
                for part in (TWO_PI_1, TWO_PI_2, TWO_PI_3):
                    then(ts(t0, turns, part, None, ALU.mult))
                    then(tt(ang, ang, t0, ALU.subtract))
                then(ts(ang, ang, PI_BELOW, -PI_BELOW, ALU.min, ALU.max))
                assert n_prep == S5_ANGLE
                pool.wait_ge(s5_trig_ready, 3)
                p = s5.pow
                then(tt(t0, sh, sh, ALU.mult))
                then(ts(t0, t0, -2.0, 1.0, ALU.mult, ALU.add))
                then(tt(p[:, 0, 1], mag, t0, ALU.mult), tt(p[:, 1, 1], mag, sn, ALU.mult),
                     pool.memset(p[:, 0, 0], 1.0), pool.memset(p[:, 1, 0], 0.0))
                for k in range(2, S5_T + 1):
                    then(tt(t0, p[:, 0, k - 1], p[:, 0, 1], ALU.mult), tt(t1, p[:, 1, k - 1], p[:, 1, 1], ALU.mult),
                         tt(t2, p[:, 0, k - 1], p[:, 1, 1], ALU.mult), tt(t3, p[:, 1, k - 1], p[:, 0, 1], ALU.mult))
                    then(tt(p[:, 0, k], t0, t1, ALU.subtract), tt(p[:, 1, k], t2, t3, ALU.add))
                then(ts(s5.rot[:, 0], p[:, 1, S5_T], -1.0, None, ALU.mult), ts(s5.rot[:, 1], p[:, 1, S5_T], 1.0, None, ALU.mult))
                then(ts(nre, p[:, 0, 1], -1.0, None, ALU.add))
                nim = p[:, 1, 1]
                then(tt(t0, nre, lre, ALU.mult), tt(t1, nim, lim, ALU.mult),
                     tt(t2, nim, lre, ALU.mult), tt(t3, nre, lim, ALU.mult))
                then(tt(mag, t0, t1, ALU.add), tt(sn, t2, t3, ALU.subtract),
                     tt(are, lre, lre, ALU.mult), tt(ang, lim, lim, ALU.mult))
                then(tt(are, are, ang, ALU.add))
                pool.wait_ge(s5_trig_ready, 4)
                then(tt(mag, mag, are, ALU.mult), tt(sn, sn, are, ALU.mult))
                full = [P, S5_G, S5_P]
                cre, cim = mag.unsqueeze(2).to_broadcast(full), sn.unsqueeze(2).to_broadcast(full)
                b, tb = s5.b, tmp_flat.rearrange("p (r c m) -> p r c m", r=2, c=S5_G)
                td = win_flat[:, 1024:2048].rearrange("p (c m) -> p c m", c=S5_G)
                then(tt(tb[:, 0], cre, b[:, 0], ALU.mult), tt(tb[:, 1], cim, b[:, 0], ALU.mult),
                     tt(td, cim, b[:, 1], ALU.mult))
                then(tt(b[:, 0], tb[:, 0], td, ALU.subtract))
                then(tt(td, cre, b[:, 1], ALU.mult))
                then(tt(b[:, 1], tb[:, 1], td, ALU.add), ts(s5.c[:, 1], s5.c[:, 1], -1.0, None, ALU.mult))
                assert n_prep == S5_PREP, n_prep

            def rope_angles():
                n = 0

                def then(*ins):
                    nonlocal n
                    for q in ins:
                        q.then_inc(rope_step, 1)
                        n += 1
                    pool.wait_ge(rope_step, n)

                pool.dma_start(rp_pos, A["positions"]).then_inc(pos_loaded, 16)
                pool.dma_start(rp_freq, A["rope_freq"]).then_inc(pos_loaded, 16)
                pool.wait_ge(pos_loaded, 32)
                tt, ts = pool.tensor_tensor, pool.tensor_scalar
                then(pool.tensor_copy(rp_f, rp_pos))
                then(*[ts(rp_ang[:, r], rp_f, rp_freq[:, r:r + 1], None, ALU.mult) for r in range(2)])
                then(ts(rp_n, rp_ang, 1 / TWO_PI, ROUND, ALU.mult, ALU.add))
                then(ts(rp_n, rp_n, ROUND, None, ALU.subtract))
                for part in (TWO_PI_1, TWO_PI_2, TWO_PI_3):
                    then(ts(rope[:, 0:2], rp_n, part, None, ALU.mult))
                    then(tt(rp_ang, rp_ang, rope[:, 0:2], ALU.subtract))
                ts(rp_ang, rp_ang, PI_BELOW, -PI_BELOW, ALU.min, ALU.max).then_inc(rope_angle, 1)

            def rope_cosines():
                pool.wait_ge(rope_sin, 4)
                pool.tensor_tensor(rp_n, rp_ang, rp_ang, ALU.mult).then_inc(rope_squared, 1)
                pool.wait_ge(rope_squared, 1)
                pool.tensor_scalar(rope[:, 0:3:2], rp_n, -2.0, 1.0, ALU.mult, ALU.add).then_inc(rope_ready, 1)

            def mix_loads(st):
                pool.wait_ge(x_ready, st["xr"])
                i = st["i"]
                pool.dma_start(mx.col, A["mix_col"][i]).then_inc(mix_loaded, 16)
                pool.dma_start(mx.tri, A["mask_tri"]).then_inc(mix_loaded, 16)
                pool.dma_start(mx.causal, A["mask_causal"]).then_inc(mix_loaded, 16)
                pool.dma_start(mx.turn_i, A["turn_i"]).then_inc(mix_loaded, 16)
                pool.dma_start(mx.turn[0:ROPE_D, :], A["turn"]).then_inc(mix_loaded, 16)
                pool.memset(mx.small, 0.0).then_inc(small_set, 1)
                pool.memset(mx.raw[:, :, 0:CONV - 1], 0.0).then_inc(pad_set, 1)

            def s5_mixer(st):
                pool.wait_ge(s5_hperm_ready, KT)
                pool.dma_start(u_dram, s5.hperm).then_inc(s5_u_stored, 16)
                pool.wait_ge(s5_u_stored, 16)
                for r in range(S5_T):
                    for f in range(KT):
                        pool.dma_start(s5.u[r * S5_P:(r + 1) * S5_P, f * KT:(f + 1) * KT, :],
                                       u_dram[:, f, r, :].rearrange("(g m) c -> m g c", m=S5_P)).then_inc(s5_u_loaded, 16)
                pool.wait_ge(s5_y_ready, 2 * KT)
                pool.dma_start(y_dram, s5.y).then_inc(s5_y_stored, 16)
                pool.wait_ge(s5_y_stored, 16)
                yd = y_dram.rearrange("(i m) (f g) c -> m f g i c", m=S5_P, f=KT)
                for g in range(KT):
                    for f in range(KT):
                        pool.dma_start(s5.yt[g * S5_P:(g + 1) * S5_P, f], yd[:, f, g]).then_inc(s5_y_loaded, 16)

            if any(st["kind"] == "s5" for st in stages):
                s5_prepare()
            if dilated:
                pool.wait_ge(e_masked, 1)
                pool.dma_start(e_dram, da.e).then_inc(e_stored, 16)
            for st in stages:
                if st["kind"] == "s5":
                    s5_mixer(st)
                if st["kind"] == "dilated":
                    dilated_mixer(st)
                if st["kind"] == "mix":
                    mix_loads(st)
                if st["kind"] == "fourier":
                    if st["xr"]:
                        pool.wait_ge(x_ready, st["xr"])
                    pool.dma_start(dft_ch, A["dft_ch"]).then_inc(dft_loaded, 16)
                    pool.dma_start(dft_sq, A["dft_sq"].rearrange("(t p) (f s) -> p t f s", p=P, f=2)
                                   ).then_inc(dft_loaded, 16)

        @block.scalar
        def _(a):
            def split(n, i=None, per=0):
                def at(v, m=1):
                    return v if i is None else i * (m * per) + v
                if i is None and n > n_panels:
                    return
                s = n % SLOTS
                a.wait_ge(panel_loaded[s], 16 * (n // SLOTS + 1) if i is None
                          else i * (16 * per // SLOTS) + 16 * (n // SLOTS + 1))
                if n >= SLOTS:
                    a.wait_ge(panel_done, at(n - SLOTS + 1))
                a.activation(w_hi[:, s, :], raw[:, s, :], ACT.Copy).then_inc(hi_ready, 1)

            def norm(st):
                n = st["norm"]
                a.wait_ge(x_loaded, 16)
                for b in range(4):
                    if st["xr"]:
                        a.wait_ge(x_ready, st["xr"] - 3 + b)
                    a.activation(h[:, 2 * b:2 * b + 2, :], x[:, 2 * b:2 * b + 2, :],
                                 ACT.Square).then_inc(sq_ready, 1)
                a.wait_ge(const_set, 2)
                a.wait_ge(ss_ready, n + 1)
                a.activation(rstd[:, :], bank[4][:, 0:S], ACT.Sqrt, bias=eps[:, 0:1],
                             scale=1.0 / D).then_inc(rms_ready, 1)
                if st["kind"] == "norm":
                    for b in range(4):
                        a.wait_ge(h_ready, 4 * n + b + 1)
                        a.activation(h_hi[:, 2 * b:2 * b + 2, :], h[:, 2 * b:2 * b + 2, :],
                                     ACT.Copy).then_inc(h_hi_ready, 1)

            def ffn(st):
                n0, f = st["n0"], st["ffn"]

                def silu(c, p, i=None):
                    def at(v, per):
                        return v if i is None else i * per + v
                    a.wait_ge(panel_done, at(p + 1, 6))
                    a.activation(gate[:, c % 2], bank[(2 * c) % PROJ_BANKS][:, :].rearrange(
                        "p (t s) -> p t s", t=2), ACT.Silu).then_inc(gate_ready, 1)

                split(n0 + 2)
                split(n0 + 3)
                silu(0, n0)
                with a.Fori(0, (FFC - 1) // 2) as i:
                    for c in (1, 2):
                        p = hidden_panel(n0, c)
                        split(p + 2, i, 6)
                        split(p + 3, i, 6)
                        silu(c, p, i)
                        split(p + 4, i, 6)
                split(n0 + 34)

            def fourier(st):
                f = st["fourier"] = sum(q["kind"] == "fourier" for q in stages[:stages.index(st)])
                for g in range(KT):
                    k = f * KT + g
                    a.wait_ge(dft_tok_ready, k + 1)
                    a.activation(dft_tok[:, g % 2], bank[4 + g % 2][:, :].rearrange("p (t n) -> p t n", t=2),
                                 ACT.Copy).then_inc(dft_tok_copied, 1)
                    if g:
                        a.wait_ge(dft_ready, k)
                        a.activation(h_hi[:, g - 1], bank[6 + (g - 1) % 2][:, 0:S], ACT.Copy).then_inc(dft_hi_ready, 1)
                a.wait_ge(dft_ready, f * KT + KT)
                a.activation(h_hi[:, KT - 1], bank[6 + (KT - 1) % 2][:, 0:S], ACT.Copy).then_inc(dft_hi_ready, 1)
                for p in range(4):
                    split(st["n0"] + p + 2)

            def s5_prepare():
                dt, are, ang, turns, mag, sn, sh = s5.t[:7]
                a.wait_ge(s5_loaded, 5 * 16)
                a.activation(dt, s5.par[:, 2], ACT.Exp).then_inc(s5_dt_ready, 1)
                a.wait_ge(s5_prep, S5_ANGLE)
                a.activation(mag, are, ACT.Exp).then_inc(s5_trig_ready, 1)
                a.activation(sn, ang, ACT.Sin).then_inc(s5_trig_ready, 1)
                a.activation(sh, ang, ACT.Sin, scale=0.5).then_inc(s5_trig_ready, 1)

            def s5_mixer(st):
                hn = st["hn"]
                a.wait_ge(h_ready, 4 * (hn + 1))
                for f in range(KT):
                    a.activation(s5.hperm[:, f], h[:, f, :].rearrange("p (c r) -> p r c", r=S5_T)[:, ::-1, :],
                                 ACT.Copy).then_inc(s5_hperm_ready, 1)
                a.wait_ge(s5_u_loaded, 16 * S5_T * KT)
                for f in range(KT):
                    for q in range(4):
                        a.wait_ge(s5_vt_ready, 4 * f + q + 1)
                        if f and q == 0:
                            a.wait_ge(s5_in_ready, f)
                        a.activation(s5.win[:, 4 * q:4 * q + 4, :], bank[4 + q % 2][:, :].rearrange(
                            "p (m q) -> p m q", m=4), ACT.Copy).then_inc(s5_win_ready, 1)
                    a.wait_ge(s5_k_ready, f + 1)
                    for e in range(2):
                        a.activation(s5.kc.rearrange("p (c e m) -> p c e m", c=NC, e=2)[:, :, e, :],
                                     bank[6 + e][:, 0:P].rearrange("p (c m) -> p c m", c=NC),
                                     ACT.Copy).then_inc(s5_k_copied, 1)
                    a.wait_ge(s5_t_ready, f + 1)
                    for q in range(2):
                        a.activation(s5.tc[:, :, 4 * q:4 * q + 4, :].rearrange("p g i m -> p i g m"), bank[7 - q][:, :].rearrange(
                            "p (i g m) -> p i g m", i=4, g=KT), ACT.Copy).then_inc(s5_t_copied, 1)
                    a.wait_ge(s5_in_ready, f + 1)
                    a.activation(s5.z[:, :, f * NC:(f + 1) * NC, :], bank[2 + f % 2][:, :].rearrange(
                        "p (r c k) -> p r c k", r=2, c=NC), ACT.Copy).then_inc(s5_in_copied, 1)
                    a.wait_ge(s5_intra_ready, f + 1)
                    a.activation(s5.y[:, f * KT:(f + 1) * KT, :], bank[f % 2][:, 0:S].rearrange(
                        "p (g c) -> p g c", g=KT), ACT.Copy).then_inc(s5_intra_copied, 1)
                for f in range(KT):
                    a.wait_ge(s5_skip_ready, f + 1)
                    a.activation(s5.gelu[:, f], s5.skip[:, f], ACT.Gelu_apprx_tanh).then_inc(s5_gelu_ready, 1)
                for b in range(4):
                    a.wait_ge(s5_gelu_ready, 2 * b + 2)
                    a.activation(h_hi[:, 2 * b:2 * b + 2, :], s5.gelu[:, 2 * b:2 * b + 2, :],
                                 ACT.Copy).then_inc(s5_g_hi_ready, 1)
                for k in range(4):
                    split(st["n0"] + 2 * k + 2)
                    split(st["n0"] + 2 * k + 3)
                    a.wait_ge(panel_done, st["n0"] + 2 * k + 2)
                    if k >= 2:
                        a.wait_ge(glu_mul_ready, k - 1)
                    a.activation(gate[:, k % 2], bank[(2 * k + 1) % PROJ_BANKS][:, :].rearrange("p (t s) -> p t s", t=2),
                                 ACT.Sigmoid).then_inc(glu_sig_ready, 1)

            def dilated_mixer(st):
                def rms(c):
                    a.wait_ge(qk_ss_ready, c + 1)
                    if c >= 2:
                        a.wait_ge(qk_ready, c - 1)
                    a.activation(da.rs[:, c % 2], bank[4 + c % 2][:, :], ACT.Sqrt, bias=eps[:, 0:1],
                                 scale=1.0 / E).then_inc(qk_rms_ready, 1)

                def square(p, c):
                    if c >= 2:
                        a.wait_ge(qk_ss_ready, c - 1)
                    a.activation(da.sq[:, c % 2], bank[p % PROJ_BANKS][:, :], ACT.Square).then_inc(qk_sq_ready, 1)

                for hb in range(HEADS // HB):
                    for g in range(NG):
                        p, c = (hb * NG + g) * 3, (hb * NG + g) * 2
                        split(st["n0"] + p + 2)
                        a.wait_ge(panel_done, st["n0"] + p + 1)
                        square(p, c)
                        split(st["n0"] + p + 3)
                        a.wait_ge(panel_done, st["n0"] + p + 2)
                        square(p + 1, c + 1)
                        rms(c)
                        split(st["n0"] + p + 4)
                        a.wait_ge(panel_done, st["n0"] + p + 3)
                        if hb and g == 0:
                            a.wait_ge(o_ready, 2 * HB * hb)
                        a.activation(da.v[:, g], bank[(p + 2) % PROJ_BANKS][:, :].rearrange("p (m n) -> p m n", m=2),
                                     ACT.Copy).then_inc(v_copied, 1)
                        rms(c + 1)

                    def copy_p(u):
                        a.wait_ge(pt_ready, u + 1)
                        if u >= 2:
                            a.wait_ge(o_ready, u - 1)
                        a.activation(da.pt[:, u % 2], psum[:, 6:8, :].rearrange("p b n -> p (b n)")[:, 0:NG * S],
                                     ACT.Copy).then_inc(pt_copied, 1)

                    def copy_o(u):
                        head, qt = u // 2, u % 2
                        rows = slice(head % 2 * E, head % 2 * E + E)
                        a.wait_ge(o_ready, u + 1)
                        a.activation(h[rows, head // 2, qt * P:(qt + 1) * P], bank[u % PROJ_BANKS][rows, 0:P],
                                     ACT.Copy).then_inc(o_copied, 1)

                    u0 = 2 * HB * hb
                    for u in range(u0, u0 + 2 * HB):
                        a.wait_ge(neg_ready, u + 1)
                        a.activation(da.sc[:, u % 2], da.sc[:, u % 2], ACT.Exp, bias=da.stat[:, 1, u:u + 1],
                                     accum_out=da.stat[:, 2, u:u + 1]).then_inc(p_ready, 1)
                        if u > u0:
                            copy_p(u - 1)
                        if u > u0 + 1:
                            copy_o(u - 2)
                    copy_p(u0 + 2 * HB - 1)
                    copy_o(u0 + 2 * HB - 2)
                    copy_o(u0 + 2 * HB - 1)
                a.wait_ge(o_copied, n_units)
                for b in range(4):
                    a.activation(h_hi[:, 2 * b:2 * b + 2, :], h[:, 2 * b:2 * b + 2, :], ACT.Copy).then_inc(o_hi_ready, 1)
                if mixes:
                    rope_sines()
                for p in range(36, 40):
                    split(st["n0"] + p + 2)

            def rope_sines():
                a.wait_ge(rope_angle, 1)
                for r in range(2):
                    a.activation(rope[:, 2 * r + 1], rp_ang[:, r], ACT.Sin).then_inc(rope_sin, 1)
                a.wait_ge(rope_sin, 2)
                for r in range(2):
                    a.activation(rp_ang[:, r], rp_ang[:, r], ACT.Sin, scale=0.5).then_inc(rope_sin, 1)

            def mixer(st):
                i, n0 = st["i"], st["n0"]

                def arrive(p):
                    split(n0 + p + 2)
                    a.wait_ge(panel_done, n0 + p + 1)
                    return bank[p % PROJ_BANKS]

                def halves(b):
                    return b[:, :].rearrange("p (m s) -> p m s", m=2)

                def conv_silu(c):
                    a.wait_ge(conv_ready, CONV_T * i + c + 1)
                    a.activation(mx.conv[:, c], mx.conv[:, c], ACT.Silu).then_inc(conv_act, 1)

                a.wait_ge(pad_set, i + 1)
                a.wait_ge(mix_loaded, 80 * (i + 1))
                for p in range(6):
                    a.activation(mx.raw[:, 2 * p:2 * p + 2, CONV - 1:], halves(arrive(p)), ACT.Copy).then_inc(mix_copied, 1)
                    if p:
                        conv_silu(2 * p - 2)
                        conv_silu(2 * p - 1)
                b = arrive(6)
                a.wait_ge(small_set, i + 1)
                a.activation(mx.ki, b[:, 0:S], ACT.Copy)
                a.activation(mx.small[32:32 + IDX_H, :], b[32:32 + IDX_H, S:2 * S], ACT.Copy)
                a.activation(mx.dt[0], b[0:SSD_H, S:2 * S], ACT.Copy).then_inc(mix_copied, 1)
                conv_silu(10)
                conv_silu(11)
                for p in range(7, 11):
                    a.activation(mx.z[:, 2 * (p - 7):2 * (p - 7) + 2, :], halves(arrive(p)), ACT.Silu).then_inc(mix_copied, 1)
                a.wait_ge(dt_arg_ready, i + 1)
                a.activation(mx.dt[2], mx.dt[1], ACT.Exp).then_inc(dt_exp_ready, 1)
                a.activation(mx.alog, mx.alog, ACT.Exp).then_inc(a_ready, 1)
                for q in range(4):
                    a.wait_ge(xt_ready, 4 * i + q + 1)
                    a.activation(mx.xt[:, :, q * 2 * P:(q + 1) * 2 * P], bank[5 + q % 2][:, :].rearrange(
                        "p (t n) -> p t n", t=2), ACT.Copy).then_inc(xt_copied, 1)
                a.wait_ge(tok_ready, i + 1)
                a.activation(mx.tok, bank[4][:, 0:2 * P].rearrange("p (t n) -> p t n", t=2), ACT.Copy).then_inc(tok_copied, 1)
                for g in range(SSD_G):
                    a.wait_ge(cb_ready, 2 * i + g + 1)
                    b = bank[7 if g == 0 else 4]
                    a.activation(mx.cb[:, g, 0], b[:, 0:S], ACT.Copy)
                    a.activation(mx.cb[:, g, 1, P:], b[:, S + P:2 * S], ACT.Copy).then_inc(cb_copied, 1)
                for j in range(SSD_H // 2):
                    for e in range(2):
                        n = SSD_H * i + 2 * j + e
                        a.wait_ge(decay_arg, n + 1)
                        d = mx.dec[:, e]
                        a.activation(d[:, 0], d[:, 0], ACT.Exp)
                        a.activation(d[:, 1, P:], d[:, 1, P:], ACT.Exp).then_inc(decay_ready, 1)
                    p = 11 + j
                    dst = mx.qi[:, 2 * j:2 * j + 2, :] if j < 2 else mx.q[:, 2 * j - 4:2 * j - 2, :] if j < 6 else \
                        mx.k[:, 2 * j - 12:2 * j - 10, :]
                    a.activation(dst, halves(arrive(p)), ACT.Copy).then_inc(mix_copied, 1)
                for p in range(19, 21):
                    a.activation(mx.k[:, 2 * (p - 17):2 * (p - 17) + 2, :], halves(arrive(p)), ACT.Copy).then_inc(mix_copied, 1)
                for p in range(21, 25):
                    if p == 21:
                        a.wait_ge(decay_used, SSD_H * (i + 1))
                    a.activation(mx.v[:, :, (p - 21) * COLS:(p - 20) * COLS], halves(arrive(p)), ACT.Copy).then_inc(mix_copied, 1)
                for g in range(SSD_G):
                    a.wait_ge(y_gated, 8 * i + 4 * g + 4)
                    a.activation(mx.z[:, 4 * g:4 * g + 4], mx.y[:, 4 * g:4 * g + 4], ACT.Square).then_inc(ysq_ready, 1)
                for g in range(SSD_G):
                    a.wait_ge(yss_ready, 2 * i + g + 1)
                    a.activation(mx.dec[:, g, 0], bank[4 + g][:, 0:S], ACT.Sqrt, bias=eps[:, 0:1],
                                 scale=SSD_G / D).then_inc(yrms_ready, 1)
                for b in range(4):
                    a.wait_ge(y_normed, 4 * i + b + 1)
                    a.activation(h_hi[:, 2 * b:2 * b + 2, :], mx.y[:, 2 * b:2 * b + 2, :], ACT.Copy).then_inc(y_hi_ready, 1)
                for p in range(25, 29):
                    split(n0 + p + 2)
                for u in range(2 * IDX_H):
                    qt = u // IDX_H
                    keys = (qt + 1) * P
                    n = 2 * IDX_H * i + u
                    a.wait_ge(idx_ready, n + 1)
                    if u >= 4:
                        a.wait_ge(idx_added, n - 3)
                    a.activation(mx.relu[:, u % 4, 0:keys], bank[4 + u % 4][:, 0:keys], ACT.Relu,
                                 scale=E ** -0.5).then_inc(relu_ready, 1)

                def copy_p(u):
                    n, keys = 2 * ATT_H * i + u, (u % 2 + 1) * P
                    a.wait_ge(att_pt_ready, n + 1)
                    if u >= 2:
                        a.wait_ge(att_o_ready, n - 1)
                    a.activation(mx.pt[:, u % 2, 0:keys], bank[6][:, 0:keys], ACT.Copy).then_inc(att_pt_copied, 1)

                def copy_o(u):
                    head, qt = u // 2, u % 2
                    a.wait_ge(att_o_ready, 2 * ATT_H * i + u + 1)
                    a.activation(mx.yatt[:, head, qt * P:(qt + 1) * P], bank[7][:, u % 2 * P:(u % 2 + 1) * P],
                                 ACT.Copy).then_inc(att_o_copied, 1)

                units = 2 * ATT_H
                for u in range(units):
                    keys = (u % 2 + 1) * P
                    a.wait_ge(att_neg, units * i + u + 1)
                    a.activation(mx.sc[:, u % 2, 0:keys], mx.sc[:, u % 2, 0:keys], ACT.Exp, bias=mx.stat[:, 1, u:u + 1],
                                 accum_out=mx.stat[:, 2, u:u + 1]).then_inc(att_p_ready, 1)
                    if u:
                        copy_p(u - 1)
                    if u > 1:
                        copy_o(u - 2)
                copy_p(units - 1)
                copy_o(units - 2)
                copy_o(units - 1)
                a.wait_ge(att_o_copied, units * (i + 1))
                a.wait_ge(panel_done, n0 + 29)
                for b in range(4):
                    a.activation(h_hi[:, 2 * b:2 * b + 2, :], mx.yatt[:, 2 * b:2 * b + 2, :], ACT.Copy).then_inc(att_hi_ready, 1)
                for p in range(29, 33):
                    split(n0 + p + 2)

            split(0)
            split(1)
            if any(st["kind"] == "s5" for st in stages):
                s5_prepare()
            todo = {"norm": norm, "final": norm, "ffn": ffn, "fourier": fourier, "s5": s5_mixer,
                    "dilated": dilated_mixer, "mix": mixer}
            for st in stages:
                todo[st["kind"]](st)

        @block.vector
        def _(v):
            def split(n, i=None, per=0):
                if i is None and n > n_panels:
                    return
                v.wait_ge(hi_ready, n + 1 if i is None else i * per + n + 1)
                s = n % SLOTS
                v.tensor_tensor(w_lo[:, s, :], raw[:, s, :], w_hi[:, s, :].bitcast(F32),
                                ALU.subtract).then_inc(lo_ready, 1)

            def norm(st):
                n = st["norm"]
                v.wait_ge(const_loaded, 32)
                v.wait_ge(rms_ready, n + 1)
                v.reciprocal(rstd[:, :], rstd[:, :]).then_inc(rstd_ready, 1)
                v.wait_ge(rstd_ready, n + 1)
                for b in range(4):
                    for c in (2 * b, 2 * b + 1):
                        ins = v.scalar_tensor_tensor(h[:, c, :], x[:, c, :], gains[:, n * KT + c:n * KT + c + 1],
                                                     rstd[:, :], ALU.mult, ALU.mult)
                    ins.then_inc(h_ready, 1)
                if st["kind"] == "norm":
                    for b in range(4):
                        v.wait_ge(h_hi_ready, 4 * n + b + 1)
                        v.tensor_tensor(h_lo[:, 2 * b:2 * b + 2, :], h[:, 2 * b:2 * b + 2, :],
                                        h_hi[:, 2 * b:2 * b + 2, :].bitcast(F32),
                                        ALU.subtract).then_inc(h_lo_ready, 1)

            def ffn(st):
                n0, f = st["n0"], st["ffn"]
                scale = 1.0 if st["i"] < BLOCK1 else 0.5

                def hidden(c, p, i=None):
                    def at(val, per):
                        return val if i is None else i * per + val
                    b = c % 2
                    v.wait_ge(panel_done, at(p + 2, 6))
                    v.wait_ge(gate_ready, at(f * FFC + c + 1, 2))
                    v.tensor_tensor(act[:, b], gate[:, b], bank[(2 * c + 1) % PROJ_BANKS][:, :].rearrange(
                        "p (t s) -> p t s", t=2), ALU.mult).then_inc(act_ready, 1)
                    v.wait_ge(act_ready, at(f * FFC + c + 1, 2))
                    v.tensor_copy(act_hi[:, b], act[:, b]).then_inc(act_hi_ready, 1)
                    v.wait_ge(act_hi_ready, at(f * FFC + c + 1, 2))
                    v.tensor_tensor(act_lo[:, b], act[:, b], act_hi[:, b].bitcast(F32),
                                    ALU.subtract).then_inc(act_lo_ready, 1)

                split(n0 + 2)
                split(n0 + 3)
                hidden(0, n0)
                with v.Fori(0, (FFC - 1) // 2) as i:
                    for c in (1, 2):
                        p = hidden_panel(n0, c)
                        split(p + 2, i, 6)
                        split(p + 3, i, 6)
                        hidden(c, p, i)
                        split(p + 4, i, 6)
                split(n0 + 34)
                v.wait_ge(panel_done, n0 + 33)
                for b in range(4):
                    v.scalar_tensor_tensor(x[:, 2 * b:2 * b + 2, :], bank[4 + b][:, :].rearrange(
                        "p (t s) -> p t s", t=2), scale, x[:, 2 * b:2 * b + 2, :],
                        ALU.mult, ALU.add).then_inc(x_ready, 1)

            def add_panel(st, k, first=0):
                v.wait_ge(panel_done, st["n0"] + first + k + 1)
                v.tensor_tensor(x[:, 2 * k:2 * k + 2, :], bank[k % PROJ_BANKS][:, :].rearrange(
                    "p (t s) -> p t s", t=2), x[:, 2 * k:2 * k + 2, :], ALU.add).then_inc(x_ready, 1)

            def fourier(st):
                f = st["fourier"]
                for g in range(KT):
                    k = f * KT + g
                    v.wait_ge(dft_hi_ready, k + 1)
                    v.tensor_tensor(h_lo[:, g], bank[6 + g % 2][:, 0:S], h_hi[:, g].bitcast(F32),
                                    ALU.subtract).then_inc(dft_lo_ready, 1)
                for p in range(4):
                    split(st["n0"] + p + 2)
                    add_panel(st, p)

            def s5_prepare():
                are = s5.t[1]
                v.wait_ge(s5_prep, S5_DEN)
                v.reciprocal(are, are).then_inc(s5_trig_ready, 1)

            def s5_product(out_, m, k, f, ahead, sem_part, sem_done):
                tmp = s5.tmp
                for d in range(2):
                    tab = [s5_table(r, ahead, d, f) for r in range(2)]
                    mm = [s5_over_rows(m[:, r], d, f) for r in range(2)]
                    v.tensor_tensor(s5_part(out_[:, 0], d), tab[0], mm[0], ALU.mult)
                    v.tensor_tensor(s5_part(out_[:, 1], d), tab[0], mm[1], ALU.mult)
                    v.tensor_tensor(s5_part(tmp[:, 0], d), tab[1], mm[1], ALU.mult)
                    last = v.tensor_tensor(s5_part(tmp[:, 1], d), tab[1], mm[0], ALU.mult)
                    last.then_inc(sem_part, 1)
                v.wait_ge(sem_part, 2 * (f + 1))
                v.tensor_tensor(out_[:, 0], out_[:, 0], tmp[:, 0], ALU.subtract if k > 0 else ALU.add)
                v.tensor_tensor(out_[:, 1], out_[:, 1], tmp[:, 1], ALU.add if k > 0 else ALU.subtract).then_inc(sem_done, 1)

            def s5_mixer(st):
                v.wait_ge(s5_prep, S5_PREP)
                for f in range(KT):
                    if f >= 2:
                        v.wait_ge(s5_k_ready, f - 1)
                    if f:
                        v.wait_ge(s5_v_ready, f)
                    s5_product(s5.buf[f % 2], s5.b, 1, f, 0, s5_v_part, s5_v_ready)
                v.wait_ge(s5_in_copied, KT)
                n = 0
                pair = [P, 2, S5_G]
                l8 = s5.pow[:, 0, S5_T].unsqueeze(1).to_broadcast(pair)
                m1, m2 = (tmp_flat[:, i * 2 * S5_G:(i + 1) * 2 * S5_G].rearrange("p (r c) -> p r c", r=2) for i in range(2))
                for k in range(1, S5_C - 1):
                    z0, z1 = s5.z[:, :, :, k - 1], s5.z[:, :, :, k]
                    v.tensor_tensor(m1, z0, l8, ALU.mult).then_inc(s5_step, 1)
                    v.tensor_tensor(m2, z0[:, ::-1, :], s5.rot, ALU.mult).then_inc(s5_step, 1)
                    v.wait_ge(s5_step, n + 1)
                    v.tensor_tensor(z1, z1, m1, ALU.add).then_inc(s5_step, 1)
                    v.wait_ge(s5_step, n + 3)
                    v.tensor_tensor(z1, z1, m2, ALU.add).then_inc(s5_step, 1)
                    n += 4
                    v.wait_ge(s5_step, n)

                def add_y(f):
                    v.wait_ge(s5_out_ready, f + 1)
                    v.wait_ge(s5_intra_copied, KT)
                    for e in range(2):
                        yf = s5.y[:, f * KT + e:(f + 1) * KT:2, :]
                        v.tensor_tensor(yf, bank[f % 2 * 2 + e][:, 0:P].rearrange("p (g c) -> p g c", g=KT // 2), yf,
                                        ALU.add).then_inc(s5_y_ready, 1)

                for f in range(KT):
                    if f >= 2:
                        v.wait_ge(s5_out_ready, f - 1)
                    if f:
                        v.wait_ge(s5_w_ready, f)
                    s5_product(s5.buf[f % 2], s5.c, -1, f, 1, s5_w_part, s5_w_ready)
                    if f:
                        add_y(f - 1)
                add_y(KT - 1)
                v.wait_ge(s5_y_loaded, 16 * KT * KT)
                for f in range(KT):
                    v.scalar_tensor_tensor(s5.skip[:, f].rearrange("p (c i) -> p c i", i=S5_T),
                                           h[:, f, :].rearrange("p (c i) -> p c i", i=S5_T), s5.d[:, f:f + 1],
                                           s5.yt[:, f].rearrange("p i c -> p c i"), ALU.mult, ALU.add).then_inc(s5_skip_ready, 1)
                for b in range(4):
                    v.wait_ge(s5_g_hi_ready, b + 1)
                    v.tensor_tensor(h_lo[:, 2 * b:2 * b + 2, :], s5.gelu[:, 2 * b:2 * b + 2, :],
                                    h_hi[:, 2 * b:2 * b + 2, :].bitcast(F32), ALU.subtract).then_inc(s5_g_lo_ready, 1)
                for k in range(4):
                    split(st["n0"] + 2 * k + 2)
                    split(st["n0"] + 2 * k + 3)
                    v.wait_ge(glu_sig_ready, k + 1)
                    v.tensor_tensor(act[:, k % 2], gate[:, k % 2], bank[(2 * k) % PROJ_BANKS][:, :].rearrange(
                        "p (t s) -> p t s", t=2), ALU.mult).then_inc(glu_mul_ready, 1)
                    v.wait_ge(glu_mul_ready, k + 1)
                    xq = x[:, 2 * k:2 * k + 2, :]
                    v.tensor_tensor(xq, act[:, k % 2], xq, ALU.add).then_inc(x_ready, 1)

            def dilated_mixer(st):
                def scale_qk(p, c):
                    hb, g, which = c // 2 // NG, c // 2 % NG, c % 2
                    v.wait_ge(qk_rms_ready, c + 1)
                    v.reciprocal(da.rs[:, c % 2], da.rs[:, c % 2]).then_inc(qk_rstd_ready, 1)
                    v.wait_ge(qk_rstd_ready, c + 1)
                    if hb:
                        v.wait_ge(sc_ready, 2 * HB * hb)
                    v.scalar_tensor_tensor((da.q, da.k)[which][:, g], bank[p % PROJ_BANKS][:, :].rearrange(
                        "p (m n) -> p m n", m=2), da.gain[:, which * NG + g:which * NG + g + 1],
                        da.rs[:, c % 2].rearrange("p (m n) -> p m n", m=2), ALU.mult, ALU.mult).then_inc(qk_ready, 1)

                v.wait_ge(e_loaded, 16 * 5)
                for hb in range(HEADS // HB):
                    for g in range(NG):
                        p, c = (hb * NG + g) * 3, (hb * NG + g) * 2
                        split(st["n0"] + p + 2)
                        split(st["n0"] + p + 3)
                        scale_qk(p, c)
                        split(st["n0"] + p + 4)
                        scale_qk(p + 1, c + 1)

                    def scale_p(u):
                        v.wait_ge(p_ready, u + 1)
                        v.reciprocal(da.stat[:, 3, u:u + 1], da.stat[:, 2, u:u + 1]).then_inc(rden_ready, 1)
                        v.wait_ge(rden_ready, u + 1)
                        v.tensor_scalar(da.sc[:, u % 2], da.sc[:, u % 2], da.stat[:, 3, u:u + 1], None,
                                        ALU.mult).then_inc(p_scaled, 1)

                    u0 = 2 * HB * hb
                    for u in range(u0, u0 + 2 * HB):
                        v.wait_ge(sc_ready, u + 1)
                        v.wait_ge(bias_loaded[u % 3], 16 * (u // 3 + 1))
                        if u >= 2:
                            v.wait_ge(pt_ready, u - 1)
                        v.scalar_tensor_tensor(
                            da.sc[:, u % 2].rearrange("p (g k) -> p g k", g=NG),
                            psum[:, 4:6, :].rearrange("p b n -> p (b n)")[:, 0:NG * S].rearrange("p (g k) -> p g k", g=NG),
                            E ** -0.5, da.bias[:, u % 3, :, ::-1], ALU.mult, ALU.add).then_inc(sc_biased, 1)
                        v.wait_ge(sc_biased, u + 1)
                        v.reduce_max(da.stat[:, 0, u:u + 1], da.sc[:, u % 2], AX.X).then_inc(max_ready, 1)
                        v.wait_ge(max_ready, u + 1)
                        v.tensor_scalar(da.stat[:, 1, u:u + 1], da.stat[:, 0, u:u + 1], -1.0, None,
                                        ALU.mult).then_inc(neg_ready, 1)
                        if u > u0:
                            scale_p(u - 1)
                    scale_p(u0 + 2 * HB - 1)
                for b in range(4):
                    v.wait_ge(o_hi_ready, b + 1)
                    v.tensor_tensor(h_lo[:, 2 * b:2 * b + 2, :], h[:, 2 * b:2 * b + 2, :],
                                    h_hi[:, 2 * b:2 * b + 2, :].bitcast(F32), ALU.subtract).then_inc(o_lo_ready, 1)
                for k in range(4):
                    split(st["n0"] + 36 + k + 2)
                    add_panel(st, k, 36)

            def mixer(st):
                nonlocal n_steps
                i, n0 = st["i"], st["n0"]

                def then(*ins):
                    nonlocal n_steps
                    for q in ins:
                        q.then_inc(mix_step, 1)
                        n_steps += 1
                    v.wait_ge(mix_step, n_steps)

                tt, ts, stt = v.tensor_tensor, v.tensor_scalar, v.scalar_tensor_tensor
                v.wait_ge(mix_loaded, 80 * (i + 1))

                def conv(p):
                    v.wait_ge(mix_copied, 25 * i + p + 1)
                    pair = (2 * p, 2 * p + 1)
                    then(*[ts(mx.conv[:, c], mx.raw[:, c, 0:S], mx.convw[:, c, 0:1], mx.convb[:, c:c + 1],
                              ALU.mult, ALU.add) for c in pair])
                    for k in range(1, CONV):
                        ops = [stt(mx.conv[:, c], mx.raw[:, c, k:k + S], mx.convw[:, c, k:k + 1], mx.conv[:, c],
                                   ALU.mult, ALU.add) for c in pair]
                        if k < CONV - 1:
                            then(*ops)
                        else:
                            for q in ops:
                                q.then_inc(conv_ready, 1)

                for p in range(6):
                    split(n0 + p + 2)
                    conv(p)
                split(n0 + 8)
                d = mx.dt
                v.wait_ge(mix_copied, 25 * i + 7)
                then(ts(d[0], d[0], mx.dtb, None, ALU.add))
                then(ts(d[1], d[0], -1.0, None, ALU.mult))
                tt(d[1], d[0], d[1], ALU.min).then_inc(dt_arg_ready, 1)
                for p in range(7, 11):
                    split(n0 + p + 2)
                v.wait_ge(dt_exp_ready, i + 1)
                then(ts(d[3], d[2], 2.0, None, ALU.add))
                then(v.reciprocal(d[3], d[3]))
                then(tt(d[2], d[2], d[3], ALU.mult))
                then(tt(d[3], d[2], d[2], ALU.mult))
                then(ts(d[4], d[3], 1.0 / (2 * LOG_TERMS + 1), None, ALU.mult))
                for k in range(LOG_TERMS - 1, 0, -1):
                    then(stt(d[4], d[4], 1.0 / (2 * k + 1), d[3], ALU.add, ALU.mult))
                then(stt(d[4], d[4], 1.0, d[2], ALU.add, ALU.mult), ts(d[0], d[0], 0.0, None, ALU.max))
                then(stt(d[0], d[4], 2.0, d[0], ALU.mult, ALU.add))
                v.wait_ge(a_ready, i + 1)
                v.wait_ge(small_set, i + 1)
                then(ts(d[5], d[0], mx.alog, -1.0, ALU.mult, ALU.mult),
                     v.tensor_copy(mx.small[64:64 + SSD_H, :], d[0]))
                v.tensor_tensor_scan(mx.small[0:SSD_H, :], ones[0:SSD_H, 0:1].to_broadcast([SSD_H, S]), d[5], 0.0,
                                     ALU.mult, ALU.add).then_inc(small_ready, 1)
                v.wait_ge(tok_copied, i + 1)
                ts(mx.wi, mx.tok[:, :, 32:32 + IDX_H], IDX_H ** -0.5, None, ALU.mult).then_inc(mix_step, 1)
                n_steps += 1
                v.wait_ge(cb_copied, 2 * i + 2)

                def y_tile(j):
                    v.wait_ge(yp_ready, 8 * i + j + 1)
                    stt(mx.y[:, j], mx.conv[:, j], mx.dskip[:, j:j + 1], bank[6 + j % 2][:, 0:S],
                        ALU.mult, ALU.add).then_inc(y_raw, 1)
                    v.wait_ge(y_raw, 8 * i + j + 1)
                    tt(mx.y[:, j], mx.y[:, j], mx.z[:, j], ALU.mult).then_inc(y_gated, 1)

                for j in range(SSD_H // 2):
                    for e in range(2):
                        hd = 2 * j + e
                        n = SSD_H * i + hd
                        v.wait_ge(cs_ready, n + 1)
                        if n >= 2:
                            v.wait_ge(decay_used, n - 1)
                        stt(mx.dec[:, e, 0], bank[4 + e][:, 0:S], mx.tok[:, 0, hd:hd + 1], mx.tri[:, 0], ALU.subtract, ALU.add)
                        stt(mx.dec[:, e, 1, P:], bank[4 + e][:, P:S], mx.tok[:, 1, hd:hd + 1], mx.tri[:, 1, P:],
                            ALU.subtract, ALU.add).then_inc(decay_arg, 1)
                    split(n0 + 11 + j + 2)
                    for e in range(2):
                        hd = 2 * j + e
                        n = SSD_H * i + hd
                        g = hd // (SSD_H // SSD_G)
                        v.wait_ge(decay_ready, n + 1)
                        if j:
                            v.wait_ge(yp_ready, 8 * i + j)
                        stt(mx.m[:, e, 0], mx.dec[:, e, 0], mx.tok[:, 0, 64 + hd:65 + hd], mx.cb[:, g, 0], ALU.mult, ALU.mult)
                        stt(mx.m[:, e, 1, P:], mx.dec[:, e, 1, P:], mx.tok[:, 1, 64 + hd:65 + hd], mx.cb[:, g, 1, P:],
                            ALU.mult, ALU.mult).then_inc(decay_used, 1)
                    if j:
                        y_tile(j - 1)
                y_tile(SSD_H // 2 - 1)
                for p in range(19, 25):
                    split(n0 + p + 2)
                for g in range(SSD_G):
                    v.wait_ge(yrms_ready, 2 * i + g + 1)
                    then(v.reciprocal(mx.dec[:, g, 0], mx.dec[:, g, 0]))
                    for c in range(4 * g, 4 * g + 4):
                        q = stt(mx.y[:, c], mx.y[:, c], mx.ygain[:, c:c + 1], mx.dec[:, g, 0], ALU.mult, ALU.mult)
                        if c % 2:
                            q.then_inc(y_normed, 1)
                for b in range(4):
                    v.wait_ge(y_hi_ready, 4 * i + b + 1)
                    tt(h_lo[:, 2 * b:2 * b + 2, :], mx.y[:, 2 * b:2 * b + 2, :],
                       h_hi[:, 2 * b:2 * b + 2, :].bitcast(F32), ALU.subtract).then_inc(y_lo_ready, 1)
                v.wait_ge(rope_ready, 1)
                for r in range(11):
                    n = 11 * i + r
                    if r < 8:
                        part = (mx.q, mx.k)[r // 4][0:ROPE_D, 2 * (r % 4):2 * (r % 4) + 2, :]
                    elif r < 10:
                        part = mx.qi[:, 2 * (r - 8):2 * (r - 8) + 2, :]
                    else:
                        part = mx.ki.unsqueeze(1)
                    rows, heads = part.shape[0], part.shape[1]
                    cos, sin = ((rope[0:rows, m + (0 if r < 8 else 2), :].unsqueeze(1).to_broadcast([rows, heads, S]))
                                for m in range(2))
                    tmp = mx.rot[0:rows, r % 4, 0:heads * S].rearrange("p (h s) -> p h s", h=heads)
                    v.wait_ge(rot_ready, n + 1)
                    tt(tmp, bank[4 + r % 4][0:rows, 0:heads * S].rearrange("p (h s) -> p h s", h=heads), sin,
                       ALU.mult).then_inc(rope_used, 1)
                    then(tt(part, part, cos, ALU.mult))
                    v.wait_ge(rope_used, n + 1)
                    tt(part, part, tmp, ALU.add).then_inc(rope_done, 1)
                    if r == 3:
                        for p in range(25, 29):
                            split(n0 + p + 2)
                for qt in range(2):
                    keys = (qt + 1) * P
                    sco = mx.score[:, qt, 0:keys]
                    for hd in range(IDX_H):
                        n = 2 * IDX_H * i + qt * IDX_H + hd
                        u = qt * IDX_H + hd
                        v.wait_ge(relu_ready, n + 1)
                        if hd:
                            v.wait_ge(idx_added, n)
                        if hd == 0:
                            v.wait_ge(mix_step, n_steps)
                            ins = ts(sco, mx.relu[:, u % 4, 0:keys], mx.wi[:, qt, hd:hd + 1], None, ALU.mult)
                        else:
                            ins = stt(sco, mx.relu[:, u % 4, 0:keys], mx.wi[:, qt, hd:hd + 1], sco, ALU.mult, ALU.add)
                        ins.then_inc(idx_added, 1)
                    v.wait_ge(idx_added, 2 * IDX_H * i + (qt + 1) * IDX_H)
                    then(tt(sco, sco, mx.causal[:, qt, 0:keys], ALU.add))
                    for _ in range(TOPK // 8):
                        then(v.max(mx.top8[:, qt], sco))
                        then(v.match_replace(sco, mx.top8[:, qt], sco, TAKEN))
                    sel = mx.sel[:, qt, 0:keys]
                    then(ts(sel, sco, TAKEN / 2, MASKED, ALU.is_gt, ALU.mult))
                    tt(sel, sel, mx.causal[:, qt, 0:keys], ALU.add).then_inc(sel_ready, 1)
                v.wait_ge(sel_ready, 2 * i + 2)
                units = 2 * ATT_H

                def scale_p(u):
                    keys = (u % 2 + 1) * P
                    v.wait_ge(att_p_ready, units * i + u + 1)
                    then(v.reciprocal(mx.stat[:, 3, u:u + 1], mx.stat[:, 2, u:u + 1]))
                    ts(mx.sc[:, u % 2, 0:keys], mx.sc[:, u % 2, 0:keys], mx.stat[:, 3, u:u + 1], None,
                       ALU.mult).then_inc(att_scaled, 1)

                for u in range(units):
                    n, qt = units * i + u, u % 2
                    keys = (qt + 1) * P
                    v.wait_ge(att_sc_ready, n + 1)
                    if u >= 2:
                        v.wait_ge(att_pt_ready, n - 1)
                    stt(mx.sc[:, u % 2, 0:keys], bank[4 + u % 2][:, 0:keys], P ** -0.5, mx.sel[:, qt, 0:keys],
                        ALU.mult, ALU.add).then_inc(att_biased, 1)
                    v.wait_ge(att_biased, n + 1)
                    then(v.reduce_max(mx.stat[:, 0, u:u + 1], mx.sc[:, u % 2, 0:keys], AX.X))
                    ts(mx.stat[:, 1, u:u + 1], mx.stat[:, 0, u:u + 1], -1.0, None, ALU.mult).then_inc(att_neg, 1)
                    if u:
                        scale_p(u - 1)
                scale_p(units - 1)
                for b in range(4):
                    v.wait_ge(att_hi_ready, 4 * i + b + 1)
                    tt(h_lo[:, 2 * b:2 * b + 2, :], mx.yatt[:, 2 * b:2 * b + 2, :],
                       h_hi[:, 2 * b:2 * b + 2, :].bitcast(F32), ALU.subtract).then_inc(att_lo_ready, 1)
                for k in range(4):
                    split(n0 + 29 + k + 2)
                    add_panel(st, k, 29)

            n_steps = 0
            v.memset(zeros[:, :].bitcast(F32), 0.0).then_inc(zeros_set, 1)
            split(0)
            split(1)
            if dilated:
                v.wait_ge(e_ready, 1)
                v.tensor_tensor(da.e, bank[0][0:NG * HEADS, :], da.mask, ALU.add).then_inc(e_masked, 1)
            if any(st["kind"] == "s5" for st in stages):
                s5_prepare()
            todo = {"norm": norm, "final": norm, "ffn": ffn, "fourier": fourier, "s5": s5_mixer,
                    "dilated": dilated_mixer, "mix": mixer}
            for st in stages:
                todo[st["kind"]](st)

        @block.tensor
        def _(t):
            def mm3(o, w, xin, start, stop):
                t.matmul(o, w[0], xin[0], start=start, stop=False, skip_group_check=True)
                t.matmul(o, w[0], xin[1], start=False, stop=False, skip_group_check=True)
                return t.matmul(o, w[1], xin[0], start=False, stop=stop, skip_group_check=True)

            def weights(n, lo, width=P):
                s = n % SLOTS
                return w_hi[:, s, lo:lo + width], w_lo[:, s, lo:lo + width]

            def project(n, j, i=None, per=0):
                t.wait_ge(lo_ready, n + 1 if i is None else i * per + n + 1)
                o = bank[j % PROJ_BANKS]
                for m in range(2):
                    for k in range(KT):
                        last = mm3(o[:, m * S:(m + 1) * S], weights(n, k * COLS + m * P),
                                   (h_hi[:, k], h_lo[:, k]), k == 0, k == KT - 1)
                last.then_inc(panel_done, 1)

            def norm(st):
                n = st["norm"]
                t.wait_ge(const_set, 2)
                for b in range(4):
                    t.wait_ge(sq_ready, 4 * n + b + 1)
                    for c in (2 * b, 2 * b + 1):
                        last = t.matmul(bank[4][:, 0:S], ones[:, :], h[:, c, :], start=(c == 0), stop=(c == KT - 1))
                last.then_inc(ss_ready, 1)

            def ffn(st):
                n0, f = st["n0"], st["ffn"]

                def down(c, p, i=None):
                    def at(val, per):
                        return val if i is None else i * per + val
                    t.wait_ge(lo_ready, at(p + 1, 6))
                    t.wait_ge(act_lo_ready, at(f * FFC + c + 1, 2))
                    for k in range(2):
                        for o in range(KT):
                            last = mm3(y_of[o], weights(p, k * D + o * P),
                                       (act_hi[:, c % 2, k], act_lo[:, c % 2, k]), False, True)
                    last.then_inc(panel_done, 1)

                t.wait_ge(h_lo_ready, 4 * (st["hn"] + 1))
                t.wait_ge(zeros_set, 1)
                for b in range(4):
                    t.matmul(bank[4 + b][:, :].rearrange("p (a m) -> p a m", m=P), zeros[:, :],
                             zeros[:, :].unsqueeze(1).to_broadcast([P, 4, P]), start=True, stop=True)
                project(n0, 0)
                project(n0 + 1, 1)
                with t.Fori(0, (FFC - 1) // 2) as i:
                    for c in (1, 2):
                        p = hidden_panel(n0, c)
                        t.wait_ge(act_ready, i * 2 + (f * FFC + c - 1))
                        project(p, 2 * c, i, 6)
                        project(p + 1, 2 * c + 1, i, 6)
                        down(c - 1, p + 2, i)
                down(FFC - 1, n0 + 32)

            def fourier(st):
                f = st["fourier"]
                t.wait_ge(dft_loaded, 32 * (f + 1))
                t.wait_ge(h_lo_ready, 4 * (st["hn"] + 1))

                def over_channels(g):
                    k = f * KT + g
                    if g >= 2:
                        t.wait_ge(dft_tok_copied, k - 1)
                    for m in range(2):
                        last = t.matmul(bank[4 + g % 2][:, m * S:(m + 1) * S], h[:, g, m * P:(m + 1) * P],
                                        dft_ch, start=True, stop=True)
                    last.then_inc(dft_tok_ready, 1)

                over_channels(0)
                for g in range(KT):
                    k = f * KT + g
                    if g + 1 < KT:
                        over_channels(g + 1)
                    t.wait_ge(dft_tok_copied, k + 1)
                    if g >= 2:
                        t.wait_ge(dft_lo_ready, k - 1)
                    for m in range(2):
                        for c in range(2):
                            last = t.matmul(bank[6 + g % 2][:, 0:S], dft_tok[:, g % 2, m, c * P:(c + 1) * P],
                                            dft_sq[:, m, c, :], start=(m + c == 0), stop=(m + c == 2))
                    last.then_inc(dft_ready, 1)
                t.wait_ge(dft_lo_ready, (f + 1) * KT)
                for p in range(4):
                    project(st["n0"] + p, p)

            def s5_mixer(st):
                half = [slice(0, S5_N), slice(S5_N, P)]
                t.wait_ge(const_loaded, 32)
                t.wait_ge(s5_u_loaded, 16 * S5_T * KT)
                t.wait_ge(s5_prep, S5_PREP)
                for f in range(KT):
                    vb = s5.buf[f % 2]
                    t.wait_ge(s5_v_ready, f + 1)
                    for q in range(4):
                        if 4 * f + q >= 2:
                            t.wait_ge(s5_win_ready, 4 * f + q - 1)
                        for m in range(4):
                            r, c = divmod(4 * q + m, NC)
                            last = t.transpose(bank[4 + q % 2][:, m * P:(m + 1) * P], vb[:, r, c, :], ident[:, :])
                        last.then_inc(s5_vt_ready, 1)
                    if f:
                        t.wait_ge(s5_t_copied, 2 * f)
                    for c in range(NC):
                        for e in range(2):
                            o = bank[6 + e][:, c * S5_P:(c + 1) * S5_P]
                            for r in range(2):
                                last = t.matmul(o, vb[half[e], r, c, :], s5.c[half[e], r, f * NC + c, :],
                                                start=(r == 0), stop=(r == 1))
                    last.then_inc(s5_k_ready, 1)
                    t.wait_ge(s5_win_ready, 4 * f + 4)
                    if f >= 2:
                        t.wait_ge(s5_in_copied, f - 1)
                    for r in range(2):
                        for c in range(NC):
                            for e in range(2):
                                g = f * KT + (c % 4) * 2 + e
                                o = bank[2 + f % 2][half[e], (r * NC + c) * S5_C:(r * NC + c + 1) * S5_C]
                                rhs = s5.u[:, g, :] if c < 4 else s5.u[:, g, ::-1]
                                last = t.matmul(o, s5.win[:, r * NC + c, half[e]], rhs, start=True, stop=True)
                    last.then_inc(s5_in_ready, 1)
                    t.wait_ge(s5_k_copied, 2 * f + 2)
                    for i in range(S5_T):
                        o = bank[7 - i // 4][:, (i % 4) * P:(i % 4 + 1) * P]
                        for d in range(2):
                            off = S5_P * i if d == 0 else 7 * S5_P + S5_P * i
                            last = t.matmul(o, s5.wide[:, off:off + P], s5.kc[:, d * P:(d + 1) * P],
                                            start=(d == 0), stop=(d == 1))
                    last.then_inc(s5_t_ready, 1)
                    t.wait_ge(s5_t_copied, 2 * f + 2)
                    if f >= 2:
                        t.wait_ge(s5_intra_copied, f - 1)
                    for g in range(KT):
                        last = t.matmul(bank[f % 2][:, g * S5_C:(g + 1) * S5_C], s5.tc[:, g].rearrange("p i m -> p (i m)"),
                                        s5.u[:, f * KT + g, :], start=True, stop=True)
                    last.then_inc(s5_intra_ready, 1)
                t.wait_ge(s5_step, 4 * (S5_C - 2))
                t.wait_ge(s5_intra_copied, KT)
                for f in range(KT):
                    wb = s5.buf[f % 2]
                    t.wait_ge(s5_w_ready, f + 1)
                    if f >= 2:
                        t.wait_ge(s5_y_ready, 2 * f - 2)
                    for g in range(KT):
                        e = g % 2
                        o = bank[f % 2 * 2 + e][:, g // 2 * S5_C:(g // 2 + 1) * S5_C]
                        for d in range(2):
                            c = d * 4 + g // 2
                            for r in range(2):
                                z = s5.z[half[e], r, f * NC + c, :]
                                rhs = z[:, 0:S5_C - 1] if d == 0 else z[:, S5_C - 2::-1]
                                last = t.matmul(o[:, 1 - d:S5_C - d], wb[half[e], r, c, :], rhs,
                                                start=(d + r == 0), stop=(d + r == 2), skip_group_check=True)
                    last.then_inc(s5_out_ready, 1)
                t.wait_ge(s5_g_lo_ready, 4)
                for p in range(8):
                    if p >= PROJ_BANKS:
                        t.wait_ge(x_ready, st["xr"] + p // 2 - 1)
                    project(st["n0"] + p, p)

            def project_tokens(n, j):
                t.wait_ge(lo_ready, n + 1)
                for m in range(2):
                    for k in range(KT):
                        cols = slice(m * P, (m + 1) * P)
                        last = mm3(bank[j % PROJ_BANKS][:, m * COLS:(m + 1) * COLS],
                                   (h_hi[:, k, cols], h_lo[:, k, cols]), weights(n, k * COLS, COLS), k == 0, k == KT - 1)
                last.then_inc(panel_done, 1)

            def dilated_mixer(st):
                n0 = st["n0"]

                def free(p):
                    if p >= PROJ_BANKS:
                        b, which = divmod(p - PROJ_BANKS, 3)
                        if which == 2:
                            t.wait_ge(v_copied, b + 1)
                        else:
                            t.wait_ge(qk_ready, 2 * b + which + 1)

                def sums(c):
                    t.wait_ge(qk_sq_ready, c + 1)
                    if c >= 2:
                        t.wait_ge(qk_rms_ready, c - 1)
                    t.matmul(bank[4 + c % 2][:, :], da.pair_ones, da.sq[:, c % 2], start=True, stop=True).then_inc(qk_ss_ready, 1)

                def scores(u):
                    head, qt = u // 2, u % 2
                    m, rows = head // 2 % 2, slice(head % 2 * E, head % 2 * E + E)
                    if u:
                        t.wait_ge(sc_biased, u)
                    for g in range(NG):
                        last = t.matmul(bank[4 + g // 2][:, g % 2 * S:(g % 2 + 1) * S],
                                        da.q[rows, g, m, qt * P:(qt + 1) * P], da.k[rows, g, m, :], start=True, stop=True)
                    last.then_inc(sc_ready, 1)

                def values(u):
                    head, qt = u // 2, u % 2
                    rows = slice(head % 2 * E, head % 2 * E + E)
                    t.wait_ge(p_scaled, u + 1)
                    if u:
                        t.wait_ge(pt_copied, u)
                    for i in range(2 * NG):
                        last = t.transpose(bank[6 + i // 4][:, i % 4 * P:(i % 4 + 1) * P],
                                           da.sc[:, u % 2, i * P:(i + 1) * P], ident[:, :])
                    last.then_inc(pt_ready, 1)

                def out_(u):
                    head, qt = u // 2, u % 2
                    rows = slice(head % 2 * E, head % 2 * E + E)
                    cols = slice(head % HB * E, head % HB * E + E)
                    t.wait_ge(pt_copied, u + 1)
                    if u >= PROJ_BANKS:
                        t.wait_ge(o_copied, u - PROJ_BANKS + 1)
                    for i in range(2 * NG):
                        last = t.matmul(bank[u % PROJ_BANKS][rows, 0:P], da.v[:, i // 2, i % 2, cols],
                                        da.pt[:, u % 2, i * P:(i + 1) * P], start=(i == 0), stop=(i == 2 * NG - 1))
                    last.then_inc(o_ready, 1)

                t.wait_ge(h_lo_ready, 4 * (st["hn"] + 1))
                t.wait_ge(e_loaded, 16 * 5)
                for hb in range(HEADS // HB):
                    if hb:
                        t.wait_ge(o_copied, 2 * HB * hb)
                    for g in range(NG):
                        p, c = (hb * NG + g) * 3, (hb * NG + g) * 2
                        free(p)
                        project(n0 + p, p)
                        free(p + 1)
                        project(n0 + p + 1, p + 1)
                        if hb and g == 0:
                            t.wait_ge(sc_biased, 2 * HB * hb)
                        sums(c)
                        free(p + 2)
                        project_tokens(n0 + p + 2, p + 2)
                        sums(c + 1)
                    u0 = 2 * HB * hb
                    t.wait_ge(qk_ready, 2 * NG * (hb + 1))
                    t.wait_ge(v_copied, NG * (hb + 1))
                    scores(u0)
                    for u in range(u0, u0 + 2 * HB):
                        if u + 1 < u0 + 2 * HB:
                            scores(u + 1)
                        values(u)
                        if u > u0:
                            out_(u - 1)
                    out_(u0 + 2 * HB - 1)
                t.wait_ge(o_lo_ready, 4)
                for k in range(4):
                    project(n0 + 36 + k, k)

            def mixer(st):
                i, n0 = st["i"], st["n0"]

                def arrive(p, tokens=False):
                    if p >= PROJ_BANKS:
                        t.wait_ge(mix_copied, 25 * i + p - PROJ_BANKS + 1)
                    (project_tokens if tokens else project)(n0 + p, p)

                def accumulate(p, k, first):
                    t.wait_ge(lo_ready, n0 + p + 1)
                    for m in range(2):
                        for c in range(KT):
                            last = mm3(bank[k][:, m * S:(m + 1) * S], weights(n0 + p, c * COLS + m * P),
                                       (h_hi[:, c], h_lo[:, c]), first and m == 0 and c == 0, c == KT - 1)
                    last.then_inc(panel_done, 1)

                t.wait_ge(h_lo_ready, 4 * (st["hn"] + 1))
                for p in range(11):
                    arrive(p)
                for q in range(4):
                    t.wait_ge(conv_act, CONV_T * i + 2 * q + 2)
                    if q >= 2:
                        t.wait_ge(xt_copied, 4 * i + q - 1)
                    for tt_ in range(2):
                        for c in range(2):
                            last = t.transpose(bank[5 + q % 2][:, (tt_ * 2 + c) * P:(tt_ * 2 + c + 1) * P],
                                               mx.conv[:, 2 * q + c, tt_ * P:(tt_ + 1) * P], ident[:, :])
                    last.then_inc(xt_ready, 1)
                t.wait_ge(small_ready, i + 1)
                for tt_ in range(2):
                    last = t.transpose(bank[4][:, tt_ * P:(tt_ + 1) * P], mx.small[:, tt_ * P:(tt_ + 1) * P], ident[:, :])
                last.then_inc(tok_ready, 1)
                t.wait_ge(conv_act, CONV_T * (i + 1))
                for g in range(SSD_G):
                    if g:
                        t.wait_ge(tok_copied, i + 1)
                    o = bank[7 if g == 0 else 4]
                    for tt_ in range(2):
                        last = t.matmul(o[:, tt_ * (S + P):2 * S if tt_ else S], mx.conv[:, 8 + g, tt_ * P:(tt_ + 1) * P],
                                        mx.conv[:, 8 + SSD_G + g, tt_ * P:], start=True, stop=True)
                    last.then_inc(cb_ready, 1)
                t.wait_ge(cb_copied, 2 * i + 2)
                t.wait_ge(xt_copied, 4 * i + 4)
                for j in range(SSD_H // 2):
                    for e in range(2):
                        n = SSD_H * i + 2 * j + e
                        if j:
                            t.wait_ge(decay_arg, n - 1)
                        t.matmul(bank[4 + e][:, 0:S], ident[0:SSD_H, 2 * j + e:2 * j + e + 1].to_broadcast([SSD_H, P]),
                                 mx.small[0:SSD_H, :], start=True, stop=True).then_inc(cs_ready, 1)
                    arrive(11 + j)
                    if j >= 2:
                        t.wait_ge(y_raw, 8 * i + j - 1)
                    for e in range(2):
                        hd = 2 * j + e
                        t.wait_ge(decay_used, SSD_H * i + hd + 1)
                        o = bank[6 + j % 2][e * SSD_P:(e + 1) * SSD_P, :]
                        heads = slice(hd * SSD_P, (hd + 1) * SSD_P)
                        t.matmul(o[:, 0:P], mx.xt[:, 0, heads], mx.m[:, e, 0, 0:P], start=True, stop=True)
                        t.matmul(o[:, P:S], mx.xt[:, 0, heads], mx.m[:, e, 0, P:], start=True, stop=False)
                        last = t.matmul(o[:, P:S], mx.xt[:, 1, heads], mx.m[:, e, 1, P:], start=False, stop=True)
                    last.then_inc(yp_ready, 1)
                for p in range(19, 25):
                    arrive(p, p >= 21)
                for g in range(SSD_G):
                    t.wait_ge(ysq_ready, 2 * i + g + 1)
                    for c in range(4):
                        last = t.matmul(bank[4 + g][:, 0:S], ones[:, :], mx.z[:, 4 * g + c], start=(c == 0), stop=(c == 3))
                    last.then_inc(yss_ready, 1)
                t.wait_ge(y_raw, 8 * i + 8)
                t.wait_ge(yrms_ready, 2 * i + 2)
                t.wait_ge(mix_copied, 25 * (i + 1))
                for r in range(11):
                    if r >= 4:
                        t.wait_ge(rope_used, 11 * i + r - 3)
                    if r < 8:
                        src = (mx.q, mx.k)[r // 4][0:ROPE_D, 2 * (r % 4):2 * (r % 4) + 2, :].rearrange("p h s -> p (h s)")
                        last = t.matmul(bank[4 + r % 4][0:ROPE_D, :], mx.turn[0:ROPE_D, :], src, start=True, stop=True)
                    elif r < 10:
                        src = mx.qi[:, 2 * (r - 8):2 * (r - 8) + 2, :].rearrange("p h s -> p (h s)")
                        last = t.matmul(bank[4 + r % 4][:, :], mx.turn_i, src, start=True, stop=True)
                    else:
                        last = t.matmul(bank[4 + r % 4][:, 0:S], mx.turn_i, mx.ki, start=True, stop=True)
                    last.then_inc(rot_ready, 1)
                    if r == 3:
                        t.wait_ge(y_lo_ready, 4 * (i + 1))
                        for k in range(4):
                            accumulate(25 + k, k, True)
                t.wait_ge(rope_done, 11 * (i + 1))
                for u in range(2 * IDX_H):
                    qt, hd = divmod(u, IDX_H)
                    rows = slice(hd % 2 * E, hd % 2 * E + E)
                    n = 2 * IDX_H * i + u
                    if u >= 4:
                        t.wait_ge(relu_ready, n - 3)
                    t.matmul(bank[4 + u % 4][:, 0:(qt + 1) * P], mx.qi[rows, hd // 2, qt * P:(qt + 1) * P],
                             mx.ki[rows, 0:(qt + 1) * P], start=True, stop=True).then_inc(idx_ready, 1)
                units = 2 * ATT_H

                def scores(u):
                    hd, qt = divmod(u, 2)
                    if u >= 2:
                        t.wait_ge(att_biased, units * i + u - 1)
                    t.matmul(bank[4 + u % 2][:, 0:(qt + 1) * P], mx.q[:, hd, qt * P:(qt + 1) * P],
                             mx.k[:, hd, 0:(qt + 1) * P], start=True, stop=True).then_inc(att_sc_ready, 1)

                def values(u):
                    qt = u % 2
                    t.wait_ge(att_scaled, units * i + u + 1)
                    if u:
                        t.wait_ge(att_pt_copied, units * i + u)
                    for k in range(qt + 1):
                        last = t.transpose(bank[6][:, k * P:(k + 1) * P], mx.sc[:, u % 2, k * P:(k + 1) * P], ident[:, :])
                    last.then_inc(att_pt_ready, 1)

                def out_(u):
                    hd, qt = divmod(u, 2)
                    t.wait_ge(att_pt_copied, units * i + u + 1)
                    if u:
                        t.wait_ge(att_o_copied, units * i + u)
                    for k in range(qt + 1):
                        last = t.matmul(bank[7][:, u % 2 * P:(u % 2 + 1) * P], mx.v[:, k, hd * P:(hd + 1) * P],
                                        mx.pt[:, u % 2, k * P:(k + 1) * P], start=(k == 0), stop=(k == qt))
                    last.then_inc(att_o_ready, 1)

                t.wait_ge(relu_ready, 2 * IDX_H * (i + 1))
                scores(0)
                for u in range(units):
                    if u + 1 < units:
                        scores(u + 1)
                    values(u)
                    if u:
                        out_(u - 1)
                out_(units - 1)
                t.wait_ge(att_lo_ready, 4 * (i + 1))
                for k in range(4):
                    accumulate(29 + k, k, False)

            if dilated:
                t.wait_ge(e_loaded, 16 * 3)
                t.matmul(bank[0][0:NG * HEADS, :], da.rel, da.onehot, start=True, stop=True).then_inc(e_ready, 1)
            todo = {"norm": norm, "final": norm, "ffn": ffn, "fourier": fourier, "s5": s5_mixer,
                    "dilated": dilated_mixer, "mix": mixer}
            for st in stages:
                todo[st["kind"]](st)


def panel_of(w, c0):
    return w[:, c0:c0 + COLS].reshape(KT, P, COLS).transpose(1, 0, 2).reshape(P, PANEL)


def rows_panel(w, c):
    return w[c * COLS:(c + 1) * COLS].reshape(2, P, D).transpose(1, 0, 2).reshape(P, PANEL)


def ffn_panels(w_in, w_out):
    yield panel_of(w_in, 0)
    yield panel_of(w_in, FF)
    for c in range(1, FFC):
        yield panel_of(w_in, c * COLS)
        yield panel_of(w_in, FF + c * COLS)
        yield rows_panel(w_out, c - 1)
    yield rows_panel(w_out, FFC - 1)


def gain_columns(g):
    return g.reshape(-1, KT, P).transpose(2, 0, 1).reshape(P, -1)


def lay_out(inp):
    x = np.asarray(inp["x"])[0]
    a = {"x": np.ascontiguousarray(x.T)}
    panels = []
    rows = []
    for i in range(BLOCK1):
        rows += [inp["norm_mix_g"][i], inp["norm_ffn_g"][i]]
        if i % 3 == 0:
            panels += [panel_of(inp["fnet_w_out"][i // 3], c * COLS) for c in range(4)]
        if i % 3 == 1:
            w = inp["s5_w_glu"][i // 3]
            panels += [panel_of(w, c * COLS + m * D) for c in range(4) for m in range(2)]
        if i % 3 == 2:
            w = inp["attn_w_qkv"][i // 3]
            panels += [panel_of(w, (g * 3 + m) * D + b * COLS) for b in range(HEADS // HB) for g in range(NG) for m in range(3)]
            panels += [panel_of(inp["attn_w_o"][i // 3], c * COLS) for c in range(4)]
        panels += ffn_panels(inp["ffn_w_gate_up"][i], inp["ffn_w_down"][i])
    cols = []
    for i in range(BLOCK2):
        rows += [inp["norm_ffn1_2"][i], inp["norm_mix_2"][i], inp["norm_ffn2_2"][i]]
        panels += ffn_panels(inp["w_ffn1_in_2"][i], inp["w_ffn1_out_2"][i])
        w = inp["w_mix_in_2"][i]
        sizes = (D, CONV_T * P, SSD_H, D, D, D, IDX_H * E, E, IDX_H)
        z, xbc, dt, q, k, v, qi, ki, wi = np.split(w, np.cumsum(sizes)[:-1], 1)
        misc = np.zeros((D, COLS), np.float32)
        misc[:, 0:E], misc[:, E:2 * E] = ki, ki
        misc[:, P:P + SSD_H], misc[:, P + 32:P + 32 + IDX_H] = dt, wi
        for part in (xbc, misc, z, qi, q, k, v, inp["w_mix_out_2"][i][:D], inp["w_mix_out_2"][i][D:]):
            panels += [panel_of(part, c) for c in range(0, part.shape[1], COLS)]
        panels += ffn_panels(inp["w_ffn2_in_2"][i], inp["w_ffn2_out_2"][i])
        tail = np.zeros((P, 3), np.float32)
        tail[:SSD_H, 0], tail[:SSD_H, 1] = inp["dt_bias_2"][i], inp["a_log_2"][i]
        cols.append(np.concatenate([
            inp["conv_w_2"][i].reshape(CONV, CONV_T, P).transpose(2, 1, 0).reshape(P, -1),
            inp["conv_b_2"][i].reshape(CONV_T, P).T,
            np.repeat(inp["d_skip_2"][i], SSD_P).reshape(KT, P).T,
            inp["ssd_norm_2"][i].reshape(KT, P).T, tail], 1))
    a["mix_col"] = np.stack(cols)
    rows.append(inp["final_norm_2"])
    a["gains"] = gain_columns(np.stack(rows))
    tok = np.arange(S).reshape(2, P).T[:, :, None]
    along = np.arange(S)[None, None, :]
    a["mask_tri"] = np.where(along >= tok, 0.0, MASKED).astype(np.float32)
    a["mask_causal"] = np.where(along <= tok, 0.0, MASKED).astype(np.float32)
    a["positions"] = np.broadcast_to(inp["positions_2"], (P, S)).astype(np.int32)

    def freqs(rot):
        return np.float32(ROPE_THETA) ** (-np.arange(0, rot, 2, dtype=np.float32) / np.float32(rot))

    def turned(rot):
        half = rot // 2
        m = np.zeros((rot, rot), np.float32)
        m[np.arange(half) + half, np.arange(half)] = -1
        m[np.arange(half), np.arange(half) + half] = 1
        return m

    a["turn"] = turned(ROPE_D)
    a["turn_i"] = np.zeros((P, P), np.float32)
    freq = np.zeros((P, 2), np.float32)
    freq[:ROPE_D, 0] = np.tile(freqs(ROPE_D), 2)
    for half in (0, E):
        a["turn_i"][half:half + ROPE_I, half:half + ROPE_I] = turned(ROPE_I)
        freq[half:half + ROPE_I, 1] = np.tile(freqs(ROPE_I), 2)
    a["rope_freq"] = freq
    k = np.arange(P)
    ang = 2 * np.pi * (np.outer(k, k) % P) / P
    a["dft_ch"] = np.concatenate([np.cos(ang), -np.sin(ang)], 1).astype(np.float32)
    k = np.arange(S)
    ang = 2 * np.pi * (np.outer(k, k) % S) / S
    scale = 1.0 / np.sqrt(S * P)
    a["dft_sq"] = (np.concatenate([np.cos(ang), np.sin(ang)], 1) * scale).astype(np.float32)
    a["rel_bias"] = inp["rel_bias"]
    rel = S - 1 - np.arange(2 * S)
    half = BUCKETS // 2
    exact = half // 2
    n = np.abs(rel)
    large = exact + (np.log(np.maximum(n, 1) / exact) / np.log(MAX_DISTANCE / exact) * (half - exact)).astype(np.int32)
    bucket = (rel > 0) * half + np.where(n < exact, n, np.minimum(large, half - 1))
    a["bucket_onehot"] = (bucket[None] == np.arange(BUCKETS)[:, None]).astype(np.float32)
    allowed = np.stack([(n % dil == 0) & (n // dil <= window // 2 // dil) for window, dil in GROUPS])
    a["group_mask"] = np.repeat(np.where(allowed, 0.0, MASKED).astype(np.float32), HEADS, 0)
    a["pair_ones"] = np.kron(np.eye(2), np.ones((E, E))).astype(np.float32)
    gains = np.concatenate([inp["attn_q_gain"][0], inp["attn_k_gain"][0]])
    a["qk_gain"] = np.tile(gains, (1, 2)).T
    a["ident"] = np.eye(P, dtype=np.float32)

    def s5_columns(w):
        w = w.reshape((2, KT, 4, 2, S5_N) + w.shape[3:])
        w = w.transpose((3, 4, 1, 0, 2) + tuple(range(5, w.ndim)))
        return w.reshape(P, -1)

    lam = [inp["s5_lambda_re"][0], inp["s5_lambda_im"][0],
           np.broadcast_to(inp["s5_log_dt"][0][:, :, None], (2, S5_G, S5_N))]
    a["s5_lam"] = np.concatenate([s5_columns(w) for w in lam], 1)
    a["s5_b"] = np.concatenate([s5_columns(inp["s5_b_" + r][0]) for r in ("re", "im")], 1)
    a["s5_c"] = np.concatenate([s5_columns(inp["s5_c_" + r][0].transpose(0, 1, 3, 2)) for r in ("re", "im")], 1)
    a["s5_d"] = gain_columns(inp["s5_d"])
    a["s5_wide"] = np.eye(P, 352, 112, dtype=np.float32)
    return a, panels


def kernel(**inputs):
    import concourse.bacc as bacc
    from concourse.bass_utils import run_bass_kernel_spmd

    data, panels = lay_out({name: np.asarray(value) for name, value in inputs.items()})
    data["panels"] = np.stack(panels + [panels[-1]])
    nc = bacc.Bacc("TRN2", target_bir_lowering=False, num_devices=1)
    arrays = {"in_" + name: np.ascontiguousarray(value) for name, value in data.items()}
    dram = {name: nc.dram_tensor("in_" + name, value.shape, mybir.dt.from_np(value.dtype), kind="ExternalInput").ap()
            for name, value in data.items()}
    out = nc.dram_tensor("out", (D, S), F32, kind="ExternalOutput").ap()
    build(nc, dram, out)
    got = run_bass_kernel_spmd(nc, [arrays], core_ids=[0]).results[0]["out"]
    return np.ascontiguousarray(np.asarray(got).T)[None]
```

```python
from contextlib import ExitStack

import numpy as np
import concourse.bass as bass
from concourse import mybir
from concourse.alu_op_type import AluOpType as ALU

F32 = mybir.dt.float32
F32R = mybir.dt.float32r
ACT = mybir.ActivationFunctionType
AX = mybir.AxisListType

P = 128
D = 1024
S = 256
KT = D // P
FF = 2816
COLS = 256
PANEL = KT * COLS
FFC = FF // COLS
SLOTS = 3
PROJ_BANKS = 4
EPS = 1e-6
TWO_PI = 2 * np.pi
TWO_PI_1 = 6.28125
TWO_PI_2 = float(np.float32(1.93500518798828125e-3))
TWO_PI_3 = TWO_PI - TWO_PI_1 - TWO_PI_2
ROUND = 1.5 * 2.0 ** 23
PI_BELOW = float(np.nextafter(np.float32(np.pi), np.float32(0)))
MASKED = -1e30
HEADS = 16
E = 64
GROUPS = ((128, 1), (512, 4), (2048, 16))
NG = len(GROUPS)
BUCKETS = 32
MAX_DISTANCE = 1024
HB = 4
SSD_H = 16
SSD_P = 64
SSD_G = 2
SSD_N = 128
CONV = 4
CONV_T = (SSD_H * SSD_P + 2 * SSD_G * SSD_N) // P
ATT_H = 8
IDX_H = 8
TOPK = min(256, S // 4)
ROPE_THETA = 500000.0
ROPE_D = P // 4
ROPE_I = E // 4
TAKEN = -3e38
LOG_TERMS = 8
S5_T = 8
S5_C = S // S5_T
S5_P = 16
S5_N = 64
S5_G = D // S5_P
BLOCK1 = 4
BLOCK2 = 2


def plan_stages():
    stages = []
    panel = xr = norm = ffn = split = 0
    mixers = ["fourier", "s5", "dilated", "fourier"]
    todo = []
    for i in range(BLOCK1):
        todo += [("norm", i), (mixers[i], i), ("norm", BLOCK1 + i), ("ffn", i)]
    for i in range(BLOCK2):
        b = 2 * BLOCK1 + 3 * i
        todo += [("norm", b), ("ffn", BLOCK1 + 2 * i), ("norm", b + 1), ("mix", i),
                 ("norm", b + 2), ("ffn", BLOCK1 + 2 * i + 1)]
    todo.append(("final", 2 * BLOCK1 + 3 * BLOCK2))
    panels_of = {"fourier": 4, "s5": 8, "dilated": 40, "ffn": 3 * FFC, "mix": 25 + 8}
    for kind, i in todo:
        st = {"kind": kind, "i": i, "n0": panel, "xr": xr}
        if kind in ("norm", "final"):
            st["norm"] = norm
            norm += 1
            st["split"] = kind == "norm" and todo[len(stages) + 1][0] != "s5"
            st["hs"] = split
            split += st["split"]
        else:
            xr += 4
            panel += panels_of[kind]
        st["hn"] = norm - 1
        st.setdefault("hs", split - 1)
        if kind == "ffn":
            st["ffn"] = ffn
            ffn += 1
        stages.append(st)
    return stages, panel


def build(nc, A, out, stop=None):
    stages, n_panels = plan_stages()
    if stop is not None:
        stages = stages[:stop]
    final = stages[-1]["kind"] == "final"

    with ExitStack() as ctx:
        def sb(name, shape, dt=F32):
            return ctx.enter_context(nc.sbuf_tensor(name, shape, dt))

        def sem(name):
            return ctx.enter_context(nc.semaphore(name))

        raw = sb("raw", [P, SLOTS, PANEL])
        w_hi = sb("w_hi", [P, SLOTS, PANEL], F32R)
        w_lo = sb("w_lo", [P, SLOTS, PANEL], F32R)
        x = sb("x", [P, KT, S])
        h = sb("h", [P, KT, S])
        h_hi = sb("h_hi", [P, KT, S], F32R)
        h_lo = sb("h_lo", [P, KT, S], F32R)
        rstd = sb("rstd", [P, S])
        gains = sb("gains", [P, A["gains"].shape[1]])
        ones = sb("ones", [P, P])
        zeros = sb("zeros", [P, P], F32R)
        eps = sb("eps", [P, 1])
        eps_head = sb("eps_head", [P, 1])
        warm = sb("warm", [P, 1])
        hidden = sb("hidden", [P, 2, 2, 2, S])
        gate, act = hidden[:, 0], hidden[:, 1]
        act_hi = sb("act_hi", [P, 2, 2, S], F32R)
        act_lo = sb("act_lo", [P, 2, 2, S], F32R)
        ident = sb("ident", [P, P])
        rope = sb("rope", [P, 4, S])
        arena = sb("arena", [P, 20672])

        psum = ctx.enter_context(nc.psum_tensor("psum", [P, 8, 512], F32))
        bank = [psum[:, i, :] for i in range(8)]

        panel_loaded = [sem(f"panel_loaded{i}") for i in range(SLOTS)]
        hi_ready = sem("hi_ready")
        lo_ready = sem("lo_ready")
        panel_done = sem("panel_done")
        x_loaded = sem("x_loaded")
        const_loaded = sem("const_loaded")
        const_set = sem("const_set")
        zeros_set = sem("zeros_set")
        x_ready = sem("x_ready")
        sq_ready = sem("sq_ready")
        ss_ready = sem("ss_ready")
        rms_ready = sem("rms_ready")
        rstd_ready = sem("rstd_ready")
        h_ready = sem("h_ready")
        h_hi_ready = sem("h_hi_ready")
        h_lo_ready = sem("h_lo_ready")
        gate_ready = sem("gate_ready")
        sums_ready = sem("sums_ready")
        act_ready = sem("act_ready")
        act_hi_ready = sem("act_hi_ready")
        act_lo_ready = sem("act_lo_ready")
        dft_loaded = sem("dft_loaded")
        dft_tok_ready = sem("dft_tok_ready")
        dft_tok_copied = sem("dft_tok_copied")
        dft_ready = sem("dft_ready")
        dft_hi_ready = sem("dft_hi_ready")
        dft_lo_ready = sem("dft_lo_ready")
        s5_loaded = sem("s5_loaded")
        s5_dt_ready = sem("s5_dt_ready")
        s5_prep = sem("s5_prep")
        s5_trig_ready = sem("s5_trig_ready")
        s5_hperm_ready = sem("s5_hperm_ready")
        s5_u_stored = {n: sem(f"s5_u_stored_{n}") for n in ("act", "pool")}
        s5_u_loaded = sem("s5_u_loaded")
        s5_v_part = sem("s5_v_part")
        s5_v_ready = sem("s5_v_ready")
        s5_vt_ready = sem("s5_vt_ready")
        s5_win_ready = sem("s5_win_ready")
        s5_k_ready = sem("s5_k_ready")
        s5_k_copied = sem("s5_k_copied")
        s5_t_ready = sem("s5_t_ready")
        s5_t_copied = sem("s5_t_copied")
        s5_intra_ready = sem("s5_intra_ready")
        s5_intra_copied = sem("s5_intra_copied")
        s5_in_ready = sem("s5_in_ready")
        s5_in_copied = sem("s5_in_copied")
        s5_step = sem("s5_step")
        s5_w_part = sem("s5_w_part")
        s5_w_ready = sem("s5_w_ready")
        s5_out_ready = sem("s5_out_ready")
        s5_y_ready = sem("s5_y_ready")
        s5_y_stored = {n: sem(f"s5_y_stored_{n}") for n in ("act0", "act1", "pool1")}
        s5_y_loaded = [sem(f"s5_y_loaded{i}") for i in range(2)]
        s5_cbd_ready = sem("s5_cbd_ready")
        s5_zbd_set = sem("s5_zbd_set")
        s5_zbd_ready = sem("s5_zbd_ready")
        s5_wp_part = sem("s5_wp_part")
        s5_wp_ready = sem("s5_wp_ready")
        s5_skip_ready = sem("s5_skip_ready")
        s5_gelu_ready = sem("s5_gelu_ready")
        s5_g_hi_ready = sem("s5_g_hi_ready")
        s5_g_lo_ready = sem("s5_g_lo_ready")
        glu_sig_ready = sem("glu_sig_ready")
        glu_mul_ready = sem("glu_mul_ready")
        e_loaded = sem("e_loaded")
        e_ready = sem("e_ready")
        e_masked = sem("e_masked")
        e_stored = sem("e_stored")
        qk_sq_ready = sem("qk_sq_ready")
        qk_ss_ready = sem("qk_ss_ready")
        qk_rms_ready = sem("qk_rms_ready")
        qk_rstd_ready = sem("qk_rstd_ready")
        qk_copied = sem("qk_copied")
        qk_ready = sem("qk_ready")
        v_copied = sem("v_copied")
        bias_loaded = [sem(f"bias_loaded{i}") for i in range(3)]
        sc_ready = sem("sc_ready")
        sc_biased = sem("sc_biased")
        max_ready = sem("max_ready")
        neg_ready = sem("neg_ready")
        p_ready = sem("p_ready")
        rden_ready = sem("rden_ready")
        p_scaled = sem("p_scaled")
        pt_ready = sem("pt_ready")
        pt_copied = sem("pt_copied")
        o_ready = sem("o_ready")
        o_copied = sem("o_copied")
        o_hi_ready = sem("o_hi_ready")
        o_lo_ready = sem("o_lo_ready")
        pos_loaded = sem("pos_loaded")
        rope_step = sem("rope_step")
        rope_angle = sem("rope_angle")
        rope_sin = sem("rope_sin")
        rope_squared = sem("rope_squared")
        rope_ready = sem("rope_ready")
        mix_loaded = sem("mix_loaded")
        pad_set = sem("pad_set")
        mix_copied = sem("mix_copied")
        conv_ready = sem("conv_ready")
        conv_act = sem("conv_act")
        dt_exp_ready = sem("dt_exp_ready")
        dt_arg_ready = sem("dt_arg_ready")
        a_ready = sem("a_ready")
        small_set = sem("small_set")
        small_ready = sem("small_ready")
        tok_ready = sem("tok_ready")
        tok_copied = sem("tok_copied")
        xt_ready = sem("xt_ready")
        xt_copied = sem("xt_copied")
        cb_ready = sem("cb_ready")
        cb_copied = sem("cb_copied")
        cs_ready = sem("cs_ready")
        decay_arg = sem("decay_arg")
        decay_ready = sem("decay_ready")
        decay_used = sem("decay_used")
        yp_ready = sem("yp_ready")
        y_raw = sem("y_raw")
        y_gated = sem("y_gated")
        ysq_ready = sem("ysq_ready")
        yss_ready = sem("yss_ready")
        yrms_ready = sem("yrms_ready")
        y_normed = sem("y_normed")
        y_hi_ready = sem("y_hi_ready")
        y_lo_ready = sem("y_lo_ready")
        rot_ready = sem("rot_ready")
        rope_used = sem("rope_used")
        rope_done = sem("rope_done")
        idx_ready = sem("idx_ready")
        relu_ready = sem("relu_ready")
        idx_added = sem("idx_added")
        sel_ready = sem("sel_ready")
        att_sc_ready = sem("att_sc_ready")
        att_biased = sem("att_biased")
        att_neg = sem("att_neg")
        att_p_ready = sem("att_p_ready")
        att_scaled = sem("att_scaled")
        att_pt_ready = sem("att_pt_ready")
        att_pt_copied = sem("att_pt_copied")
        att_o_ready = sem("att_o_ready")
        att_o_copied = sem("att_o_copied")
        att_hi_ready = sem("att_hi_ready")
        att_lo_ready = sem("att_lo_ready")
        mix_step = sem("mix_step")
        stored = sem("stored")

        block = ctx.enter_context(nc.Block())

        y_of = [bank[4 + o // 2][:, (o % 2) * S:(o % 2 + 1) * S] for o in range(KT)]

        def hidden_panel(n0, c):
            return n0 if c == 0 else n0 + 2 + 3 * (c - 1)

        dft_ch = arena[:, 0:S]
        dft_sq = arena[:, S:S + 2 * 2 * S].rearrange("p (t f s) -> p t f s", t=2, f=2)
        dft_tok = arena[:, 5 * S:5 * S + 2 * 2 * S].rearrange("p (b t n) -> p b t n", b=2, t=2)

        NC = 8

        class s5:
            at = 0

            @classmethod
            def take(cls, n):
                cls.at += n
                return arena[:, cls.at - n:cls.at]

        s5.z = s5.take(2 * S5_G * S5_C).rearrange("p (r c k) -> p r c k", r=2, c=S5_G)
        s5.hperm = s5.z[:, 0].rearrange("p c k -> p (c k)").rearrange("p (f t c) -> p f t c", f=KT, t=S5_T)
        u_flat = s5.take(S5_G * S5_C)
        s5.u = u_flat.rearrange("p (g c) -> p g c", g=S5_G)
        s5.buf = [s5.take(2 * NC * P).rearrange("p (r c m) -> p r c m", r=2, c=NC) for _ in range(2)]
        win_flat = s5.take(2 * NC * P)
        s5.win = win_flat.rearrange("p (m q) -> p m q", m=2 * NC)
        b_flat = s5.take(2 * S5_G * S5_P)
        s5.b = b_flat.rearrange("p (r c m) -> p r c m", r=2, c=S5_G)
        s5.c = s5.take(2 * S5_G * S5_P).rearrange("p (r c m) -> p r c m", r=2, c=S5_G)
        s5.pow = s5.take(2 * (S5_T + 1) * S5_G).rearrange("p (r k c) -> p r k c", r=2, k=S5_T + 1)
        tmp_flat = s5.take(2 * NC * P)
        s5.tmp = tmp_flat[:, NC * P:].rearrange("p (r c m) -> p r c m", r=2, c=NC // 2)
        s5.kc = s5.take(2 * P)
        s5.tc = rope[:, :, :].rearrange("p r s -> p (r s)").rearrange("p (g i m) -> p g i m", g=KT, i=S5_T)
        s5.wide = win_flat
        s5.rot = s5.take(2 * S5_G).rearrange("p (r c) -> p r c", r=2)
        s5.d = s5.take(KT)
        s5.wide = s5.take(352)
        y_flat = hidden[:, :, :, :, :].rearrange("p a b t s -> p (a b t s)")
        s5.y = y_flat.rearrange("p (g c) -> p g c", g=S5_G)
        s5.w = s5.buf + [v.rearrange("p (r c m) -> p r c m", r=2, c=NC) for v in (win_flat, b_flat)]
        s5.wtmp = s5.tc.rearrange("p g i m -> p (g i m)").rearrange("p (r c m) -> p r c m", r=2, c=NC // 2)
        s5.cbd = tmp_flat[:, 0:2 * 2 * NC * 2 * S5_P].rearrange("p (b r c n) -> p b r c n", b=2, r=2, c=NC)
        s5.zbd = u_flat.rearrange("p (b r c n) -> p b r c n", b=2, r=2, c=NC)
        s5.yt = tmp_flat.rearrange("p (f t c) -> p f t c", f=KT, t=S5_T)
        s5.par = win_flat[:, 0:3 * S5_G].rearrange("p (r c) -> p r c", r=3)
        s5.t = [win_flat[:, (3 + i) * S5_G:(4 + i) * S5_G] for i in range(16)]
        assert s5.at <= arena.shape[1], s5.at
        u_dram = nc.dram_tensor("s5_u", (S5_T, S5_P, KT, KT, S5_C), F32, kind="Internal").ap()
        y_dram = nc.dram_tensor("s5_y", (2, KT, S5_P, KT // 2, S5_T, S5_C), F32, kind="Internal").ap()
        W_POOL = (0, 1, 2, 5)

        def s5_table(r, ahead, d, f):
            c0 = f * NC + d * NC // 2
            cols = slice(c0, c0 + NC // 2)
            if d == 0:
                tab = s5.pow[:, r, ahead:ahead + S5_T, cols]
            else:
                tab = s5.pow[:, r, S5_T - 1 + ahead:(ahead - 1 if ahead else None):-1, cols]
            return tab.rearrange("p k c -> p c k").unsqueeze(3).to_broadcast([P, NC // 2, S5_T, S5_P])

        def s5_over_rows(v, d, f):
            c0 = f * NC + d * NC // 2
            return v[:, c0:c0 + NC // 2, :].unsqueeze(2).to_broadcast([P, NC // 2, S5_T, S5_P])

        def s5_part(v, d):
            return v[:, d * NC // 2:(d + 1) * NC // 2, :].rearrange("p c (k m) -> p c k m", k=S5_T)

        def s5_store_u(eng, groups, stored):
            for g in groups:
                eng.dma_start(u_dram[:, :, :, g, :].rearrange("r m f c -> m f r c"),
                              s5.hperm[g * S5_P:(g + 1) * S5_P]).then_inc(stored, 16)

        def s5_store_y(eng, half, rows, stored):
            n = S5_G * S5_C // 2
            for i in rows:
                eng.dma_start(y_dram[half, :, :, :, i, :].rearrange("g m f c -> m f g c"),
                              y_flat[i * S5_P:(i + 1) * S5_P, half * n:(half + 1) * n].rearrange(
                                  "m (f g c) -> m f g c", f=KT // 2, g=KT)).then_inc(stored, 16)

        def s5_load_y(eng, half):
            tiles = slice(half * KT // 2, (half + 1) * KT // 2)
            eng.dma_start(s5.yt[:, tiles].rearrange("p f t c -> p (f t c)"),
                          y_dram[half].rearrange("g m f i c -> (g m) (f i c)")).then_inc(s5_y_loaded[half], 16)

        assert all(d % 2 == 0 for _, d in GROUPS[1:]) and GROUPS[0][1] == 1
        UNITS = 2 * HB
        QK = 2 * NG
        PANELS = 3 * NG
        BLOCKS = HEADS // HB

        def da_bank(u):
            return bank[3] if u >= (BLOCKS - 1) * UNITS and u % 2 else bank[4]

        def da_panels(u):
            hb, s = divmod(u, UNITS)
            if hb + 1 == BLOCKS:
                return []
            more = PANELS - UNITS
            p = (hb + 1) * PANELS
            return list(range(p, p + more + 1)) if s == 0 else [p + more + s]

        def da_panel(p):
            hb, i = divmod(p, PANELS)
            return hb, i, hb * QK + i if i < QK else hb * NG + i - QK
        class da:
            at = 0

            @classmethod
            def take(cls, n):
                cls.at += n
                return arena[:, cls.at - n:cls.at]

        da.qk = da.take(2 * 2 * NG * 2 * S).rearrange("p (b w g m s) -> p b w g m s", b=2, w=2, g=NG, m=2)
        da.v = da.take(2 * NG * 2 * S).rearrange("p (b g m s) -> p b g m s", b=2, g=NG, m=2)
        da.sq = da.take(2 * 2 * S).rearrange("p (b n) -> p b n", b=2)
        da.rs = da.take(2 * 2 * S).rearrange("p (b n) -> p b n", b=2)
        da.rq = da.take(2 * NG * UNITS).rearrange("p (b g m t e) -> p b g m t e", b=2, g=NG, m=2, t=2)
        da.sc = da.take(3 * 2 * S).rearrange("p (b n) -> p b n", b=3)
        da.pt = da.take(2 * 2 * S).rearrange("p (b n) -> p b n", b=2)
        da.bias = da.take(3 * NG * S).rearrange("p (b g k) -> p b g k", b=3, g=NG)
        da.pair_ones = da.take(P)
        da.gain = da.take(2 * NG)
        n_units = HEADS * 2
        da.stat = da.take(4 * n_units).rearrange("p (r u) -> p r u", r=4)
        e_at, e_w = 9 * S, 2 * S
        da.rel = arena[0:BUCKETS, e_at:e_at + NG * HEADS]
        e_at += NG * HEADS
        da.onehot = arena[0:BUCKETS, e_at:e_at + e_w]
        da.mask = arena[0:NG * HEADS, e_at + e_w:e_at + 2 * e_w]
        da.e = arena[0:NG * HEADS, e_at + 2 * e_w:e_at + 3 * e_w]
        assert e_at + 3 * e_w <= 4096
        e_dram = nc.dram_tensor("bias_by_distance", (NG * HEADS, 2 * S), F32, kind="Internal").ap()
        dilated = any(st["kind"] == "dilated" for st in stages)

        class mx:
            at = 0

            @classmethod
            def take(cls, n):
                cls.at += n
                assert cls.at <= arena.shape[1], cls.at
                return arena[:, cls.at - n:cls.at]

        mx.q = mx.take(ATT_H * S).rearrange("p (h s) -> p h s", h=ATT_H)
        mx.k = mx.take(ATT_H * S).rearrange("p (h s) -> p h s", h=ATT_H)
        v_flat = mx.take(2 * D)
        mx.v = v_flat.rearrange("p (t n) -> p t n", t=2)
        mx.dt = [v_flat[0:SSD_H, i * S:(i + 1) * S] for i in range(8)]
        mx.qi = mx.take(4 * S).rearrange("p (h s) -> p h s", h=4)
        mx.ki = mx.take(S)
        mx.small = mx.take(S)
        mx.tok = mx.take(2 * P).rearrange("p (t n) -> p t n", t=2)
        mx.tri = mx.take(2 * S).rearrange("p (t l) -> p t l", t=2)
        mx.causal = mx.take(2 * S).rearrange("p (t k) -> p t k", t=2)
        mx.turn_i = mx.take(P)
        mx.turn = mx.take(ROPE_D)
        mx.col = mx.take(CONV_T * (CONV + 1) + KT + KT + 3)
        mx.convw = mx.col[:, 0:CONV_T * CONV].rearrange("p (c k) -> p c k", c=CONV_T)
        mx.convb = mx.col[:, CONV_T * CONV:CONV_T * (CONV + 1)]
        mx.dskip = mx.col[:, CONV_T * (CONV + 1):CONV_T * (CONV + 1) + KT]
        mx.ygain = mx.col[:, CONV_T * (CONV + 1) + KT:CONV_T * (CONV + 1) + 2 * KT]
        mx.dtb = mx.col[0:SSD_H, CONV_T * (CONV + 1) + 2 * KT:][:, 0:1]
        mx.alog = mx.col[0:SSD_H, CONV_T * (CONV + 1) + 2 * KT:][:, 1:2]
        mx.wi = mx.take(2 * IDX_H).rearrange("p (t h) -> p t h", t=2)
        ssd_at = mx.at
        mx.z = mx.take(KT * S).rearrange("p (c s) -> p c s", c=KT)
        mx.raw = mx.take(CONV_T * (S + CONV - 1)).rearrange("p (c s) -> p c s", c=CONV_T)
        mx.conv = mx.take(CONV_T * S).rearrange("p (c s) -> p c s", c=CONV_T)
        mx.cb = mx.take(SSD_G * 2 * S).rearrange("p (g t l) -> p g t l", g=SSD_G, t=2)
        mx.dec = mx.take(2 * 2 * S).rearrange("p (b t l) -> p b t l", b=2, t=2)
        mx.m = mx.take(2 * 2 * S).rearrange("p (b t l) -> p b t l", b=2, t=2)
        mx.xt = hidden[:, :, :, :, :].rearrange("p a b t s -> p (a b t s)").rearrange("p (t n) -> p t n", t=2)
        mx.y = h
        mx.at = ssd_at + KT * S
        mx.yatt = mx.take(KT * S).rearrange("p (c s) -> p c s", c=KT)
        mx.relu = mx.take(4 * S).rearrange("p (b s) -> p b s", b=4)
        mx.score = mx.take(2 * S).rearrange("p (t s) -> p t s", t=2)
        mx.sel = mx.take(2 * S).rearrange("p (t s) -> p t s", t=2)
        mx.sc = mx.take(2 * S).rearrange("p (b s) -> p b s", b=2)
        mx.pt = mx.take(2 * S).rearrange("p (b s) -> p b s", b=2)
        mx.top8 = mx.take(2 * 8).rearrange("p (t s) -> p t s", t=2)
        mx.stat = mx.take(4 * 2 * ATT_H).rearrange("p (r u) -> p r u", r=4)
        mx.rot = hidden[:, :, :, :, :].rearrange("p a b t s -> p (a b t s)").rearrange("p (b n) -> p b n", b=4)
        mixes = any(st["kind"] == "mix" for st in stages)
        rp_flat = arena[:, da.at:da.at + 7 * S]
        rp_pos = rp_flat[:, 0:S].bitcast(mybir.dt.int32)
        rp_freq = rp_flat[:, S:S + 2]
        rp_f = rp_flat[:, 2 * S - 128:3 * S - 128]
        rp_ang = rp_flat[:, 3 * S:5 * S].rearrange("p (r s) -> p r s", r=2)
        rp_n = rp_flat[:, 5 * S:7 * S].rearrange("p (r s) -> p r s", r=2)

        @block.sync
        def _(sp):
            sp.dma_start(x[:, :, :], A["x"].rearrange("(c p) t -> p c t", p=P)).then_inc(x_loaded, 16)
            sp.dma_start(gains[:, :], A["gains"]).then_inc(const_loaded, 16)
            sp.dma_start(ident[:, :], A["ident"]).then_inc(const_loaded, 16)
            if any(st["kind"] == "s5" for st in stages):
                for dst, name in ((s5.par, "s5_lam"), (s5.b, "s5_b"), (s5.c, "s5_c")):
                    sp.dma_start(dst, A[name].rearrange("p (r c) -> p r c", r=dst.shape[1]) if dst is s5.par
                                 else A[name].rearrange("p (r c m) -> p r c m", r=2, c=S5_G)).then_inc(s5_loaded, 16)
                sp.dma_start(s5.d, A["s5_d"]).then_inc(s5_loaded, 16)
                sp.dma_start(s5.wide, A["s5_wide"]).then_inc(s5_loaded, 16)
            for n in range(SLOTS):
                sp.dma_start(raw[:, n, :], A["panels"][n]).then_inc(panel_loaded[n], 16)
            rounds = (n_panels + 1 - SLOTS) // SLOTS
            with sp.Fori(0, rounds) as i:
                for k in range(SLOTS):
                    sp.wait_ge(lo_ready, i * SLOTS + k + 1)
                    sp.dma_start(raw[:, k, :], A["panels"][bass.ds(i * SLOTS + (SLOTS + k), 1), :, :]
                                 .rearrange("o p n -> p (o n)")).then_inc(panel_loaded[k], 16)
            for n in range(SLOTS * (rounds + 1), n_panels + 1):
                sp.wait_ge(lo_ready, n - SLOTS + 1)
                sp.dma_start(raw[:, n % SLOTS, :], A["panels"][n]).then_inc(panel_loaded[n % SLOTS], 16)
            if final:
                sp.wait_ge(h_ready, 4 * (stages[-1]["norm"] + 1))
                sp.dma_start(out.rearrange("(c p) t -> p c t", p=P), h[:, :, :]).then_inc(stored, 16)
            else:
                sp.wait_ge(x_ready, stages[-1]["xr"] + 4)
                sp.dma_start(out.rearrange("(c p) t -> p c t", p=P), x[:, :, :]).then_inc(stored, 16)
            sp.wait_ge(stored, 16)

        S5_ANGLE, S5_DEN, S5_PREP = 11, 71, 80

        @block.gpsimd
        def _(pool):
            pool.memset(ones[:, :], 1.0).then_inc(const_set, 1)
            pool.memset(eps[:, :], EPS).then_inc(const_set, 1)
            pool.memset(eps_head[:, :], E * EPS).then_inc(const_set, 1)
            if dilated:
                pool.dma_start(da.rel, A["rel_bias"]).then_inc(e_loaded, 16)
                pool.dma_start(da.onehot, A["bucket_onehot"]).then_inc(e_loaded, 16)
                pool.dma_start(da.mask, A["group_mask"]).then_inc(e_loaded, 16)

            def dilated_mixer(st):
                pool.wait_ge(x_ready, st["xr"])
                pool.dma_start(da.pair_ones, A["pair_ones"]).then_inc(e_loaded, 16)
                pool.dma_start(da.gain, A["qk_gain"]).then_inc(e_loaded, 16)
                if mixes:
                    rope_angles()
                pool.wait_ge(e_stored, 16)
                for u in range(n_units):
                    head, qt = u // 2, u % 2
                    if u >= 3:
                        pool.wait_ge(sc_biased, u - 2)
                    src = bass.AP(e_dram.tensor, head * 2 * S + qt, [[2, P], [HEADS * 2 * S, NG], [1, S]])
                    pool.dma_start(da.bias[:, u % 3], src).then_inc(bias_loaded[u % 3], 16)
                if mixes:
                    rope_cosines()

            n_prep = 0

            def then(*ins):
                nonlocal n_prep
                for q in ins:
                    q.then_inc(s5_prep, 1)
                    n_prep += 1
                pool.wait_ge(s5_prep, n_prep)

            def s5_prepare():
                tt, ts = pool.tensor_tensor, pool.tensor_scalar
                lre, lim = s5.par[:, 0], s5.par[:, 1]
                dt, are, ang, turns, mag, sn, sh, t0, t1, t2, t3, nre, nim = s5.t[:13]
                pool.wait_ge(s5_loaded, 5 * 16)
                pool.wait_ge(s5_dt_ready, 1)
                then(tt(are, lre, dt, ALU.mult), tt(ang, lim, dt, ALU.mult))
                then(ts(turns, ang, 1 / TWO_PI, ROUND, ALU.mult, ALU.add))
                then(ts(turns, turns, ROUND, None, ALU.subtract))
                for part in (TWO_PI_1, TWO_PI_2, TWO_PI_3):
                    then(ts(t0, turns, part, None, ALU.mult))
                    then(tt(ang, ang, t0, ALU.subtract))
                then(ts(ang, ang, PI_BELOW, -PI_BELOW, ALU.min, ALU.max))
                assert n_prep == S5_ANGLE
                pool.wait_ge(s5_trig_ready, 3)
                p = s5.pow
                then(tt(t0, sh, sh, ALU.mult))
                then(ts(t0, t0, -2.0, 1.0, ALU.mult, ALU.add))
                then(tt(p[:, 0, 1], mag, t0, ALU.mult), tt(p[:, 1, 1], mag, sn, ALU.mult),
                     pool.memset(p[:, 0, 0], 1.0), pool.memset(p[:, 1, 0], 0.0))
                for k in range(2, S5_T + 1):
                    then(tt(t0, p[:, 0, k - 1], p[:, 0, 1], ALU.mult), tt(t1, p[:, 1, k - 1], p[:, 1, 1], ALU.mult),
                         tt(t2, p[:, 0, k - 1], p[:, 1, 1], ALU.mult), tt(t3, p[:, 1, k - 1], p[:, 0, 1], ALU.mult))
                    then(tt(p[:, 0, k], t0, t1, ALU.subtract), tt(p[:, 1, k], t2, t3, ALU.add))
                then(ts(s5.rot[:, 0], p[:, 1, S5_T], -1.0, None, ALU.mult), ts(s5.rot[:, 1], p[:, 1, S5_T], 1.0, None, ALU.mult))
                then(ts(nre, p[:, 0, 1], -1.0, None, ALU.add))
                nim = p[:, 1, 1]
                then(tt(t0, nre, lre, ALU.mult), tt(t1, nim, lim, ALU.mult),
                     tt(t2, nim, lre, ALU.mult), tt(t3, nre, lim, ALU.mult))
                then(tt(mag, t0, t1, ALU.add), tt(sn, t2, t3, ALU.subtract),
                     tt(are, lre, lre, ALU.mult), tt(ang, lim, lim, ALU.mult))
                then(tt(are, are, ang, ALU.add))
                pool.wait_ge(s5_trig_ready, 4)
                then(tt(mag, mag, are, ALU.mult), tt(sn, sn, are, ALU.mult))
                full = [P, S5_G, S5_P]
                cre, cim = mag.unsqueeze(2).to_broadcast(full), sn.unsqueeze(2).to_broadcast(full)
                b, tb = s5.b, tmp_flat.rearrange("p (r c m) -> p r c m", r=2, c=S5_G)
                td = win_flat[:, 1024:2048].rearrange("p (c m) -> p c m", c=S5_G)
                then(tt(tb[:, 0], cre, b[:, 0], ALU.mult), tt(tb[:, 1], cim, b[:, 0], ALU.mult),
                     tt(td, cim, b[:, 1], ALU.mult))
                then(tt(b[:, 0], tb[:, 0], td, ALU.subtract))
                then(tt(td, cre, b[:, 1], ALU.mult))
                then(tt(b[:, 1], tb[:, 1], td, ALU.add), ts(s5.c[:, 1], s5.c[:, 1], -1.0, None, ALU.mult))
                assert n_prep == S5_PREP, n_prep

            def rope_angles():
                n = 0

                def then(*ins):
                    nonlocal n
                    for q in ins:
                        q.then_inc(rope_step, 1)
                        n += 1
                    pool.wait_ge(rope_step, n)

                pool.dma_start(rp_pos, A["positions"]).then_inc(pos_loaded, 16)
                pool.dma_start(rp_freq, A["rope_freq"]).then_inc(pos_loaded, 16)
                pool.wait_ge(pos_loaded, 32)
                tt, ts = pool.tensor_tensor, pool.tensor_scalar
                then(pool.tensor_copy(rp_f, rp_pos))
                then(*[ts(rp_ang[:, r], rp_f, rp_freq[:, r:r + 1], None, ALU.mult) for r in range(2)])
                then(ts(rp_n, rp_ang, 1 / TWO_PI, ROUND, ALU.mult, ALU.add))
                then(ts(rp_n, rp_n, ROUND, None, ALU.subtract))
                for part in (TWO_PI_1, TWO_PI_2, TWO_PI_3):
                    then(ts(rope[:, 0:2], rp_n, part, None, ALU.mult))
                    then(tt(rp_ang, rp_ang, rope[:, 0:2], ALU.subtract))
                ts(rp_ang, rp_ang, PI_BELOW, -PI_BELOW, ALU.min, ALU.max).then_inc(rope_angle, 1)

            def rope_cosines():
                pool.wait_ge(rope_sin, 4)
                pool.tensor_tensor(rp_n, rp_ang, rp_ang, ALU.mult).then_inc(rope_squared, 1)
                pool.wait_ge(rope_squared, 1)
                pool.tensor_scalar(rope[:, 0:3:2], rp_n, -2.0, 1.0, ALU.mult, ALU.add).then_inc(rope_ready, 1)

            def mix_loads(st):
                pool.wait_ge(x_ready, st["xr"])
                i = st["i"]
                pool.dma_start(mx.col, A["mix_col"][i]).then_inc(mix_loaded, 16)
                pool.dma_start(mx.tri, A["mask_tri"]).then_inc(mix_loaded, 16)
                pool.dma_start(mx.causal, A["mask_causal"]).then_inc(mix_loaded, 16)
                pool.dma_start(mx.turn_i, A["turn_i"]).then_inc(mix_loaded, 16)
                pool.dma_start(mx.turn[0:ROPE_D, :], A["turn"]).then_inc(mix_loaded, 16)
                pool.memset(mx.small, 0.0).then_inc(small_set, 1)
                pool.memset(mx.raw[:, :, 0:CONV - 1], 0.0).then_inc(pad_set, 1)

            def s5_mixer(st):
                def spread_c(f):
                    if f >= 2:
                        pool.wait_ge(s5_k_ready, f - 1)
                    for r in range(2):
                        for e in range(2):
                            half = slice(e * S5_N, (e + 1) * S5_N)
                            pool.tensor_copy(s5.cbd[half, f % 2, r, :, e * S5_P:(e + 1) * S5_P],
                                             s5.c[half, r, f * NC:(f + 1) * NC, :]).then_inc(s5_cbd_ready, 1)
                    pool.wait_ge(s5_cbd_ready, 1 + 4 * (f + 1))

                pool.memset(s5.cbd, 0.0).then_inc(s5_cbd_ready, 1)
                pool.wait_ge(s5_cbd_ready, 1)
                spread_c(0)
                spread_c(1)
                pool.wait_ge(s5_hperm_ready, KT)
                s5_store_u(pool, range(KT // 2), s5_u_stored["pool"])
                for q in s5_u_stored.values():
                    pool.wait_ge(q, 16 * KT // 2)
                pool.dma_start(s5.u.rearrange("p g c -> p (g c)"), u_dram.rearrange("r m f g c -> (r m) (f g c)")
                               ).then_inc(s5_u_loaded, 16)
                for f in range(2, KT):
                    spread_c(f)
                pool.wait_ge(s5_intra_ready, KT)
                pool.memset(s5.zbd, 0.0).then_inc(s5_zbd_set, 1)
                for n, f in enumerate(W_POOL):
                    if f >= 4:
                        pool.wait_ge(s5_out_ready, f - 3)
                    for d in range(2):
                        tab = [s5_table(r, 1, d, f) for r in range(2)]
                        cc = [s5_over_rows(s5.c[:, r], d, f) for r in range(2)]
                        w, tmp = s5.w[f % 4], s5.wtmp.rearrange("p r c (k m) -> p r c k m", k=S5_T)
                        w_re, w_im = s5_part(w[:, 0], d), s5_part(w[:, 1], d)
                        pool.tensor_tensor(w_re, tab[0], cc[0], ALU.mult)
                        pool.tensor_tensor(w_im, tab[0], cc[1], ALU.mult)
                        pool.tensor_tensor(tmp[:, 0], tab[1], cc[1], ALU.mult)
                        pool.tensor_tensor(tmp[:, 1], tab[1], cc[0], ALU.mult).then_inc(s5_wp_part, 1)
                        pool.wait_ge(s5_wp_part, 3 * n + 2 * d + 1)
                        pool.tensor_tensor(w_re, w_re, tmp[:, 0], ALU.add)
                        ins = pool.tensor_tensor(w_im, w_im, tmp[:, 1], ALU.subtract)
                        ins.then_inc(s5_wp_part if d == 0 else s5_wp_ready, 1)
                        if d == 0:
                            pool.wait_ge(s5_wp_part, 3 * n + 2)
                    pool.wait_ge(s5_wp_ready, n + 1)
                pool.wait_ge(s5_y_ready, KT)
                s5_store_y(pool, 1, range(S5_T // 2), s5_y_stored["pool1"])

            if any(st["kind"] == "s5" for st in stages):
                s5_prepare()
            if dilated:
                pool.wait_ge(e_masked, 1)
                pool.dma_start(e_dram, da.e).then_inc(e_stored, 16)
            for st in stages:
                if st["kind"] == "s5":
                    s5_mixer(st)
                if st["kind"] == "dilated":
                    dilated_mixer(st)
                if st["kind"] == "mix":
                    mix_loads(st)
                if st["kind"] == "fourier":
                    if st["xr"]:
                        pool.wait_ge(x_ready, st["xr"])
                    pool.dma_start(dft_ch, A["dft_ch"]).then_inc(dft_loaded, 16)
                    pool.dma_start(dft_sq, A["dft_sq"].rearrange("(t p) (f s) -> p t f s", p=P, f=2)
                                   ).then_inc(dft_loaded, 16)

        @block.scalar
        def _(a):
            def split(n, i=None, per=0):
                def at(v, m=1):
                    return v if i is None else i * (m * per) + v
                if i is None and n > n_panels:
                    return
                s = n % SLOTS
                a.wait_ge(panel_loaded[s], 16 * (n // SLOTS + 1) if i is None
                          else i * (16 * per // SLOTS) + 16 * (n // SLOTS + 1))
                if n >= SLOTS:
                    a.wait_ge(panel_done, at(n - SLOTS + 1))
                a.activation(w_hi[:, s, :], raw[:, s, :], ACT.Copy).then_inc(hi_ready, 1)

            def norm(st):
                n = st["norm"]
                a.wait_ge(x_loaded, 16)
                for b in range(4):
                    if st["xr"]:
                        a.wait_ge(x_ready, st["xr"] - 3 + b)
                    a.activation(h[:, 2 * b:2 * b + 2, :], x[:, 2 * b:2 * b + 2, :],
                                 ACT.Square).then_inc(sq_ready, 1)
                a.wait_ge(const_set, 3)
                a.activation(warm[:, :], eps[:, :], ACT.Sqrt)
                a.wait_ge(ss_ready, n + 1)
                a.activation(rstd[:, :], bank[4][:, 0:S], ACT.Sqrt, bias=eps[:, 0:1],
                             scale=1.0 / D).then_inc(rms_ready, 1)
                if st["split"]:
                    for b in range(4):
                        a.wait_ge(h_ready, 4 * n + b + 1)
                        a.activation(h_hi[:, 2 * b:2 * b + 2, :], h[:, 2 * b:2 * b + 2, :],
                                     ACT.Copy).then_inc(h_hi_ready, 1)

            def ffn(st):
                n0, f = st["n0"], st["ffn"]

                def silu(c, p, i=None):
                    def at(v, per):
                        return v if i is None else i * per + v
                    a.wait_ge(panel_done, at(p + 1, 6))
                    a.activation(gate[:, c % 2], bank[(2 * c) % PROJ_BANKS][:, :].rearrange(
                        "p (t s) -> p t s", t=2), ACT.Silu).then_inc(gate_ready, 1)

                split(n0 + 2)
                split(n0 + 3)
                silu(0, n0)
                with a.Fori(0, (FFC - 1) // 2) as i:
                    for c in (1, 2):
                        p = hidden_panel(n0, c)
                        split(p + 2, i, 6)
                        split(p + 3, i, 6)
                        silu(c, p, i)
                        split(p + 4, i, 6)
                split(n0 + 34)

            def fourier(st):
                f = st["fourier"] = sum(q["kind"] == "fourier" for q in stages[:stages.index(st)])
                for g in range(KT):
                    k = f * KT + g
                    a.wait_ge(dft_tok_ready, k + 1)
                    a.activation(dft_tok[:, g % 2], bank[4 + g % 2][:, :].rearrange("p (t n) -> p t n", t=2),
                                 ACT.Copy).then_inc(dft_tok_copied, 1)
                    if g:
                        a.wait_ge(dft_ready, k)
                        a.activation(h_hi[:, g - 1], bank[6 + (g - 1) % 2][:, 0:S], ACT.Copy).then_inc(dft_hi_ready, 1)
                a.wait_ge(dft_ready, f * KT + KT)
                a.activation(h_hi[:, KT - 1], bank[6 + (KT - 1) % 2][:, 0:S], ACT.Copy).then_inc(dft_hi_ready, 1)
                for p in range(4):
                    split(st["n0"] + p + 2)

            def s5_prepare():
                dt, are, ang, turns, mag, sn, sh = s5.t[:7]
                a.wait_ge(s5_loaded, 5 * 16)
                a.activation(dt, s5.par[:, 2], ACT.Exp).then_inc(s5_dt_ready, 1)
                a.wait_ge(s5_prep, S5_ANGLE)
                a.activation(mag, are, ACT.Exp).then_inc(s5_trig_ready, 1)
                a.activation(sn, ang, ACT.Sin).then_inc(s5_trig_ready, 1)
                a.activation(sh, ang, ACT.Sin, scale=0.5).then_inc(s5_trig_ready, 1)

            def s5_mixer(st):
                hn = st["hn"]
                a.wait_ge(h_ready, 4 * (hn + 1))
                for f in range(KT):
                    a.activation(s5.hperm[:, f], h[:, f, :].rearrange("p (c r) -> p r c", r=S5_T)[:, ::-1, :],
                                 ACT.Copy).then_inc(s5_hperm_ready, 1)
                a.wait_ge(s5_hperm_ready, KT)
                s5_store_u(a, range(KT // 2, KT), s5_u_stored["act"])

                def factors(f):
                    for q in range(4):
                        a.wait_ge(s5_vt_ready, 4 * f + q + 1)
                        if f and q == 0:
                            a.wait_ge(s5_in_ready, f)
                        a.activation(s5.win[:, 4 * q:4 * q + 4, :], bank[4 + q % 2][:, :].rearrange(
                            "p (m q) -> p m q", m=4), ACT.Copy).then_inc(s5_win_ready, 1)
                    a.wait_ge(s5_k_ready, f + 1)
                    a.activation(s5.kc, bank[0][:, 0:2 * P], ACT.Copy).then_inc(s5_k_copied, 1)

                factors(0)
                for f in range(KT):
                    a.wait_ge(s5_in_ready, f + 1)
                    a.activation(s5.z[:, :, f * NC:(f + 1) * NC, :], bank[2 + f % 2][:, :].rearrange(
                        "p (r c k) -> p r c k", r=2, c=NC), ACT.Copy).then_inc(s5_in_copied, 1)
                    a.wait_ge(s5_t_ready, f + 1)
                    for q in range(2):
                        a.activation(s5.tc[:, :, 4 * q:4 * q + 4, :].rearrange("p g i m -> p i g m"), bank[7 - q][:, :].rearrange(
                            "p (i g m) -> p i g m", i=4, g=KT), ACT.Copy).then_inc(s5_t_copied, 1)
                    if f + 1 < KT:
                        factors(f + 1)
                    a.wait_ge(s5_intra_ready, f + 1)
                    a.activation(s5.y[:, f * KT:(f + 1) * KT, :], bank[1][:, 0:S].rearrange(
                        "p (g c) -> p g c", g=KT), ACT.Copy).then_inc(s5_intra_copied, 1)
                a.wait_ge(s5_zbd_set, 1)
                a.wait_ge(s5_step, 4 * (S5_C - 2))
                for f in range(KT):
                    if f >= 2:
                        a.wait_ge(s5_out_ready, f - 1)
                    for d in range(2):
                        for e in range(2):
                            half = slice(e * S5_N, (e + 1) * S5_N)
                            z = s5.z[half, :, f * NC + 4 * d:f * NC + 4 * d + 4, :]
                            at = e * S5_C + 1 - d
                            a.activation(s5.zbd[half, f % 2, :, 4 * d:4 * d + 4, at:at + S5_C - 1],
                                         z[:, :, :, 0:S5_C - 1] if d == 0 else z[:, :, :, S5_C - 2::-1],
                                         ACT.Copy).then_inc(s5_zbd_ready, 1)
                    if f == KT - 2:
                        a.wait_ge(s5_y_ready, KT // 2)
                        s5_store_y(a, 0, range(S5_T), s5_y_stored["act0"])
                a.wait_ge(s5_y_stored["act0"], 16 * S5_T)
                s5_load_y(a, 0)
                a.wait_ge(s5_y_ready, KT)
                s5_store_y(a, 1, range(S5_T // 2, S5_T), s5_y_stored["act1"])
                for q in ("act1", "pool1"):
                    a.wait_ge(s5_y_stored[q], 16 * S5_T // 2)
                s5_load_y(a, 1)
                for f in range(KT):
                    a.wait_ge(s5_skip_ready, f + 1)
                    a.activation(h[:, f], h[:, f], ACT.Gelu_apprx_tanh).then_inc(s5_gelu_ready, 1)
                    if f % 2:
                        a.wait_ge(s5_gelu_ready, f + 1)
                        a.activation(h_hi[:, f - 1:f + 1, :], h[:, f - 1:f + 1, :], ACT.Copy).then_inc(s5_g_hi_ready, 1)
                for k in range(4):
                    split(st["n0"] + 2 * k + 2)
                    split(st["n0"] + 2 * k + 3)
                    a.wait_ge(panel_done, st["n0"] + 2 * k + 2)
                    if k >= 2:
                        a.wait_ge(glu_mul_ready, k - 1)
                    a.activation(gate[:, k % 2], bank[(2 * k + 1) % PROJ_BANKS][:, :].rearrange("p (t s) -> p t s", t=2),
                                 ACT.Sigmoid).then_inc(glu_sig_ready, 1)

            def dilated_mixer(st):
                n0 = st["n0"]

                def evacuate(p):
                    hb, i, c = da_panel(p)
                    b = bank[p % 3]
                    a.wait_ge(panel_done, n0 + p + 1)
                    if i < QK:
                        if c >= 2:
                            a.wait_ge(qk_ss_ready, c - 1)
                        a.activation(da.sq[:, c % 2], b[:, :], ACT.Square).then_inc(qk_sq_ready, 1)
                        if hb >= 2:
                            a.wait_ge(sc_ready, UNITS * (hb - 1))
                        g, which = i // 2, i % 2
                        a.activation(da.qk[:, hb % 2, which, g], b[:, :].rearrange("p (m n) -> p m n", m=2), ACT.Copy,
                                     scale=da.gain[:, which * NG + g:which * NG + g + 1]).then_inc(qk_copied, 1)
                    else:
                        if hb >= 2:
                            a.wait_ge(o_ready, UNITS * (hb - 1))
                        a.activation(da.v[:, hb % 2, i - QK], b[:, :].rearrange("p (m n) -> p m n", m=2),
                                     ACT.Copy).then_inc(v_copied, 1)
                    if i % 2 == 0 and 2 <= i <= QK:
                        c, g = hb * QK + i - 2, i // 2 - 1
                        a.wait_ge(qk_ss_ready, c + 2)
                        if hb >= 2:
                            a.wait_ge(sc_biased, UNITS * (hb - 1))
                        a.activation(da.rq[:, hb % 2, g].rearrange("p m t e -> p (m t e)"), bank[3][:, 0:UNITS], ACT.Sqrt,
                                     bias=eps_head[:, 0:1]).then_inc(qk_rms_ready, 1)
                        if c >= 4:
                            a.wait_ge(qk_ready, c - 2)
                        a.activation(da.rs[:, c // 2 % 2], bank[5][:, :], ACT.Sqrt, bias=eps[:, 0:1],
                                     scale=1.0 / E).then_inc(qk_rms_ready, 1)

                def exp(u):
                    a.wait_ge(neg_ready, u + 1)
                    a.activation(da.sc[:, u % 3], da.sc[:, u % 3], ACT.Exp, bias=da.stat[:, 1, u:u + 1],
                                 accum_out=da.stat[:, 2, u:u + 1]).then_inc(p_ready, 1)

                def copy_p(u):
                    a.wait_ge(pt_ready, u + 1)
                    if u >= 2:
                        a.wait_ge(o_ready, u - 1)
                    a.activation(da.pt[:, u % 2], bank[6][:, :], ACT.Copy).then_inc(pt_copied, 1)

                def copy_o(u):
                    head, qt = u // 2, u % 2
                    rows = slice(head % 2 * E, head % 2 * E + E)
                    a.wait_ge(o_ready, u + 1)
                    a.activation(h[rows, head // 2, qt::2], bank[7][rows, 0:P], ACT.Copy).then_inc(o_copied, 1)

                def upper(b):
                    a.wait_ge(o_copied, UNITS * (b + 1))
                    a.activation(h_hi[:, 2 * b:2 * b + 2, :], h[:, 2 * b:2 * b + 2, :], ACT.Copy).then_inc(o_hi_ready, 1)

                a.wait_ge(e_loaded, 16 * 5)
                for p in range(PANELS):
                    split(n0 + p + 2)
                    evacuate(p)
                last = n_units - UNITS
                for u in range(last):
                    panels = da_panels(u)
                    if u:
                        copy_p(u - 1)
                    split(n0 + panels[0] + 2)
                    exp(u)
                    if u:
                        copy_o(u - 1)
                    evacuate(panels[0])
                    for p in panels[1:]:
                        split(n0 + p + 2)
                        evacuate(p)
                copy_p(last - 1)
                split(n0 + 38)
                exp(last)
                copy_o(last - 1)
                for b in range(BLOCKS - 1):
                    upper(b)
                for u in range(last + 1, n_units + 2):
                    if u < n_units:
                        exp(u)
                    if u - 1 < n_units:
                        copy_p(u - 1)
                    if u - 2 >= last:
                        copy_o(u - 2)
                upper(BLOCKS - 1)
                if mixes:
                    rope_sines()
                for p in range(37, 40):
                    split(n0 + p + 2)

            def rope_sines():
                a.wait_ge(rope_angle, 1)
                for r in range(2):
                    a.activation(rope[:, 2 * r + 1], rp_ang[:, r], ACT.Sin).then_inc(rope_sin, 1)
                a.wait_ge(rope_sin, 2)
                for r in range(2):
                    a.activation(rp_ang[:, r], rp_ang[:, r], ACT.Sin, scale=0.5).then_inc(rope_sin, 1)

            def mixer(st):
                i, n0 = st["i"], st["n0"]

                def arrive(p):
                    split(n0 + p + 2)
                    a.wait_ge(panel_done, n0 + p + 1)
                    return bank[p % PROJ_BANKS]

                def halves(b):
                    return b[:, :].rearrange("p (m s) -> p m s", m=2)

                def conv_silu(c):
                    a.wait_ge(conv_ready, CONV_T * i + c + 1)
                    a.activation(mx.conv[:, c], mx.conv[:, c], ACT.Silu).then_inc(conv_act, 1)

                a.wait_ge(pad_set, i + 1)
                a.wait_ge(mix_loaded, 80 * (i + 1))
                for p in range(6):
                    a.activation(mx.raw[:, 2 * p:2 * p + 2, CONV - 1:], halves(arrive(p)), ACT.Copy).then_inc(mix_copied, 1)
                    if p:
                        conv_silu(2 * p - 2)
                        conv_silu(2 * p - 1)
                b = arrive(6)
                a.wait_ge(small_set, i + 1)
                a.activation(mx.ki, b[:, 0:S], ACT.Copy)
                a.activation(mx.small[32:32 + IDX_H, :], b[32:32 + IDX_H, S:2 * S], ACT.Copy)
                a.activation(mx.dt[0], b[0:SSD_H, S:2 * S], ACT.Copy).then_inc(mix_copied, 1)
                conv_silu(10)
                conv_silu(11)
                for p in range(7, 11):
                    a.activation(mx.z[:, 2 * (p - 7):2 * (p - 7) + 2, :], halves(arrive(p)), ACT.Silu).then_inc(mix_copied, 1)
                a.wait_ge(dt_arg_ready, i + 1)
                a.activation(mx.dt[2], mx.dt[1], ACT.Exp).then_inc(dt_exp_ready, 1)
                a.activation(mx.alog, mx.alog, ACT.Exp).then_inc(a_ready, 1)
                for q in range(4):
                    a.wait_ge(xt_ready, 4 * i + q + 1)
                    a.activation(mx.xt[:, :, q * 2 * P:(q + 1) * 2 * P], bank[5 + q % 2][:, :].rearrange(
                        "p (t n) -> p t n", t=2), ACT.Copy).then_inc(xt_copied, 1)
                a.wait_ge(tok_ready, i + 1)
                a.activation(mx.tok, bank[4][:, 0:2 * P].rearrange("p (t n) -> p t n", t=2), ACT.Copy).then_inc(tok_copied, 1)
                for g in range(SSD_G):
                    a.wait_ge(cb_ready, 2 * i + g + 1)
                    b = bank[7 if g == 0 else 4]
                    a.activation(mx.cb[:, g, 0], b[:, 0:S], ACT.Copy)
                    a.activation(mx.cb[:, g, 1, P:], b[:, S + P:2 * S], ACT.Copy).then_inc(cb_copied, 1)
                for j in range(SSD_H // 2):
                    for e in range(2):
                        n = SSD_H * i + 2 * j + e
                        a.wait_ge(decay_arg, n + 1)
                        d = mx.dec[:, e]
                        a.activation(d[:, 0], d[:, 0], ACT.Exp)
                        a.activation(d[:, 1, P:], d[:, 1, P:], ACT.Exp).then_inc(decay_ready, 1)
                    p = 11 + j
                    dst = mx.qi[:, 2 * j:2 * j + 2, :] if j < 2 else mx.q[:, 2 * j - 4:2 * j - 2, :] if j < 6 else \
                        mx.k[:, 2 * j - 12:2 * j - 10, :]
                    a.activation(dst, halves(arrive(p)), ACT.Copy).then_inc(mix_copied, 1)
                for p in range(19, 21):
                    a.activation(mx.k[:, 2 * (p - 17):2 * (p - 17) + 2, :], halves(arrive(p)), ACT.Copy).then_inc(mix_copied, 1)
                for p in range(21, 25):
                    if p == 21:
                        a.wait_ge(decay_used, SSD_H * (i + 1))
                    a.activation(mx.v[:, :, (p - 21) * COLS:(p - 20) * COLS], halves(arrive(p)), ACT.Copy).then_inc(mix_copied, 1)
                for g in range(SSD_G):
                    a.wait_ge(y_gated, 8 * i + 4 * g + 4)
                    a.activation(mx.z[:, 4 * g:4 * g + 4], mx.y[:, 4 * g:4 * g + 4], ACT.Square).then_inc(ysq_ready, 1)
                for g in range(SSD_G):
                    a.wait_ge(yss_ready, 2 * i + g + 1)
                    a.activation(mx.dec[:, g, 0], bank[4 + g][:, 0:S], ACT.Sqrt, bias=eps[:, 0:1],
                                 scale=SSD_G / D).then_inc(yrms_ready, 1)
                for b in range(4):
                    a.wait_ge(y_normed, 4 * i + b + 1)
                    a.activation(h_hi[:, 2 * b:2 * b + 2, :], mx.y[:, 2 * b:2 * b + 2, :], ACT.Copy).then_inc(y_hi_ready, 1)
                for p in range(25, 29):
                    split(n0 + p + 2)
                for u in range(2 * IDX_H):
                    qt = u // IDX_H
                    keys = (qt + 1) * P
                    n = 2 * IDX_H * i + u
                    a.wait_ge(idx_ready, n + 1)
                    if u >= 4:
                        a.wait_ge(idx_added, n - 3)
                    a.activation(mx.relu[:, u % 4, 0:keys], bank[4 + u % 4][:, 0:keys], ACT.Relu,
                                 scale=E ** -0.5).then_inc(relu_ready, 1)

                def copy_p(u):
                    n, keys = 2 * ATT_H * i + u, (u % 2 + 1) * P
                    a.wait_ge(att_pt_ready, n + 1)
                    if u >= 2:
                        a.wait_ge(att_o_ready, n - 1)
                    a.activation(mx.pt[:, u % 2, 0:keys], bank[6][:, 0:keys], ACT.Copy).then_inc(att_pt_copied, 1)

                def copy_o(u):
                    head, qt = u // 2, u % 2
                    a.wait_ge(att_o_ready, 2 * ATT_H * i + u + 1)
                    a.activation(mx.yatt[:, head, qt * P:(qt + 1) * P], bank[7][:, u % 2 * P:(u % 2 + 1) * P],
                                 ACT.Copy).then_inc(att_o_copied, 1)

                units = 2 * ATT_H
                for u in range(units):
                    keys = (u % 2 + 1) * P
                    a.wait_ge(att_neg, units * i + u + 1)
                    a.activation(mx.sc[:, u % 2, 0:keys], mx.sc[:, u % 2, 0:keys], ACT.Exp, bias=mx.stat[:, 1, u:u + 1],
                                 accum_out=mx.stat[:, 2, u:u + 1]).then_inc(att_p_ready, 1)
                    if u:
                        copy_p(u - 1)
                    if u > 1:
                        copy_o(u - 2)
                copy_p(units - 1)
                copy_o(units - 2)
                copy_o(units - 1)
                a.wait_ge(att_o_copied, units * (i + 1))
                a.wait_ge(panel_done, n0 + 29)
                for b in range(4):
                    a.activation(h_hi[:, 2 * b:2 * b + 2, :], mx.yatt[:, 2 * b:2 * b + 2, :], ACT.Copy).then_inc(att_hi_ready, 1)
                for p in range(29, 33):
                    split(n0 + p + 2)

            split(0)
            split(1)
            if any(st["kind"] == "s5" for st in stages):
                s5_prepare()
            todo = {"norm": norm, "final": norm, "ffn": ffn, "fourier": fourier, "s5": s5_mixer,
                    "dilated": dilated_mixer, "mix": mixer}
            for st in stages:
                todo[st["kind"]](st)

        @block.vector
        def _(v):
            def split(n, i=None, per=0):
                if i is None and n > n_panels:
                    return
                v.wait_ge(hi_ready, n + 1 if i is None else i * per + n + 1)
                s = n % SLOTS
                v.tensor_tensor(w_lo[:, s, :], raw[:, s, :], w_hi[:, s, :].bitcast(F32),
                                ALU.subtract).then_inc(lo_ready, 1)

            def norm(st):
                n = st["norm"]
                v.wait_ge(const_loaded, 32)
                v.wait_ge(rms_ready, n + 1)
                v.reciprocal(rstd[:, :], rstd[:, :]).then_inc(rstd_ready, 1)
                v.wait_ge(rstd_ready, n + 1)
                for b in range(5):
                    if b < 4:
                        for c in (2 * b, 2 * b + 1):
                            ins = v.scalar_tensor_tensor(h[:, c, :], x[:, c, :], gains[:, n * KT + c:n * KT + c + 1],
                                                         rstd[:, :], ALU.mult, ALU.mult)
                        ins.then_inc(h_ready, 1)
                    if b and st["split"]:
                        v.wait_ge(h_hi_ready, 4 * st["hs"] + b)
                        v.tensor_tensor(h_lo[:, 2 * b - 2:2 * b, :], h[:, 2 * b - 2:2 * b, :],
                                        h_hi[:, 2 * b - 2:2 * b, :].bitcast(F32),
                                        ALU.subtract).then_inc(h_lo_ready, 1)

            def ffn(st):
                n0, f = st["n0"], st["ffn"]
                scale = 1.0 if st["i"] < BLOCK1 else 0.5

                def hidden(c, p, i=None):
                    def at(val, per):
                        return val if i is None else i * per + val
                    b = c % 2
                    v.wait_ge(panel_done, at(p + 2, 6))
                    v.wait_ge(gate_ready, at(f * FFC + c + 1, 2))
                    v.tensor_tensor(act[:, b], gate[:, b], bank[(2 * c + 1) % PROJ_BANKS][:, :].rearrange(
                        "p (t s) -> p t s", t=2), ALU.mult).then_inc(act_ready, 1)
                    v.wait_ge(act_ready, at(f * FFC + c + 1, 2))
                    v.tensor_copy(act_hi[:, b], act[:, b]).then_inc(act_hi_ready, 1)
                    v.wait_ge(act_hi_ready, at(f * FFC + c + 1, 2))
                    v.tensor_tensor(act_lo[:, b], act[:, b], act_hi[:, b].bitcast(F32),
                                    ALU.subtract).then_inc(act_lo_ready, 1)

                split(n0 + 2)
                if st["s5_follows"]:
                    s5_first()
                split(n0 + 3)
                hidden(0, n0)
                with v.Fori(0, (FFC - 1) // 2) as i:
                    for c in (1, 2):
                        p = hidden_panel(n0, c)
                        split(p + 2, i, 6)
                        split(p + 3, i, 6)
                        hidden(c, p, i)
                        split(p + 4, i, 6)
                for b in range(4):
                    if b < 3:
                        v.wait_ge(sums_ready, 3 * f + b + 1)
                    else:
                        v.wait_ge(panel_done, n0 + 33)
                    v.scalar_tensor_tensor(x[:, 2 * b:2 * b + 2, :], bank[4 + b][:, :].rearrange(
                        "p (t s) -> p t s", t=2), scale, x[:, 2 * b:2 * b + 2, :],
                        ALU.mult, ALU.add).then_inc(x_ready, 1)
                split(n0 + 34)

            def add_panel(st, k, first=0):
                v.wait_ge(panel_done, st["n0"] + first + k + 1)
                v.tensor_tensor(x[:, 2 * k:2 * k + 2, :], bank[k % PROJ_BANKS][:, :].rearrange(
                    "p (t s) -> p t s", t=2), x[:, 2 * k:2 * k + 2, :], ALU.add).then_inc(x_ready, 1)

            def fourier(st):
                f = st["fourier"]
                for g in range(KT):
                    k = f * KT + g
                    v.wait_ge(dft_hi_ready, k + 1)
                    v.tensor_tensor(h_lo[:, g], bank[6 + g % 2][:, 0:S], h_hi[:, g].bitcast(F32),
                                    ALU.subtract).then_inc(dft_lo_ready, 1)
                for p in range(4):
                    split(st["n0"] + p + 2)
                    add_panel(st, p)

            def s5_prepare():
                are = s5.t[1]
                v.wait_ge(s5_prep, S5_DEN)
                v.reciprocal(are, are).then_inc(s5_trig_ready, 1)

            def s5_product(out_, m, k, f, ahead, sem_part, sem_done, n):
                for d in range(2):
                    tab = [s5_table(r, ahead, d, f) for r in range(2)]
                    mm = [s5_over_rows(m[:, r], d, f) for r in range(2)]
                    re, im = s5_part(out_[:, 0], d), s5_part(out_[:, 1], d)
                    tmp = s5.tmp.rearrange("p r c (k m) -> p r c k m", k=S5_T)
                    v.tensor_tensor(re, tab[0], mm[0], ALU.mult)
                    v.tensor_tensor(im, tab[0], mm[1], ALU.mult)
                    v.tensor_tensor(tmp[:, 0], tab[1], mm[1], ALU.mult)
                    v.tensor_tensor(tmp[:, 1], tab[1], mm[0], ALU.mult).then_inc(sem_part, 1)
                    v.wait_ge(sem_part, 3 * n + 2 * d + 1)
                    v.tensor_tensor(re, re, tmp[:, 0], ALU.subtract if k > 0 else ALU.add)
                    ins = v.tensor_tensor(im, im, tmp[:, 1], ALU.add if k > 0 else ALU.subtract)
                    ins.then_inc(sem_part if d == 0 else sem_done, 1)
                    if d == 0:
                        v.wait_ge(sem_part, 3 * n + 2)

            def s5_first():
                v.wait_ge(s5_prep, S5_PREP)
                s5_product(s5.buf[0], s5.b, 1, 0, 0, s5_v_part, s5_v_ready, 0)

            def s5_mixer(st):
                for f in range(1, KT):
                    if f >= 2:
                        v.wait_ge(s5_k_ready, f - 1)
                    v.wait_ge(s5_v_ready, f)
                    s5_product(s5.buf[f % 2], s5.b, 1, f, 0, s5_v_part, s5_v_ready, f)
                v.wait_ge(s5_in_copied, KT)
                n = 0
                pair = [P, 2, S5_G]
                l8 = s5.pow[:, 0, S5_T].unsqueeze(1).to_broadcast(pair)
                m1, m2 = (tmp_flat[:, i * 2 * S5_G:(i + 1) * 2 * S5_G].rearrange("p (r c) -> p r c", r=2) for i in range(2))
                for k in range(1, S5_C - 1):
                    z0, z1 = s5.z[:, :, :, k - 1], s5.z[:, :, :, k]
                    v.tensor_tensor(m1, z0, l8, ALU.mult).then_inc(s5_step, 1)
                    v.tensor_tensor(m2, z0[:, ::-1, :], s5.rot, ALU.mult).then_inc(s5_step, 1)
                    v.wait_ge(s5_step, n + 1)
                    v.tensor_tensor(z1, z1, m1, ALU.add).then_inc(s5_step, 1)
                    v.wait_ge(s5_step, n + 3)
                    v.tensor_tensor(z1, z1, m2, ALU.add).then_inc(s5_step, 1)
                    n += 4
                    v.wait_ge(s5_step, n)

                v.wait_ge(s5_intra_copied, KT)
                w_dve = [f for f in range(KT) if f not in W_POOL]
                added = 0
                for n, f in enumerate(w_dve + [KT]):
                    if f < KT:
                        if f >= 4:
                            v.wait_ge(s5_out_ready, f - 3)
                        if n:
                            v.wait_ge(s5_w_ready, n)
                        s5_product(s5.w[f % 4], s5.c, -1, f, 1, s5_w_part, s5_w_ready, n)
                    while added < (f - 2 if f < KT else KT):
                        v.wait_ge(s5_out_ready, added + 1)
                        yf = s5.y[:, added * KT:(added + 1) * KT, :]
                        v.tensor_tensor(yf, bank[4 + added % 4][:, 0:S].rearrange("p (g c) -> p g c", g=KT), yf,
                                        ALU.add).then_inc(s5_y_ready, 1)
                        added += 1
                for f in range(KT):
                    if f % (KT // 2) == 0:
                        v.wait_ge(s5_y_loaded[f // (KT // 2)], 16)
                    hf = h[:, f, :].rearrange("p (c i) -> p c i", i=S5_T)
                    v.scalar_tensor_tensor(hf, hf, s5.d[:, f:f + 1], s5.yt[:, f].rearrange("p i c -> p c i"),
                                           ALU.mult, ALU.add).then_inc(s5_skip_ready, 1)
                    for b in {3: (0,), 5: (1,), 7: (2, 3)}.get(f, ()):
                        v.wait_ge(s5_g_hi_ready, b + 1)
                        v.tensor_tensor(h_lo[:, 2 * b:2 * b + 2, :], h[:, 2 * b:2 * b + 2, :],
                                        h_hi[:, 2 * b:2 * b + 2, :].bitcast(F32), ALU.subtract).then_inc(s5_g_lo_ready, 1)
                for k in range(4):
                    split(st["n0"] + 2 * k + 2)
                    split(st["n0"] + 2 * k + 3)
                    v.wait_ge(glu_sig_ready, k + 1)
                    v.tensor_tensor(act[:, k % 2], gate[:, k % 2], bank[(2 * k) % PROJ_BANKS][:, :].rearrange(
                        "p (t s) -> p t s", t=2), ALU.mult).then_inc(glu_mul_ready, 1)
                    v.wait_ge(glu_mul_ready, k + 1)
                    xq = x[:, 2 * k:2 * k + 2, :]
                    v.tensor_tensor(xq, act[:, k % 2], xq, ALU.add).then_inc(x_ready, 1)

            def dilated_mixer(st):
                n0 = st["n0"]

                def scale_due(p):
                    hb, i, _ = da_panel(p)
                    if i % 2 == 0 or not 3 <= i <= QK + 1:
                        return
                    g, c = (i - 3) // 2, hb * QK + i - 3
                    rq, rs, k = da.rq[:, hb % 2, g], da.rs[:, c // 2 % 2], da.qk[:, hb % 2, 1, g]
                    v.wait_ge(qk_rms_ready, c + 2)
                    v.reciprocal(rq, rq).then_inc(qk_ready, 1)
                    v.reciprocal(rs, rs).then_inc(qk_rstd_ready, 1)
                    v.wait_ge(qk_rstd_ready, c // 2 + 1)
                    v.wait_ge(qk_copied, c + 2)
                    v.tensor_tensor(k, k, rs.rearrange("p (m n) -> p m n", m=2), ALU.mult).then_inc(qk_ready, 1)

                def bias(u):
                    qt = u % 2
                    v.wait_ge(sc_ready, u + 1)
                    v.wait_ge(bias_loaded[u % 3], 16 * (u // 3 + 1))
                    if u >= 3:
                        v.wait_ge(pt_ready, u - 2)
                    if u % UNITS == 0:
                        v.wait_ge(qk_ready, QK * (u // UNITS + 1))
                    hb, m, e = u // UNITS, u // 4 % 2, u // 2 % 2
                    tiles = [da.bias[:, u % 3, 0, ::-1].rearrange("p (j z) -> p z j", z=2)]
                    tiles += [da.bias[:, u % 3, g:g + 1, S - 1 - qt::-2] for g in range(1, NG)]
                    at = 0
                    for g, tile in enumerate(tiles):
                        cols = slice(at, at + tile.shape[1] * P)
                        at = cols.stop
                        ins = v.scalar_tensor_tensor(da.sc[:, u % 3, cols].rearrange("p (z j) -> p z j", j=P),
                                                     da_bank(u)[:, cols].rearrange("p (z j) -> p z j", j=P),
                                                     da.rq[:, hb % 2, g, m, qt, e:e + 1], tile, ALU.mult, ALU.add)
                    ins.then_inc(sc_biased, 1)
                    v.wait_ge(sc_biased, u + 1)
                    v.reduce_max(da.stat[:, 0, u:u + 1], da.sc[:, u % 3], AX.X).then_inc(max_ready, 1)
                    v.wait_ge(max_ready, u + 1)
                    v.tensor_scalar(da.stat[:, 1, u:u + 1], da.stat[:, 0, u:u + 1], -1.0, None,
                                    ALU.mult).then_inc(neg_ready, 1)

                def scale_p(u):
                    v.wait_ge(p_ready, u + 1)
                    v.reciprocal(da.stat[:, 3, u:u + 1], da.stat[:, 2, u:u + 1]).then_inc(rden_ready, 1)
                    v.wait_ge(rden_ready, u + 1)
                    v.tensor_scalar(da.sc[:, u % 3], da.sc[:, u % 3], da.stat[:, 3, u:u + 1], None,
                                    ALU.mult).then_inc(p_scaled, 1)

                def lower(b):
                    v.wait_ge(o_hi_ready, b + 1)
                    v.tensor_tensor(h_lo[:, 2 * b:2 * b + 2, :], h[:, 2 * b:2 * b + 2, :],
                                    h_hi[:, 2 * b:2 * b + 2, :].bitcast(F32), ALU.subtract).then_inc(o_lo_ready, 1)

                for p in range(PANELS):
                    split(n0 + p + 2)
                    scale_due(p)
                last = n_units - UNITS
                for u in range(last):
                    bias(u)
                    panels = da_panels(u)
                    split(n0 + panels[0] + 2)
                    scale_p(u)
                    scale_due(panels[0])
                    for p in panels[1:]:
                        split(n0 + p + 2)
                        scale_due(p)
                bias(last)
                split(n0 + 38)
                for u in range(last + 1, n_units + 1):
                    if u < n_units:
                        bias(u)
                    scale_p(u - 1)
                    if u - last <= BLOCKS - 1:
                        lower(u - last - 1)
                lower(BLOCKS - 1)
                for k in range(4):
                    if k:
                        split(n0 + 36 + k + 2)
                    add_panel(st, k, 36)

            def mixer(st):
                nonlocal n_steps
                i, n0 = st["i"], st["n0"]

                def then(*ins):
                    nonlocal n_steps
                    for q in ins:
                        q.then_inc(mix_step, 1)
                        n_steps += 1
                    v.wait_ge(mix_step, n_steps)

                tt, ts, stt = v.tensor_tensor, v.tensor_scalar, v.scalar_tensor_tensor
                v.wait_ge(mix_loaded, 80 * (i + 1))

                def conv(p):
                    v.wait_ge(mix_copied, 25 * i + p + 1)
                    pair = (2 * p, 2 * p + 1)
                    then(*[ts(mx.conv[:, c], mx.raw[:, c, 0:S], mx.convw[:, c, 0:1], mx.convb[:, c:c + 1],
                              ALU.mult, ALU.add) for c in pair])
                    for k in range(1, CONV):
                        ops = [stt(mx.conv[:, c], mx.raw[:, c, k:k + S], mx.convw[:, c, k:k + 1], mx.conv[:, c],
                                   ALU.mult, ALU.add) for c in pair]
                        if k < CONV - 1:
                            then(*ops)
                        else:
                            for q in ops:
                                q.then_inc(conv_ready, 1)

                for p in range(6):
                    split(n0 + p + 2)
                    conv(p)
                split(n0 + 8)
                d = mx.dt
                v.wait_ge(mix_copied, 25 * i + 7)
                then(ts(d[0], d[0], mx.dtb, None, ALU.add))
                then(ts(d[1], d[0], -1.0, None, ALU.mult))
                tt(d[1], d[0], d[1], ALU.min).then_inc(dt_arg_ready, 1)
                for p in range(7, 11):
                    split(n0 + p + 2)
                v.wait_ge(dt_exp_ready, i + 1)
                then(ts(d[3], d[2], 2.0, None, ALU.add))
                then(v.reciprocal(d[3], d[3]))
                then(tt(d[2], d[2], d[3], ALU.mult))
                then(tt(d[3], d[2], d[2], ALU.mult))
                then(ts(d[4], d[3], 1.0 / (2 * LOG_TERMS + 1), None, ALU.mult))
                for k in range(LOG_TERMS - 1, 0, -1):
                    then(stt(d[4], d[4], 1.0 / (2 * k + 1), d[3], ALU.add, ALU.mult))
                then(stt(d[4], d[4], 1.0, d[2], ALU.add, ALU.mult), ts(d[0], d[0], 0.0, None, ALU.max))
                then(stt(d[0], d[4], 2.0, d[0], ALU.mult, ALU.add))
                v.wait_ge(a_ready, i + 1)
                v.wait_ge(small_set, i + 1)
                then(ts(d[5], d[0], mx.alog, -1.0, ALU.mult, ALU.mult),
                     v.tensor_copy(mx.small[64:64 + SSD_H, :], d[0]))
                v.tensor_tensor_scan(mx.small[0:SSD_H, :], ones[0:SSD_H, 0:1].to_broadcast([SSD_H, S]), d[5], 0.0,
                                     ALU.mult, ALU.add).then_inc(small_ready, 1)
                v.wait_ge(tok_copied, i + 1)
                ts(mx.wi, mx.tok[:, :, 32:32 + IDX_H], IDX_H ** -0.5, None, ALU.mult).then_inc(mix_step, 1)
                n_steps += 1
                v.wait_ge(cb_copied, 2 * i + 2)

                def y_tile(j):
                    v.wait_ge(yp_ready, 8 * i + j + 1)
                    stt(mx.y[:, j], mx.conv[:, j], mx.dskip[:, j:j + 1], bank[6 + j % 2][:, 0:S],
                        ALU.mult, ALU.add).then_inc(y_raw, 1)
                    v.wait_ge(y_raw, 8 * i + j + 1)
                    tt(mx.y[:, j], mx.y[:, j], mx.z[:, j], ALU.mult).then_inc(y_gated, 1)

                for j in range(SSD_H // 2):
                    for e in range(2):
                        hd = 2 * j + e
                        n = SSD_H * i + hd
                        v.wait_ge(cs_ready, n + 1)
                        if n >= 2:
                            v.wait_ge(decay_used, n - 1)
                        stt(mx.dec[:, e, 0], bank[4 + e][:, 0:S], mx.tok[:, 0, hd:hd + 1], mx.tri[:, 0], ALU.subtract, ALU.add)
                        stt(mx.dec[:, e, 1, P:], bank[4 + e][:, P:S], mx.tok[:, 1, hd:hd + 1], mx.tri[:, 1, P:],
                            ALU.subtract, ALU.add).then_inc(decay_arg, 1)
                    split(n0 + 11 + j + 2)
                    for e in range(2):
                        hd = 2 * j + e
                        n = SSD_H * i + hd
                        g = hd // (SSD_H // SSD_G)
                        v.wait_ge(decay_ready, n + 1)
                        if j:
                            v.wait_ge(yp_ready, 8 * i + j)
                        stt(mx.m[:, e, 0], mx.dec[:, e, 0], mx.tok[:, 0, 64 + hd:65 + hd], mx.cb[:, g, 0], ALU.mult, ALU.mult)
                        stt(mx.m[:, e, 1, P:], mx.dec[:, e, 1, P:], mx.tok[:, 1, 64 + hd:65 + hd], mx.cb[:, g, 1, P:],
                            ALU.mult, ALU.mult).then_inc(decay_used, 1)
                    if j:
                        y_tile(j - 1)
                y_tile(SSD_H // 2 - 1)
                for p in range(19, 25):
                    split(n0 + p + 2)
                for g in range(SSD_G):
                    v.wait_ge(yrms_ready, 2 * i + g + 1)
                    then(v.reciprocal(mx.dec[:, g, 0], mx.dec[:, g, 0]))
                    for c in range(4 * g, 4 * g + 4):
                        q = stt(mx.y[:, c], mx.y[:, c], mx.ygain[:, c:c + 1], mx.dec[:, g, 0], ALU.mult, ALU.mult)
                        if c % 2:
                            q.then_inc(y_normed, 1)
                for b in range(4):
                    v.wait_ge(y_hi_ready, 4 * i + b + 1)
                    tt(h_lo[:, 2 * b:2 * b + 2, :], mx.y[:, 2 * b:2 * b + 2, :],
                       h_hi[:, 2 * b:2 * b + 2, :].bitcast(F32), ALU.subtract).then_inc(y_lo_ready, 1)
                v.wait_ge(rope_ready, 1)
                for r in range(11):
                    n = 11 * i + r
                    if r < 8:
                        part = (mx.q, mx.k)[r // 4][0:ROPE_D, 2 * (r % 4):2 * (r % 4) + 2, :]
                    elif r < 10:
                        part = mx.qi[:, 2 * (r - 8):2 * (r - 8) + 2, :]
                    else:
                        part = mx.ki.unsqueeze(1)
                    rows, heads = part.shape[0], part.shape[1]
                    cos, sin = ((rope[0:rows, m + (0 if r < 8 else 2), :].unsqueeze(1).to_broadcast([rows, heads, S]))
                                for m in range(2))
                    tmp = mx.rot[0:rows, r % 4, 0:heads * S].rearrange("p (h s) -> p h s", h=heads)
                    v.wait_ge(rot_ready, n + 1)
                    tt(tmp, bank[4 + r % 4][0:rows, 0:heads * S].rearrange("p (h s) -> p h s", h=heads), sin,
                       ALU.mult).then_inc(rope_used, 1)
                    then(tt(part, part, cos, ALU.mult))
                    v.wait_ge(rope_used, n + 1)
                    tt(part, part, tmp, ALU.add).then_inc(rope_done, 1)
                    if r == 3:
                        for p in range(25, 29):
                            split(n0 + p + 2)
                for qt in range(2):
                    keys = (qt + 1) * P
                    sco = mx.score[:, qt, 0:keys]
                    for hd in range(IDX_H):
                        n = 2 * IDX_H * i + qt * IDX_H + hd
                        u = qt * IDX_H + hd
                        v.wait_ge(relu_ready, n + 1)
                        if hd:
                            v.wait_ge(idx_added, n)
                        if hd == 0:
                            v.wait_ge(mix_step, n_steps)
                            ins = ts(sco, mx.relu[:, u % 4, 0:keys], mx.wi[:, qt, hd:hd + 1], None, ALU.mult)
                        else:
                            ins = stt(sco, mx.relu[:, u % 4, 0:keys], mx.wi[:, qt, hd:hd + 1], sco, ALU.mult, ALU.add)
                        ins.then_inc(idx_added, 1)
                    v.wait_ge(idx_added, 2 * IDX_H * i + (qt + 1) * IDX_H)
                    then(tt(sco, sco, mx.causal[:, qt, 0:keys], ALU.add))
                    for _ in range(TOPK // 8):
                        then(v.max(mx.top8[:, qt], sco))
                        then(v.match_replace(sco, mx.top8[:, qt], sco, TAKEN))
                    sel = mx.sel[:, qt, 0:keys]
                    then(ts(sel, sco, TAKEN / 2, MASKED, ALU.is_gt, ALU.mult))
                    tt(sel, sel, mx.causal[:, qt, 0:keys], ALU.add).then_inc(sel_ready, 1)
                v.wait_ge(sel_ready, 2 * i + 2)
                units = 2 * ATT_H

                def scale_p(u):
                    keys = (u % 2 + 1) * P
                    v.wait_ge(att_p_ready, units * i + u + 1)
                    then(v.reciprocal(mx.stat[:, 3, u:u + 1], mx.stat[:, 2, u:u + 1]))
                    ts(mx.sc[:, u % 2, 0:keys], mx.sc[:, u % 2, 0:keys], mx.stat[:, 3, u:u + 1], None,
                       ALU.mult).then_inc(att_scaled, 1)

                for u in range(units):
                    n, qt = units * i + u, u % 2
                    keys = (qt + 1) * P
                    v.wait_ge(att_sc_ready, n + 1)
                    if u >= 2:
                        v.wait_ge(att_pt_ready, n - 1)
                    stt(mx.sc[:, u % 2, 0:keys], bank[4 + u % 2][:, 0:keys], P ** -0.5, mx.sel[:, qt, 0:keys],
                        ALU.mult, ALU.add).then_inc(att_biased, 1)
                    v.wait_ge(att_biased, n + 1)
                    then(v.reduce_max(mx.stat[:, 0, u:u + 1], mx.sc[:, u % 2, 0:keys], AX.X))
                    ts(mx.stat[:, 1, u:u + 1], mx.stat[:, 0, u:u + 1], -1.0, None, ALU.mult).then_inc(att_neg, 1)
                    if u:
                        scale_p(u - 1)
                scale_p(units - 1)
                for b in range(4):
                    v.wait_ge(att_hi_ready, 4 * i + b + 1)
                    tt(h_lo[:, 2 * b:2 * b + 2, :], mx.yatt[:, 2 * b:2 * b + 2, :],
                       h_hi[:, 2 * b:2 * b + 2, :].bitcast(F32), ALU.subtract).then_inc(att_lo_ready, 1)
                for k in range(4):
                    split(n0 + 29 + k + 2)
                    add_panel(st, k, 29)

            n_steps = 0
            v.memset(zeros[:, :].bitcast(F32), 0.0).then_inc(zeros_set, 1)
            split(0)
            split(1)
            if dilated:
                v.wait_ge(e_ready, 1)
                v.tensor_tensor(da.e, bank[0][0:NG * HEADS, :], da.mask, ALU.add).then_inc(e_masked, 1)
            if any(st["kind"] == "s5" for st in stages):
                s5_prepare()
            todo = {"norm": norm, "final": norm, "ffn": ffn, "fourier": fourier, "s5": s5_mixer,
                    "dilated": dilated_mixer, "mix": mixer}
            for n, st in enumerate(stages):
                st["s5_follows"] = [q["kind"] for q in stages[n + 1:n + 3]] == ["norm", "s5"]
                todo[st["kind"]](st)

        @block.tensor
        def _(t):
            def mm3(o, w, xin, start, stop):
                t.matmul(o, w[0], xin[0], start=start, stop=False, skip_group_check=True)
                t.matmul(o, w[0], xin[1], start=False, stop=False, skip_group_check=True)
                return t.matmul(o, w[1], xin[0], start=False, stop=stop, skip_group_check=True)

            def weights(n, lo, width=P):
                s = n % SLOTS
                return w_hi[:, s, lo:lo + width], w_lo[:, s, lo:lo + width]

            def project(n, j, i=None, per=0, parts=None, o=None):
                t.wait_ge(lo_ready, n + 1 if i is None else i * per + n + 1)
                o = bank[j % PROJ_BANKS] if o is None else o
                for k, m in [(k, m) for k in range(KT) for m in range(2)] if parts else \
                        [(k, m) for m in range(2) for k in range(KT)]:
                    if parts and m == 0 and k % 2 == 0:
                        t.wait_ge(parts[0], parts[1] + k // 2 + 1)
                    last = mm3(o[:, m * S:(m + 1) * S], weights(n, k * COLS + m * P), (h_hi[:, k], h_lo[:, k]),
                               k == 0 and (m == 0 or parts is None), k == KT - 1)
                last.then_inc(panel_done, 1)

            def norm(st):
                n = st["norm"]
                t.wait_ge(const_set, 3)
                for b in range(4):
                    t.wait_ge(sq_ready, 4 * n + b + 1)
                    for c in (2 * b, 2 * b + 1):
                        last = t.matmul(bank[4][:, 0:S], ones[:, :], h[:, c, :], start=(c == 0), stop=(c == KT - 1))
                last.then_inc(ss_ready, 1)

            def ffn(st):
                n0, f = st["n0"], st["ffn"]

                def down(c, p, i=None):
                    def at(val, per):
                        return val if i is None else i * per + val
                    t.wait_ge(lo_ready, at(p + 1, 6))
                    t.wait_ge(act_lo_ready, at(f * FFC + c + 1, 2))
                    for k in range(2):
                        for o in range(KT):
                            last = mm3(y_of[o], weights(p, k * D + o * P),
                                       (act_hi[:, c % 2, k], act_lo[:, c % 2, k]), False, True)
                            if c == FFC - 1 and k == 1 and o % 2 and o < KT - 1:
                                last.then_inc(sums_ready, 1)
                    last.then_inc(panel_done, 1)

                t.wait_ge(zeros_set, 1)
                t.wait_ge(rms_ready, st["hn"] + 1)
                for b in range(4):
                    t.matmul(bank[4 + b][:, :].rearrange("p (a m) -> p a m", m=P), zeros[:, :],
                             zeros[:, :].unsqueeze(1).to_broadcast([P, 4, P]), start=True, stop=True)
                project(n0, 0, parts=(h_lo_ready, 4 * st["hs"]))
                project(n0 + 1, 1)
                with t.Fori(0, (FFC - 1) // 2) as i:
                    for c in (1, 2):
                        p = hidden_panel(n0, c)
                        t.wait_ge(act_ready, i * 2 + (f * FFC + c - 1))
                        project(p, 2 * c, i, 6)
                        project(p + 1, 2 * c + 1, i, 6)
                        down(c - 1, p + 2, i)
                down(FFC - 1, n0 + 32)

            def fourier(st):
                f = st["fourier"]
                t.wait_ge(dft_loaded, 32 * (f + 1))
                t.wait_ge(h_lo_ready, 4 * (st["hs"] + 1))

                def over_channels(g):
                    k = f * KT + g
                    if g >= 2:
                        t.wait_ge(dft_tok_copied, k - 1)
                    for m in range(2):
                        last = t.matmul(bank[4 + g % 2][:, m * S:(m + 1) * S], h[:, g, m * P:(m + 1) * P],
                                        dft_ch, start=True, stop=True)
                    last.then_inc(dft_tok_ready, 1)

                over_channels(0)
                for g in range(KT):
                    k = f * KT + g
                    if g + 1 < KT:
                        over_channels(g + 1)
                    t.wait_ge(dft_tok_copied, k + 1)
                    if g >= 2:
                        t.wait_ge(dft_lo_ready, k - 1)
                    for m in range(2):
                        for c in range(2):
                            last = t.matmul(bank[6 + g % 2][:, 0:S], dft_tok[:, g % 2, m, c * P:(c + 1) * P],
                                            dft_sq[:, m, c, :], start=(m + c == 0), stop=(m + c == 2))
                    last.then_inc(dft_ready, 1)
                t.wait_ge(dft_lo_ready, (f + 1) * KT)
                for p in range(4):
                    project(st["n0"] + p, p)

            def s5_mixer(st):
                half = [slice(0, S5_N), slice(S5_N, P)]

                def factors(f):
                    vb = s5.buf[f % 2]
                    t.wait_ge(s5_v_ready, f + 1)
                    for q in range(4):
                        if 4 * f + q >= 2:
                            t.wait_ge(s5_win_ready, 4 * f + q - 1)
                        for m in range(4):
                            r, c = divmod(4 * q + m, NC)
                            last = t.transpose(bank[4 + q % 2][:, m * P:(m + 1) * P], vb[:, r, c, :], ident[:, :])
                        last.then_inc(s5_vt_ready, 1)
                    if f:
                        t.wait_ge(s5_k_copied, f)
                    t.wait_ge(s5_cbd_ready, 1 + 4 * (f + 1))
                    for c in range(NC):
                        for r in range(2):
                            last = t.matmul(bank[0][:, c * 2 * S5_P:(c + 1) * 2 * S5_P], vb[:, r, c, :],
                                            s5.cbd[:, f % 2, r, c, :], start=(r == 0), stop=(r == 1))
                    last.then_inc(s5_k_ready, 1)

                t.wait_ge(rms_ready, st["hn"] + 1)
                factors(0)
                t.wait_ge(s5_u_loaded, 16)
                for f in range(KT):
                    t.wait_ge(s5_win_ready, 4 * f + 4)
                    if f >= 2:
                        t.wait_ge(s5_in_copied, f - 1)
                    for r in range(2):
                        for c in range(NC):
                            for e in range(2):
                                g = f * KT + (c % 4) * 2 + e
                                o = bank[2 + f % 2][half[e], (r * NC + c) * S5_C:(r * NC + c + 1) * S5_C]
                                rhs = s5.u[:, g, :] if c < 4 else s5.u[:, g, ::-1]
                                last = t.matmul(o, s5.win[:, r * NC + c, half[e]], rhs, start=True, stop=True)
                    last.then_inc(s5_in_ready, 1)
                    t.wait_ge(s5_k_copied, f + 1)
                    if f:
                        t.wait_ge(s5_t_copied, 2 * f)
                    for i in range(S5_T):
                        o = bank[7 - i // 4][:, (i % 4) * P:(i % 4 + 1) * P]
                        for d in range(2):
                            off = S5_P * i if d == 0 else 7 * S5_P + S5_P * i
                            last = t.matmul(o, s5.wide[:, off:off + P], s5.kc[:, d * P:(d + 1) * P],
                                            start=(d == 0), stop=(d == 1))
                    last.then_inc(s5_t_ready, 1)
                    if f + 1 < KT:
                        factors(f + 1)
                    t.wait_ge(s5_t_copied, 2 * f + 2)
                    if f:
                        t.wait_ge(s5_intra_copied, f)
                    for g in range(KT):
                        last = t.matmul(bank[1][:, g * S5_C:(g + 1) * S5_C], s5.tc[:, g].rearrange("p i m -> p (i m)"),
                                        s5.u[:, f * KT + g, :], start=True, stop=True)
                    last.then_inc(s5_intra_ready, 1)
                w_dve = [f for f in range(KT) if f not in W_POOL]
                for f in range(KT):
                    if f in W_POOL:
                        t.wait_ge(s5_wp_ready, W_POOL.index(f) + 1)
                    else:
                        t.wait_ge(s5_w_ready, w_dve.index(f) + 1)
                    t.wait_ge(s5_zbd_ready, 4 * f + 4)
                    if f >= 4:
                        t.wait_ge(s5_y_ready, f - 3)
                    for pair in range(4):
                        o = bank[4 + f % 4][:, pair * 2 * S5_C:(pair + 1) * 2 * S5_C]
                        for d in range(2):
                            for r in range(2):
                                last = t.matmul(o, s5.w[f % 4][:, r, 4 * d + pair, :], s5.zbd[:, f % 2, r, 4 * d + pair, :],
                                                start=(d + r == 0), stop=(d + r == 2))
                    last.then_inc(s5_out_ready, 1)
                for p in range(8):
                    if p >= PROJ_BANKS:
                        t.wait_ge(x_ready, st["xr"] + p // 2 - 1)
                    project(st["n0"] + p, p, parts=None if p else (s5_g_lo_ready, 0))

            def project_tokens(n, o, tokens):
                t.wait_ge(lo_ready, n + 1)
                for m in range(2):
                    for k in range(KT):
                        last = mm3(o[:, m * COLS:(m + 1) * COLS], (h_hi[:, k, tokens[m]], h_lo[:, k, tokens[m]]),
                                   weights(n, k * COLS, COLS), k == 0, k == KT - 1)
                last.then_inc(panel_done, 1)

            def dilated_mixer(st):
                n0 = st["n0"]
                alone = n_units - UNITS

                def sums(c):
                    t.wait_ge(qk_sq_ready, c + 1)
                    if c >= 2:
                        t.wait_ge(qk_rms_ready, c - 1)
                    if c % 2 == 0:
                        for m in range(2):
                            for qt in range(2):
                                at = (2 * m + qt) * 2
                                last = t.matmul(bank[3][:, at:at + 2], da.sq[:, 0, m * S + qt:(m + 1) * S:2],
                                                da.pair_ones[:, 0:P:E], start=True, stop=True)
                    else:
                        last = t.matmul(bank[5][:, :], da.pair_ones, da.sq[:, 1], start=True, stop=True)
                    last.then_inc(qk_ss_ready, 1)

                def panel(p):
                    hb, i, _ = da_panel(p)
                    if p >= 3:
                        _, i3, c3 = da_panel(p - 3)
                        t.wait_ge(qk_copied if i3 < QK else v_copied, c3 + 1)
                    o = bank[p % 3]
                    if i < QK:
                        project(n0 + p, 0, o=o, parts=None if p else (h_lo_ready, 4 * st["hs"]))
                    else:
                        project_tokens(n0 + p, o, (slice(0, S, 2), slice(1, S, 2)))
                    if 1 <= i <= QK:
                        sums(hb * QK + i - 1)

                def scores(u):
                    hb, head, qt = u // UNITS, u // 2, u % 2
                    m, rows = head // 2 % 2, slice(head % 2 * E, head % 2 * E + E)
                    t.wait_ge(qk_ready, QK * (hb + 1))
                    if u:
                        t.wait_ge(sc_biased, u if u <= alone + 1 else u - 1)
                    q, k = da.qk[rows, hb % 2, 0, :, m], da.qk[rows, hb % 2, 1, :, m]
                    t.matmul(da_bank(u)[:, 0:S].rearrange("p (z j) -> p z j", z=2), q[:, 0, qt::2],
                             k[:, 0, :].rearrange("p (j z) -> p z j", z=2), start=True, stop=True)
                    for g in range(1, NG):
                        last = t.matmul(da_bank(u)[:, S + (g - 1) * P:S + g * P], q[:, g, qt::2], k[:, g, qt::2],
                                        start=True, stop=True)
                    last.then_inc(sc_ready, 1)

                def values(u):
                    t.wait_ge(p_scaled, u + 1)
                    if u:
                        t.wait_ge(pt_copied, u)
                    for i in range(4):
                        last = t.transpose(bank[6][:, i * P:(i + 1) * P], da.sc[:, u % 3, i * P:(i + 1) * P], ident[:, :])
                    last.then_inc(pt_ready, 1)

                def out_(u):
                    hb, head, qt = u // UNITS, u // 2, u % 2
                    rows = slice(head % 2 * E, head % 2 * E + E)
                    cols = slice(head % HB * E, head % HB * E + E)
                    t.wait_ge(pt_copied, u + 1)
                    t.wait_ge(v_copied, NG * (hb + 1))
                    if u:
                        t.wait_ge(o_copied, u)
                    for i, (g, parity) in enumerate(((0, 0), (0, 1), (1, qt), (2, qt))):
                        last = t.matmul(bank[7][rows, 0:P], da.v[:, hb % 2, g, parity, cols],
                                        da.pt[:, u % 2, i * P:(i + 1) * P], start=(i == 0), stop=(i == 3))
                    last.then_inc(o_ready, 1)

                def output(k, tiles):
                    t.wait_ge(lo_ready, n0 + 36 + k + 1)
                    t.wait_ge(o_lo_ready, (tiles[-1] + 2) // 2)
                    for c in tiles:
                        for m in range(2):
                            last = mm3(bank[k][:, m * S:(m + 1) * S], weights(n0 + 36 + k, c * COLS + m * P),
                                       (h_hi[:, c], h_lo[:, c]), c + m == 0, c == KT - 1)
                    if tiles[-1] == KT - 1:
                        last.then_inc(panel_done, 1)

                t.wait_ge(rms_ready, st["hn"] + 1)
                t.wait_ge(e_loaded, 16 * 5)
                for p in range(PANELS):
                    panel(p)
                for u in range(alone):
                    scores(u)
                    if u:
                        out_(u - 1)
                    for p in da_panels(u):
                        panel(p)
                    values(u)
                scores(alone)
                out_(alone - 1)
                scores(alone + 1)
                early = list(range(KT - 2))
                for u in range(alone, n_units):
                    if u + 2 < n_units:
                        scores(u + 2)
                    values(u)
                    if u > alone:
                        out_(u - 1)
                    if u - alone in (2, 4, 6):
                        output((u - alone) // 2 - 1, early)
                out_(n_units - 1)
                for k in range(3):
                    output(k, [KT - 2, KT - 1])
                output(3, early + [KT - 2, KT - 1])

            def mixer(st):
                i, n0 = st["i"], st["n0"]

                def arrive(p, tokens=False, first=False):
                    if p >= PROJ_BANKS:
                        t.wait_ge(mix_copied, 25 * i + p - PROJ_BANKS + 1)
                    if tokens:
                        project_tokens(n0 + p, bank[p % PROJ_BANKS], (slice(0, P), slice(P, S)))
                    else:
                        project(n0 + p, p, parts=(h_lo_ready, 4 * st["hs"]) if first else None)

                def accumulate(p, k, first):
                    t.wait_ge(lo_ready, n0 + p + 1)
                    for m in range(2):
                        for c in range(KT):
                            last = mm3(bank[k][:, m * S:(m + 1) * S], weights(n0 + p, c * COLS + m * P),
                                       (h_hi[:, c], h_lo[:, c]), first and m == 0 and c == 0, c == KT - 1)
                    last.then_inc(panel_done, 1)

                for p in range(11):
                    arrive(p, first=p == 0)
                for q in range(4):
                    t.wait_ge(conv_act, CONV_T * i + 2 * q + 2)
                    if q >= 2:
                        t.wait_ge(xt_copied, 4 * i + q - 1)
                    for tt_ in range(2):
                        for c in range(2):
                            last = t.transpose(bank[5 + q % 2][:, (tt_ * 2 + c) * P:(tt_ * 2 + c + 1) * P],
                                               mx.conv[:, 2 * q + c, tt_ * P:(tt_ + 1) * P], ident[:, :])
                    last.then_inc(xt_ready, 1)
                t.wait_ge(small_ready, i + 1)
                for tt_ in range(2):
                    last = t.transpose(bank[4][:, tt_ * P:(tt_ + 1) * P], mx.small[:, tt_ * P:(tt_ + 1) * P], ident[:, :])
                last.then_inc(tok_ready, 1)
                t.wait_ge(conv_act, CONV_T * (i + 1))
                for g in range(SSD_G):
                    if g:
                        t.wait_ge(tok_copied, i + 1)
                    o = bank[7 if g == 0 else 4]
                    for tt_ in range(2):
                        last = t.matmul(o[:, tt_ * (S + P):2 * S if tt_ else S], mx.conv[:, 8 + g, tt_ * P:(tt_ + 1) * P],
                                        mx.conv[:, 8 + SSD_G + g, tt_ * P:], start=True, stop=True)
                    last.then_inc(cb_ready, 1)
                t.wait_ge(cb_copied, 2 * i + 2)
                t.wait_ge(xt_copied, 4 * i + 4)
                for j in range(SSD_H // 2):
                    for e in range(2):
                        n = SSD_H * i + 2 * j + e
                        if j:
                            t.wait_ge(decay_arg, n - 1)
                        t.matmul(bank[4 + e][:, 0:S], ident[0:SSD_H, 2 * j + e:2 * j + e + 1].to_broadcast([SSD_H, P]),
                                 mx.small[0:SSD_H, :], start=True, stop=True).then_inc(cs_ready, 1)
                    arrive(11 + j)
                    if j >= 2:
                        t.wait_ge(y_raw, 8 * i + j - 1)
                    for e in range(2):
                        hd = 2 * j + e
                        t.wait_ge(decay_used, SSD_H * i + hd + 1)
                        o = bank[6 + j % 2][e * SSD_P:(e + 1) * SSD_P, :]
                        heads = slice(hd * SSD_P, (hd + 1) * SSD_P)
                        t.matmul(o[:, 0:P], mx.xt[:, 0, heads], mx.m[:, e, 0, 0:P], start=True, stop=True)
                        t.matmul(o[:, P:S], mx.xt[:, 0, heads], mx.m[:, e, 0, P:], start=True, stop=False)
                        last = t.matmul(o[:, P:S], mx.xt[:, 1, heads], mx.m[:, e, 1, P:], start=False, stop=True)
                    last.then_inc(yp_ready, 1)
                for p in range(19, 25):
                    arrive(p, p >= 21)
                for g in range(SSD_G):
                    t.wait_ge(ysq_ready, 2 * i + g + 1)
                    for c in range(4):
                        last = t.matmul(bank[4 + g][:, 0:S], ones[:, :], mx.z[:, 4 * g + c], start=(c == 0), stop=(c == 3))
                    last.then_inc(yss_ready, 1)
                t.wait_ge(y_raw, 8 * i + 8)
                t.wait_ge(yrms_ready, 2 * i + 2)
                t.wait_ge(mix_copied, 25 * (i + 1))
                for r in range(11):
                    if r >= 4:
                        t.wait_ge(rope_used, 11 * i + r - 3)
                    if r < 8:
                        src = (mx.q, mx.k)[r // 4][0:ROPE_D, 2 * (r % 4):2 * (r % 4) + 2, :].rearrange("p h s -> p (h s)")
                        last = t.matmul(bank[4 + r % 4][0:ROPE_D, :], mx.turn[0:ROPE_D, :], src, start=True, stop=True)
                    elif r < 10:
                        src = mx.qi[:, 2 * (r - 8):2 * (r - 8) + 2, :].rearrange("p h s -> p (h s)")
                        last = t.matmul(bank[4 + r % 4][:, :], mx.turn_i, src, start=True, stop=True)
                    else:
                        last = t.matmul(bank[4 + r % 4][:, 0:S], mx.turn_i, mx.ki, start=True, stop=True)
                    last.then_inc(rot_ready, 1)
                    if r == 3:
                        t.wait_ge(y_lo_ready, 4 * (i + 1))
                        for k in range(4):
                            accumulate(25 + k, k, True)
                t.wait_ge(rope_done, 11 * (i + 1))
                for u in range(2 * IDX_H):
                    qt, hd = divmod(u, IDX_H)
                    rows = slice(hd % 2 * E, hd % 2 * E + E)
                    n = 2 * IDX_H * i + u
                    if u >= 4:
                        t.wait_ge(relu_ready, n - 3)
                    t.matmul(bank[4 + u % 4][:, 0:(qt + 1) * P], mx.qi[rows, hd // 2, qt * P:(qt + 1) * P],
                             mx.ki[rows, 0:(qt + 1) * P], start=True, stop=True).then_inc(idx_ready, 1)
                units = 2 * ATT_H

                def scores(u):
                    hd, qt = divmod(u, 2)
                    if u >= 2:
                        t.wait_ge(att_biased, units * i + u - 1)
                    t.matmul(bank[4 + u % 2][:, 0:(qt + 1) * P], mx.q[:, hd, qt * P:(qt + 1) * P],
                             mx.k[:, hd, 0:(qt + 1) * P], start=True, stop=True).then_inc(att_sc_ready, 1)

                def values(u):
                    qt = u % 2
                    t.wait_ge(att_scaled, units * i + u + 1)
                    if u:
                        t.wait_ge(att_pt_copied, units * i + u)
                    for k in range(qt + 1):
                        last = t.transpose(bank[6][:, k * P:(k + 1) * P], mx.sc[:, u % 2, k * P:(k + 1) * P], ident[:, :])
                    last.then_inc(att_pt_ready, 1)

                def out_(u):
                    hd, qt = divmod(u, 2)
                    t.wait_ge(att_pt_copied, units * i + u + 1)
                    if u:
                        t.wait_ge(att_o_copied, units * i + u)
                    for k in range(qt + 1):
                        last = t.matmul(bank[7][:, u % 2 * P:(u % 2 + 1) * P], mx.v[:, k, hd * P:(hd + 1) * P],
                                        mx.pt[:, u % 2, k * P:(k + 1) * P], start=(k == 0), stop=(k == qt))
                    last.then_inc(att_o_ready, 1)

                t.wait_ge(relu_ready, 2 * IDX_H * (i + 1))
                scores(0)
                for u in range(units):
                    if u + 1 < units:
                        scores(u + 1)
                    values(u)
                    if u:
                        out_(u - 1)
                out_(units - 1)
                t.wait_ge(att_lo_ready, 4 * (i + 1))
                for k in range(4):
                    accumulate(29 + k, k, False)

            if dilated:
                t.wait_ge(e_loaded, 16 * 3)
                t.matmul(bank[0][0:NG * HEADS, :], da.rel, da.onehot, start=True, stop=True).then_inc(e_ready, 1)
            todo = {"norm": norm, "final": norm, "ffn": ffn, "fourier": fourier, "s5": s5_mixer,
                    "dilated": dilated_mixer, "mix": mixer}
            for st in stages:
                todo[st["kind"]](st)


def panel_of(w, c0):
    return w[:, c0:c0 + COLS].reshape(KT, P, COLS).transpose(1, 0, 2).reshape(P, PANEL)


def rows_panel(w, c):
    return w[c * COLS:(c + 1) * COLS].reshape(2, P, D).transpose(1, 0, 2).reshape(P, PANEL)


def ffn_panels(w_in, w_out):
    yield panel_of(w_in, 0)
    yield panel_of(w_in, FF)
    for c in range(1, FFC):
        yield panel_of(w_in, c * COLS)
        yield panel_of(w_in, FF + c * COLS)
        yield rows_panel(w_out, c - 1)
    yield rows_panel(w_out, FFC - 1)


def gain_columns(g):
    return g.reshape(-1, KT, P).transpose(2, 0, 1).reshape(P, -1)


def lay_out(inp):
    x = np.asarray(inp["x"])[0]
    a = {"x": np.ascontiguousarray(x.T)}
    panels = []
    rows = []
    for i in range(BLOCK1):
        rows += [inp["norm_mix_g"][i], inp["norm_ffn_g"][i]]
        if i % 3 == 0:
            panels += [panel_of(inp["fnet_w_out"][i // 3], c * COLS) for c in range(4)]
        if i % 3 == 1:
            w = inp["s5_w_glu"][i // 3]
            panels += [panel_of(w, c * COLS + m * D) for c in range(4) for m in range(2)]
        if i % 3 == 2:
            w = inp["attn_w_qkv"][i // 3]
            for b in range(HEADS // HB):
                panels += [panel_of(w, (g * 3 + m) * D + b * COLS) for ms in ((0, 1), (2,)) for g in range(NG) for m in ms]
            panels += [panel_of(inp["attn_w_o"][i // 3], c * COLS) for c in range(4)]
        panels += ffn_panels(inp["ffn_w_gate_up"][i], inp["ffn_w_down"][i])
    cols = []
    for i in range(BLOCK2):
        rows += [inp["norm_ffn1_2"][i], inp["norm_mix_2"][i], inp["norm_ffn2_2"][i]]
        panels += ffn_panels(inp["w_ffn1_in_2"][i], inp["w_ffn1_out_2"][i])
        w = inp["w_mix_in_2"][i]
        sizes = (D, CONV_T * P, SSD_H, D, D, D, IDX_H * E, E, IDX_H)
        z, xbc, dt, q, k, v, qi, ki, wi = np.split(w, np.cumsum(sizes)[:-1], 1)
        misc = np.zeros((D, COLS), np.float32)
        misc[:, 0:E], misc[:, E:2 * E] = ki, ki
        misc[:, P:P + SSD_H], misc[:, P + 32:P + 32 + IDX_H] = dt, wi
        for part in (xbc, misc, z, qi, q, k, v, inp["w_mix_out_2"][i][:D], inp["w_mix_out_2"][i][D:]):
            panels += [panel_of(part, c) for c in range(0, part.shape[1], COLS)]
        panels += ffn_panels(inp["w_ffn2_in_2"][i], inp["w_ffn2_out_2"][i])
        tail = np.zeros((P, 3), np.float32)
        tail[:SSD_H, 0], tail[:SSD_H, 1] = inp["dt_bias_2"][i], inp["a_log_2"][i]
        cols.append(np.concatenate([
            inp["conv_w_2"][i].reshape(CONV, CONV_T, P).transpose(2, 1, 0).reshape(P, -1),
            inp["conv_b_2"][i].reshape(CONV_T, P).T,
            np.repeat(inp["d_skip_2"][i], SSD_P).reshape(KT, P).T,
            inp["ssd_norm_2"][i].reshape(KT, P).T, tail], 1))
    a["mix_col"] = np.stack(cols)
    rows.append(inp["final_norm_2"])
    a["gains"] = gain_columns(np.stack(rows))
    tok = np.arange(S).reshape(2, P).T[:, :, None]
    along = np.arange(S)[None, None, :]
    a["mask_tri"] = np.where(along >= tok, 0.0, MASKED).astype(np.float32)
    a["mask_causal"] = np.where(along <= tok, 0.0, MASKED).astype(np.float32)
    a["positions"] = np.broadcast_to(inp["positions_2"], (P, S)).astype(np.int32)

    def freqs(rot):
        return np.float32(ROPE_THETA) ** (-np.arange(0, rot, 2, dtype=np.float32) / np.float32(rot))

    def turned(rot):
        half = rot // 2
        m = np.zeros((rot, rot), np.float32)
        m[np.arange(half) + half, np.arange(half)] = -1
        m[np.arange(half), np.arange(half) + half] = 1
        return m

    a["turn"] = turned(ROPE_D)
    a["turn_i"] = np.zeros((P, P), np.float32)
    freq = np.zeros((P, 2), np.float32)
    freq[:ROPE_D, 0] = np.tile(freqs(ROPE_D), 2)
    for half in (0, E):
        a["turn_i"][half:half + ROPE_I, half:half + ROPE_I] = turned(ROPE_I)
        freq[half:half + ROPE_I, 1] = np.tile(freqs(ROPE_I), 2)
    a["rope_freq"] = freq
    k = np.arange(P)
    ang = 2 * np.pi * (np.outer(k, k) % P) / P
    a["dft_ch"] = np.concatenate([np.cos(ang), -np.sin(ang)], 1).astype(np.float32)
    k = np.arange(S)
    ang = 2 * np.pi * (np.outer(k, k) % S) / S
    scale = 1.0 / np.sqrt(S * P)
    a["dft_sq"] = (np.concatenate([np.cos(ang), np.sin(ang)], 1) * scale).astype(np.float32)
    a["rel_bias"] = inp["rel_bias"]
    rel = S - 1 - np.arange(2 * S)
    half = BUCKETS // 2
    exact = half // 2
    n = np.abs(rel)
    large = exact + (np.log(np.maximum(n, 1) / exact) / np.log(MAX_DISTANCE / exact) * (half - exact)).astype(np.int32)
    bucket = (rel > 0) * half + np.where(n < exact, n, np.minimum(large, half - 1))
    a["bucket_onehot"] = (bucket[None] == np.arange(BUCKETS)[:, None]).astype(np.float32)
    allowed = np.stack([(n % dil == 0) & (n // dil <= window // 2 // dil) for window, dil in GROUPS])
    a["group_mask"] = np.repeat(np.where(allowed, 0.0, MASKED).astype(np.float32), HEADS, 0)
    a["pair_ones"] = np.kron(np.eye(2), np.ones((E, E))).astype(np.float32)
    gains = np.concatenate([inp["attn_q_gain"][0], inp["attn_k_gain"][0]])
    a["qk_gain"] = np.tile(gains, (1, 2)).T
    a["ident"] = np.eye(P, dtype=np.float32)

    def s5_columns(w):
        w = w.reshape((2, KT, 4, 2, S5_N) + w.shape[3:])
        w = w.transpose((3, 4, 1, 0, 2) + tuple(range(5, w.ndim)))
        return w.reshape(P, -1)

    lam = [inp["s5_lambda_re"][0], inp["s5_lambda_im"][0],
           np.broadcast_to(inp["s5_log_dt"][0][:, :, None], (2, S5_G, S5_N))]
    a["s5_lam"] = np.concatenate([s5_columns(w) for w in lam], 1)
    a["s5_b"] = np.concatenate([s5_columns(inp["s5_b_" + r][0]) for r in ("re", "im")], 1)
    a["s5_c"] = np.concatenate([s5_columns(inp["s5_c_" + r][0].transpose(0, 1, 3, 2)) for r in ("re", "im")], 1)
    a["s5_d"] = gain_columns(inp["s5_d"])
    a["s5_wide"] = np.eye(P, 352, 112, dtype=np.float32)
    return a, panels


def kernel(**inputs):
    import concourse.bacc as bacc
    from concourse.bass_utils import run_bass_kernel_spmd

    data, panels = lay_out({name: np.asarray(value) for name, value in inputs.items()})
    data["panels"] = np.stack(panels + [panels[-1]])
    nc = bacc.Bacc("TRN2", target_bir_lowering=False, num_devices=1)
    arrays = {"in_" + name: np.ascontiguousarray(value) for name, value in data.items()}
    dram = {name: nc.dram_tensor("in_" + name, value.shape, mybir.dt.from_np(value.dtype), kind="ExternalInput").ap()
            for name, value in data.items()}
    out = nc.dram_tensor("out", (D, S), F32, kind="ExternalOutput").ap()
    build(nc, dram, out)
    got = run_bass_kernel_spmd(nc, [arrays], core_ids=[0]).results[0]["out"]
    return np.ascontiguousarray(np.asarray(got).T)[None]
```

```python
from contextlib import ExitStack

import numpy as np
import concourse.bass as bass
from concourse import mybir
from concourse.alu_op_type import AluOpType as ALU

F32 = mybir.dt.float32
F32R = mybir.dt.float32r
ACT = mybir.ActivationFunctionType
AX = mybir.AxisListType

P = 128
D = 1024
S = 256
KT = D // P
FF = 2816
COLS = 256
PANEL = KT * COLS
FFC = FF // COLS
SLOTS = 3
PROJ_BANKS = 4
EPS = 1e-6
TWO_PI = 2 * np.pi
TWO_PI_1 = 6.28125
TWO_PI_2 = float(np.float32(1.93500518798828125e-3))
TWO_PI_3 = TWO_PI - TWO_PI_1 - TWO_PI_2
ROUND = 1.5 * 2.0 ** 23
PI_BELOW = float(np.nextafter(np.float32(np.pi), np.float32(0)))
MASKED = -1e30
HEADS = 16
E = 64
GROUPS = ((128, 1), (512, 4), (2048, 16))
NG = len(GROUPS)
BUCKETS = 32
MAX_DISTANCE = 1024
HB = 4
SSD_H = 16
SSD_P = 64
SSD_G = 2
SSD_N = 128
CONV = 4
CONV_T = (SSD_H * SSD_P + 2 * SSD_G * SSD_N) // P
ATT_H = 8
IDX_H = 8
TOPK = min(256, S // 4)
ROPE_THETA = 500000.0
ROPE_D = P // 4
ROPE_I = E // 4
TAKEN = -3e38
LOG_TERMS = 8
S5_T = 8
S5_C = S // S5_T
S5_P = 16
S5_N = 64
S5_G = D // S5_P
BLOCK1 = 4
BLOCK2 = 2


def plan_stages():
    stages = []
    panel = xr = norm = ffn = split = whole = 0
    mixers = ["fourier", "s5", "dilated", "fourier"]
    todo = []
    for i in range(BLOCK1):
        todo += [("norm", i), (mixers[i], i), ("norm", BLOCK1 + i), ("ffn", i)]
    for i in range(BLOCK2):
        b = 2 * BLOCK1 + 3 * i
        todo += [("norm", b), ("ffn", BLOCK1 + 2 * i), ("norm", b + 1), ("mix", i),
                 ("norm", b + 2), ("ffn", BLOCK1 + 2 * i + 1)]
    todo.append(("final", 2 * BLOCK1 + 3 * BLOCK2))
    panels_of = {"fourier": 4, "s5": 8, "dilated": 40, "ffn": 3 * FFC, "mix": 25 + 8}
    for kind, i in todo:
        st = {"kind": kind, "i": i, "n0": panel, "xr": xr}
        if kind in ("norm", "final"):
            st["norm"] = norm
            norm += 1
            st["split"] = kind == "norm" and todo[len(stages) + 1][0] not in ("fourier", "s5")
            st["late"] = kind == "norm" and todo[len(stages) + 1][0] == "ffn"
            st["after_ffn"] = kind == "norm" and bool(stages) and stages[-1]["kind"] == "ffn"
            st["whole"] = whole
            whole += not st["late"]
            st["dft"] = kind == "norm" and todo[len(stages) + 1][0] == "fourier"
            st["hs"] = split
            split += st["split"]
        else:
            xr += 4
            panel += panels_of[kind]
        st["hn"] = norm - 1
        st.setdefault("hs", split - 1)
        st.setdefault("whole", whole - 1)
        if kind == "ffn":
            st["ffn"] = ffn
            ffn += 1
        stages.append(st)
    return stages, panel


def build(nc, A, out):
    stages, n_panels = plan_stages()

    with ExitStack() as ctx:
        def sb(name, shape, dt=F32):
            return ctx.enter_context(nc.sbuf_tensor(name, shape, dt))

        def sem(name):
            return ctx.enter_context(nc.semaphore(name))

        raw = sb("raw", [P, SLOTS, PANEL])
        w_hi = sb("w_hi", [P, SLOTS, PANEL], F32R)
        w_lo = sb("w_lo", [P, SLOTS, PANEL], F32R)
        x = sb("x", [P, KT, S])
        h = sb("h", [P, KT, S])
        h_hi = sb("h_hi", [P, KT, S], F32R)
        h_lo = sb("h_lo", [P, KT, S], F32R)
        rstd = sb("rstd", [P, S])
        gains = sb("gains", [P, A["gains"].shape[1]])
        ones = sb("ones", [P, P])
        zeros = sb("zeros", [P, P], F32R)
        eps = sb("eps", [P, 1])
        eps_head = sb("eps_head", [P, 1])
        warm = sb("warm", [P, 1])
        hidden = sb("hidden", [P, 2, 2, 2, S])
        gate, act = hidden[:, 0], hidden[:, 1]
        act_hi = sb("act_hi", [P, 2, 2, S], F32R)
        act_lo = sb("act_lo", [P, 2, 2, S], F32R)
        ident = sb("ident", [P, P])
        rope = sb("rope", [P, 4, S])
        arena = sb("arena", [P, 20672])

        psum = ctx.enter_context(nc.psum_tensor("psum", [P, 8, 512], F32))
        bank = [psum[:, i, :] for i in range(8)]

        panel_loaded = [sem(f"panel_loaded{i}") for i in range(SLOTS)]
        hi_ready = sem("hi_ready")
        lo_ready = sem("lo_ready")
        panel_done = sem("panel_done")
        x_loaded = sem("x_loaded")
        const_loaded = sem("const_loaded")
        const_set = sem("const_set")
        zeros_set = sem("zeros_set")
        x_ready = sem("x_ready")
        sq_ready = sem("sq_ready")
        sq_added = sem("sq_added")
        ss_ready = sem("ss_ready")
        rms_ready = sem("rms_ready")
        rstd_ready = sem("rstd_ready")
        h_ready = sem("h_ready")
        h_hi_ready = sem("h_hi_ready")
        h_lo_ready = sem("h_lo_ready")
        gate_ready = sem("gate_ready")
        scaled = sem("scaled")
        sums_ready = sem("sums_ready")
        act_ready = sem("act_ready")
        act_hi_ready = sem("act_hi_ready")
        act_lo_ready = sem("act_lo_ready")
        dft_loaded = sem("dft_loaded")
        dft_tok_ready = sem("dft_tok_ready")
        dft_tok_copied = sem("dft_tok_copied")
        dft_ready = sem("dft_ready")
        dft_hi_ready = sem("dft_hi_ready")
        dft_lo_ready = sem("dft_lo_ready")
        s5_loaded = sem("s5_loaded")
        s5_dt_ready = sem("s5_dt_ready")
        s5_prep = sem("s5_prep")
        s5_trig_ready = sem("s5_trig_ready")
        s5_hperm_ready = sem("s5_hperm_ready")
        s5_u_stored = {n: sem(f"s5_u_stored_{n}") for n in ("act", "pool")}
        s5_u_loaded = sem("s5_u_loaded")
        s5_v_part = sem("s5_v_part")
        s5_v_ready = sem("s5_v_ready")
        s5_vt_ready = sem("s5_vt_ready")
        s5_win_ready = sem("s5_win_ready")
        s5_k_ready = sem("s5_k_ready")
        s5_k_copied = sem("s5_k_copied")
        s5_t_ready = sem("s5_t_ready")
        s5_t_copied = sem("s5_t_copied")
        s5_intra_ready = sem("s5_intra_ready")
        s5_intra_copied = sem("s5_intra_copied")
        s5_in_ready = sem("s5_in_ready")
        s5_in_copied = sem("s5_in_copied")
        s5_step = sem("s5_step")
        s5_w_part = sem("s5_w_part")
        s5_w_ready = sem("s5_w_ready")
        s5_out_ready = sem("s5_out_ready")
        s5_y_ready = sem("s5_y_ready")
        s5_y_stored = {n: sem(f"s5_y_stored_{n}") for n in ("act0", "act1", "pool1")}
        s5_y_loaded = [sem(f"s5_y_loaded{i}") for i in range(2)]
        s5_cbd_ready = sem("s5_cbd_ready")
        s5_zbd_ready = sem("s5_zbd_ready")
        s5_wp_part = sem("s5_wp_part")
        s5_wp_ready = sem("s5_wp_ready")
        s5_skip_ready = sem("s5_skip_ready")
        s5_gelu_ready = sem("s5_gelu_ready")
        s5_g_hi_ready = sem("s5_g_hi_ready")
        s5_g_lo_ready = sem("s5_g_lo_ready")
        glu_sig_ready = sem("glu_sig_ready")
        glu_mul_ready = sem("glu_mul_ready")
        e_loaded = sem("e_loaded")
        e_ready = sem("e_ready")
        e_masked = sem("e_masked")
        e_stored = sem("e_stored")
        qk_sq_ready = sem("qk_sq_ready")
        qk_ss_ready = sem("qk_ss_ready")
        qk_rms_ready = sem("qk_rms_ready")
        qk_rstd_ready = sem("qk_rstd_ready")
        qk_copied = sem("qk_copied")
        qk_ready = sem("qk_ready")
        v_copied = sem("v_copied")
        bias_loaded = [sem(f"bias_loaded{i}") for i in range(3)]
        sc_ready = sem("sc_ready")
        sc_biased = sem("sc_biased")
        max_ready = sem("max_ready")
        neg_ready = sem("neg_ready")
        p_ready = sem("p_ready")
        rden_ready = sem("rden_ready")
        p_scaled = sem("p_scaled")
        pt_ready = sem("pt_ready")
        pt_copied = sem("pt_copied")
        o_ready = sem("o_ready")
        o_copied = sem("o_copied")
        o_hi_ready = sem("o_hi_ready")
        o_lo_ready = sem("o_lo_ready")
        pos_loaded = sem("pos_loaded")
        rope_step = sem("rope_step")
        rope_angle = sem("rope_angle")
        rope_sin = sem("rope_sin")
        rope_squared = sem("rope_squared")
        rope_ready = sem("rope_ready")
        mix_loaded = sem("mix_loaded")
        mix_copied = sem("mix_copied")
        conv_first = sem("conv_first")
        conv_ready = sem("conv_ready")
        conv_act = sem("conv_act")
        dt_exp_ready = sem("dt_exp_ready")
        dt_arg_ready = sem("dt_arg_ready")
        small_set = sem("small_set")
        small_ready = sem("small_ready")
        tok_ready = sem("tok_ready")
        tok_copied = sem("tok_copied")
        xt_ready = sem("xt_ready")
        xt_copied = sem("xt_copied")
        cb_ready = sem("cb_ready")
        cb_copied = sem("cb_copied")
        cs_ready = sem("cs_ready")
        decay_arg = sem("decay_arg")
        decay_ready = sem("decay_ready")
        decay_used = sem("decay_used")
        yp_ready = sem("yp_ready")
        y_raw = sem("y_raw")
        y_gated = sem("y_gated")
        ysq_ready = sem("ysq_ready")
        yss_ready = sem("yss_ready")
        yrms_ready = sem("yrms_ready")
        y_normed = sem("y_normed")
        y_hi_ready = sem("y_hi_ready")
        y_lo_ready = sem("y_lo_ready")
        rot_ready = sem("rot_ready")
        rope_used = sem("rope_used")
        rope_done = sem("rope_done")
        halves_swapped = sem("halves_swapped")
        turn_step = sem("turn_step")
        heads_turned = sem("heads_turned")
        cs_hi_ready = sem("cs_hi_ready")
        cs_lo_ready = sem("cs_lo_ready")
        idx_ready = sem("idx_ready")
        relu_ready = sem("relu_ready")
        idx_added = sem("idx_added")
        sel_ready = sem("sel_ready")
        att_sc_ready = sem("att_sc_ready")
        att_biased = sem("att_biased")
        att_neg = sem("att_neg")
        att_p_ready = sem("att_p_ready")
        att_scaled = sem("att_scaled")
        att_pt_ready = sem("att_pt_ready")
        att_pt_copied = sem("att_pt_copied")
        att_o_ready = sem("att_o_ready")
        att_o_copied = sem("att_o_copied")
        att_hi_ready = sem("att_hi_ready")
        att_lo_ready = sem("att_lo_ready")
        mix_step = sem("mix_step")
        stored = sem("stored")

        block = ctx.enter_context(nc.Block())

        y_of = [bank[4 + o // 2][:, (o % 2) * S:(o % 2 + 1) * S] for o in range(KT)]

        SUMS_BANK = {True: 3, False: 4}

        def hidden_panel(n0, c):
            return n0 if c == 0 else n0 + 2 + 3 * (c - 1)

        dft_ch = arena[:, 0:S]
        dft_sq = arena[:, S:S + 2 * 2 * S].rearrange("p (t f s) -> p t f s", t=2, f=2)
        dft_tok = arena[:, 5 * S:5 * S + 2 * 2 * S].rearrange("p (b t n) -> p b t n", b=2, t=2)

        NC = 8

        class s5:
            at = 0

            @classmethod
            def take(cls, n):
                cls.at += n
                return arena[:, cls.at - n:cls.at]

        s5.z = s5.take(2 * S5_G * S5_C).rearrange("p (r c k) -> p r c k", r=2, c=S5_G)
        s5.hperm = s5.z[:, 0].rearrange("p c k -> p (c k)").rearrange("p (f t c) -> p f t c", f=KT, t=S5_T)
        u_flat = s5.take(S5_G * S5_C)
        s5.u = u_flat.rearrange("p (g c) -> p g c", g=S5_G)
        s5.buf = [s5.take(2 * NC * P).rearrange("p (r c m) -> p r c m", r=2, c=NC) for _ in range(2)]
        win_flat = s5.take(2 * NC * P)
        s5.win = win_flat.rearrange("p (m q) -> p m q", m=2 * NC)
        b_flat = s5.take(2 * S5_G * S5_P)
        s5.b = b_flat.rearrange("p (r c m) -> p r c m", r=2, c=S5_G)
        s5.c = s5.take(2 * S5_G * S5_P).rearrange("p (r c m) -> p r c m", r=2, c=S5_G)
        s5.pow = s5.take(2 * (S5_T + 1) * S5_G).rearrange("p (r k c) -> p r k c", r=2, k=S5_T + 1)
        tmp_flat = s5.take(2 * NC * P)
        s5.tmp = tmp_flat[:, NC * P:].rearrange("p (r c m) -> p r c m", r=2, c=NC // 2)
        LAGS = 2 * S5_T - 1
        s5.kc = s5.take(LAGS * S5_P)
        s5.tc = rope[:, :, :].rearrange("p r s -> p (r s)").rearrange("p (g i m) -> p g i m", g=KT, i=S5_T)
        s5.rot = s5.take(2 * S5_G).rearrange("p (r c) -> p r c", r=2)
        s5.d = s5.take(KT)
        z_pool, z_dve = slice(0, S5_G // 2), slice(S5_G // 2, S5_G)
        s5.zp = s5.take(2 * S5_G).rearrange("p (i r c) -> p i r c", i=2, r=2)
        s5.back = [s5.take(2 * P)[0:2 * S5_C], s5.take(2 * P)[0:2 * S5_C], rstd[0:2 * S5_C, :]]
        s5_back_ready, s5_back_copied = s5_t_ready, s5_t_copied
        y_flat = hidden[:, :, :, :, :].rearrange("p a b t s -> p (a b t s)")
        s5.y = y_flat.rearrange("p (g c) -> p g c", g=S5_G)
        s5.w = s5.buf + [v.rearrange("p (r c m) -> p r c m", r=2, c=NC) for v in (win_flat, b_flat)]
        s5.wtmp = s5.tc.rearrange("p g i m -> p (g i m)").rearrange("p (r c m) -> p r c m", r=2, c=NC // 2)
        s5.cbd = tmp_flat[:, 0:2 * 2 * NC * 2 * S5_P].rearrange("p (b r c n) -> p b r c n", b=2, r=2, c=NC)
        s5.zbd = u_flat.rearrange("p (b r c n) -> p b r c n", b=2, r=2, c=NC)
        s5.yt = tmp_flat.rearrange("p (f t c) -> p f t c", f=KT, t=S5_T)
        s5.par = win_flat[:, 0:3 * S5_G].rearrange("p (r c) -> p r c", r=3)
        s5.t = [win_flat[:, (3 + i) * S5_G:(4 + i) * S5_G] for i in range(16)]
        assert s5.at <= arena.shape[1], s5.at
        u_dram = nc.dram_tensor("s5_u", (S5_T, S5_P, KT, KT, S5_C), F32, kind="Internal").ap()
        y_dram = nc.dram_tensor("s5_y", (2, KT, S5_P, KT // 2, S5_T, S5_C), F32, kind="Internal").ap()
        Y_POOL = 3
        U_POOL = 3
        W_POOL = (1, 4)

        def s5_table(r, ahead, d, f):
            c0 = f * NC + d * NC // 2
            cols = slice(c0, c0 + NC // 2)
            if d == 0:
                tab = s5.pow[:, r, ahead:ahead + S5_T, cols]
            else:
                tab = s5.pow[:, r, S5_T - 1 + ahead:(ahead - 1 if ahead else None):-1, cols]
            return tab.rearrange("p k c -> p c k").unsqueeze(3).to_broadcast([P, NC // 2, S5_T, S5_P])

        def s5_over_rows(v, d, f):
            c0 = f * NC + d * NC // 2
            return v[:, c0:c0 + NC // 2, :].unsqueeze(2).to_broadcast([P, NC // 2, S5_T, S5_P])

        def s5_part(v, d):
            return v[:, d * NC // 2:(d + 1) * NC // 2, :].rearrange("p c (k m) -> p c k m", k=S5_T)

        def s5_store_u(eng, groups, stored):
            for g in groups:
                eng.dma_start(u_dram[:, :, :, g, :].rearrange("r m f c -> m f r c"),
                              s5.hperm[g * S5_P:(g + 1) * S5_P]).then_inc(stored, 16)

        def s5_store_y(eng, half, rows, stored):
            n = S5_G * S5_C // 2
            for i in rows:
                eng.dma_start(y_dram[half, :, :, :, i, :].rearrange("g m f c -> m f g c"),
                              y_flat[i * S5_P:(i + 1) * S5_P, half * n:(half + 1) * n].rearrange(
                                  "m (f g c) -> m f g c", f=KT // 2, g=KT)).then_inc(stored, 16)

        def s5_load_y(eng, half):
            tiles = slice(half * KT // 2, (half + 1) * KT // 2)
            eng.dma_start(s5.yt[:, tiles].rearrange("p f t c -> p (f t c)"),
                          y_dram[half].rearrange("g m f i c -> (g m) (f i c)")).then_inc(s5_y_loaded[half], 16)

        assert all(d % 2 == 0 for _, d in GROUPS[1:]) and GROUPS[0][1] == 1
        UNITS = 2 * HB
        QK = 2 * NG
        PANELS = 3 * NG
        BLOCKS = HEADS // HB

        def da_bank(u):
            return bank[3] if u >= (BLOCKS - 1) * UNITS and u % 2 else bank[4]

        def da_panels(u):
            hb, s = divmod(u, UNITS)
            if hb + 1 == BLOCKS:
                return []
            more = PANELS - UNITS
            p = (hb + 1) * PANELS
            return list(range(p, p + more + 1)) if s == 0 else [p + more + s]

        def da_panel(p):
            hb, i = divmod(p, PANELS)
            return hb, i, hb * QK + i if i < QK else hb * NG + i - QK
        class da:
            at = 0

            @classmethod
            def take(cls, n):
                cls.at += n
                return arena[:, cls.at - n:cls.at]

        da.qk = da.take(2 * 2 * NG * 2 * S).rearrange("p (b w g m s) -> p b w g m s", b=2, w=2, g=NG, m=2)
        da.v = da.take(2 * NG * 2 * S).rearrange("p (b g m s) -> p b g m s", b=2, g=NG, m=2)
        da.sq = da.take(2 * 2 * S).rearrange("p (b n) -> p b n", b=2)
        da.rs = da.take(2 * 2 * S).rearrange("p (b n) -> p b n", b=2)
        da.rq = da.take(2 * NG * UNITS).rearrange("p (b g m t e) -> p b g m t e", b=2, g=NG, m=2, t=2)
        da.sc = da.take(3 * 2 * S).rearrange("p (b n) -> p b n", b=3)
        da.pt = da.take(2 * 2 * S).rearrange("p (b n) -> p b n", b=2)
        da.bias = da.take(3 * NG * S).rearrange("p (b g k) -> p b g k", b=3, g=NG)
        da.pair_ones = da.take(P)
        da.gain = da.take(2 * NG)
        n_units = HEADS * 2
        da.stat = da.take(4 * n_units).rearrange("p (r u) -> p r u", r=4)
        e_at, e_w = 9 * S, 2 * S
        da.rel = arena[0:BUCKETS, e_at:e_at + NG * HEADS]
        e_at += NG * HEADS
        da.onehot = arena[0:BUCKETS, e_at:e_at + e_w]
        da.mask = arena[0:NG * HEADS, e_at + e_w:e_at + 2 * e_w]
        da.e = arena[0:NG * HEADS, e_at + 2 * e_w:e_at + 3 * e_w]
        assert e_at + 3 * e_w <= 4096
        e_dram = nc.dram_tensor("bias_by_distance", (NG * HEADS, 2 * S), F32, kind="Internal").ap()

        class mx:
            at = 0

            @classmethod
            def take(cls, n):
                cls.at += n
                assert cls.at <= arena.shape[1], cls.at
                return arena[:, cls.at - n:cls.at]

        mx.q = mx.take(ATT_H * S).rearrange("p (h s) -> p h s", h=ATT_H)
        mx.k = mx.take(ATT_H * S).rearrange("p (h s) -> p h s", h=ATT_H)
        v_flat = mx.take(2 * D)
        mx.v = v_flat.rearrange("p (t n) -> p t n", t=2)
        mx.dt = [v_flat[0:SSD_H, i * S:(i + 1) * S] for i in range(8)]
        qi_at = mx.at
        mx.qi = mx.take(4 * S).rearrange("p (h s) -> p h s", h=4)
        mx.ki = mx.take(S)
        mx.small = mx.take(S)
        mx.tok = mx.take(2 * P).rearrange("p (t n) -> p t n", t=2)
        mx.tri = mx.take(2 * S).rearrange("p (t l) -> p t l", t=2)
        mx.causal = mx.take(2 * S).rearrange("p (t k) -> p t k", t=2)
        mx.turn_i = mx.take(P)
        mx.col = mx.take(CONV_T * (CONV + 1) + KT + KT + 3)
        mx.convw = mx.col[:, 0:CONV_T * CONV].rearrange("p (c k) -> p c k", c=CONV_T)
        mx.convb = mx.col[:, CONV_T * CONV:CONV_T * (CONV + 1)]
        mx.dskip = mx.col[:, CONV_T * (CONV + 1):CONV_T * (CONV + 1) + KT]
        mx.ygain = mx.col[:, CONV_T * (CONV + 1) + KT:CONV_T * (CONV + 1) + 2 * KT]
        mx.dtb = mx.col[0:SSD_H, CONV_T * (CONV + 1) + 2 * KT:][:, 0:1]
        mx.alog = mx.col[0:SSD_H, CONV_T * (CONV + 1) + 2 * KT:][:, 1:2]
        mx.wi = mx.take(2 * IDX_H).rearrange("p (t h) -> p t h", t=2)
        mx.z = mx.take(KT * S).rearrange("p (c s) -> p c s", c=KT)
        raw_at = mx.at
        mx.raw = mx.take(CONV_T * (S + CONV - 1)).rearrange("p (c s) -> p c s", c=CONV_T)
        mx.conv = mx.take(CONV_T * S).rearrange("p (c s) -> p c s", c=CONV_T)
        mx.cb = mx.take(SSD_G * 2 * S).rearrange("p (g t l) -> p g t l", g=SSD_G, t=2)
        mx.dec = mx.take(2 * 2 * S).rearrange("p (b t l) -> p b t l", b=2, t=2)
        mx.m = mx.take(2 * 2 * S).rearrange("p (b t l) -> p b t l", b=2, t=2)
        mx.xt = hidden[:, :, :, :, :].rearrange("p a b t s -> p (a b t s)").rearrange("p (t n) -> p t n", t=2)
        mx.y = h
        mx.top8 = mx.take(2 * 8).rearrange("p (t s) -> p t s", t=2)
        mx.relu = mx.y
        mx.score = mx.z[:, 6:8]
        mx.rot = mx.xt.rearrange("p t n -> p (t n)").rearrange("p (b n) -> p b n", b=4)
        cs_hi, cs_lo = act_hi[0:SSD_H, 0, 0], act_lo[0:SSD_H, 0, 0]
        pick_head = act_hi[0:SSD_H, 1, 0, 0:SSD_H]
        mx.sel = mx.causal
        mx.at = qi_at
        mx.sc = mx.take(3 * S).rearrange("p (b s) -> p b s", b=3)
        mx.stat = mx.take(4 * 2 * ATT_H).rearrange("p (r u) -> p r u", r=4)
        assert mx.at <= qi_at + 4 * S
        mx.swap = arena[0:ROPE_D, raw_at:raw_at + 4 * 2 * S].rearrange("p (b h s) -> p b h s", b=4, h=2)
        mx.at = raw_at
        mx.yatt = mx.take(KT * S).rearrange("p (c s) -> p c s", c=KT)
        mx.pt = mx.take(2 * S).rearrange("p (b s) -> p b s", b=2)
        assert mx.at <= raw_at + CONV_T * (S + CONV - 1)
        mx.rms = mx.dec[:, 0]
        MISC, QI, XBC, Q, K_, Z, V, OUT_SSD, OUT_ATT, MIX_END = np.cumsum([0, 1, 2, 6, 4, 4, 4, 4, 4, 4]).tolist()
        SSD_0 = Q + 3
        UNITS_AFTER = {Z + 3: (0,), V: (1, 2), V + 1: (3, 4), V + 2: (5, 6), V + 3: (7, 8), OUT_SSD: (9, 10),
                       OUT_SSD + 1: (11, 12), OUT_SSD + 2: (13, 14), OUT_SSD + 3: (15,)}
        ROTS = 3
        RELUS = 8

        def ssd_out_tile(c):
            return (act_hi[:, c // 2, c % 2], act_lo[:, c // 2, c % 2]) if c < 4 else (h_hi[:, c - 4], h_lo[:, c - 4])

        def att_out_tile(c):
            return (h_hi[:, 4 + c], h_lo[:, 4 + c]) if c < 4 else (act_hi[:, c // 2 - 2, c % 2], act_lo[:, c // 2 - 2, c % 2])

        def out_pair(parts, of_att, b):
            in_h, in_act = parts
            if of_att:
                return in_h[:, 4 + 2 * b:6 + 2 * b] if b < 2 else in_act[:, b - 2]
            return in_act[:, b] if b < 2 else in_h[:, 2 * b - 4:2 * b - 2]

        rp_flat = arena[:, da.at:da.at + 7 * S]
        rp_pos = rp_flat[:, 0:S].bitcast(mybir.dt.int32)
        rp_freq = rp_flat[:, S:S + 2]
        rp_f = rp_flat[:, 2 * S - 128:3 * S - 128]
        rp_ang = rp_flat[:, 3 * S:5 * S].rearrange("p (r s) -> p r s", r=2)
        rp_n = rp_flat[:, 5 * S:7 * S].rearrange("p (r s) -> p r s", r=2)

        @block.sync
        def _(sp):
            sp.dma_start(x[:, :, :], A["x"].rearrange("(c p) t -> p c t", p=P)).then_inc(x_loaded, 16)
            sp.dma_start(gains[:, :], A["gains"]).then_inc(const_loaded, 16)
            sp.dma_start(ident[:, :], A["ident"]).then_inc(const_loaded, 16)
            sp.dma_start(s5.par, A["s5_lam"].rearrange("p (r c) -> p r c", r=3)).then_inc(const_loaded, 16)
            for n in range(SLOTS):
                sp.dma_start(raw[:, n, :], A["panels"][n]).then_inc(panel_loaded[n], 16)
            for dst, name in ((s5.b, "s5_b"), (s5.c, "s5_c")):
                sp.dma_start(dst, A[name].rearrange("p (r c m) -> p r c m", r=2, c=S5_G)).then_inc(s5_loaded, 16)
            sp.dma_start(s5.d, A["s5_d"]).then_inc(s5_loaded, 16)
            rounds = (n_panels + 1 - SLOTS) // SLOTS
            with sp.Fori(0, rounds) as i:
                for k in range(SLOTS):
                    sp.wait_ge(lo_ready, i * SLOTS + k + 1)
                    sp.dma_start(raw[:, k, :], A["panels"][bass.ds(i * SLOTS + (SLOTS + k), 1), :, :]
                                 .rearrange("o p n -> p (o n)")).then_inc(panel_loaded[k], 16)
            for n in range(SLOTS * (rounds + 1), n_panels + 1):
                sp.wait_ge(lo_ready, n - SLOTS + 1)
                sp.dma_start(raw[:, n % SLOTS, :], A["panels"][n]).then_inc(panel_loaded[n % SLOTS], 16)
            for b in range(4):
                sp.wait_ge(h_ready, 4 * stages[-1]["whole"] + b + 1)
                sp.dma_start(out.rearrange("(c p) t -> p c t", p=P)[:, 2 * b:2 * b + 2],
                             h[:, 2 * b:2 * b + 2, :]).then_inc(stored, 16)
            sp.wait_ge(stored, 4 * 16)

        S5_DEN, S5_ANGLE, S5_PREP = 3, 14, 80

        @block.gpsimd
        def _(pool):
            pool.memset(ones[:, :], 1.0).then_inc(const_set, 1)
            pool.memset(eps[:, :], EPS).then_inc(const_set, 1)
            pool.memset(eps_head[:, :], E * EPS).then_inc(const_set, 1)
            pool.dma_start(da.rel, A["rel_bias"]).then_inc(e_loaded, 16)
            pool.dma_start(da.onehot, A["bucket_onehot"]).then_inc(e_loaded, 16)
            pool.dma_start(da.mask, A["group_mask"]).then_inc(e_loaded, 16)

            def dilated_mixer(st):
                pool.wait_ge(x_ready, st["xr"])
                pool.dma_start(da.pair_ones, A["pair_ones"]).then_inc(e_loaded, 16)
                pool.dma_start(da.gain, A["qk_gain"]).then_inc(e_loaded, 16)
                rope_angles()
                pool.wait_ge(e_stored, 16)
                for u in range(n_units):
                    head, qt = u // 2, u % 2
                    if u >= 3:
                        pool.wait_ge(sc_biased, u - 2)
                    src = bass.AP(e_dram.tensor, head * 2 * S + qt, [[2, P], [HEADS * 2 * S, NG], [1, S]])
                    pool.dma_start(da.bias[:, u % 3], src).then_inc(bias_loaded[u % 3], 16)
                rope_cosines()

            n_prep = 0

            def then(*ins):
                nonlocal n_prep
                for q in ins:
                    q.then_inc(s5_prep, 1)
                    n_prep += 1
                pool.wait_ge(s5_prep, n_prep)

            def s5_prepare():
                tt, ts = pool.tensor_tensor, pool.tensor_scalar
                lre, lim = s5.par[:, 0], s5.par[:, 1]
                dt, are, ang, turns, mag, sn, sh, t0, t1, t2, t3, nre, den, lim2 = s5.t[:14]
                pool.wait_ge(const_loaded, 3 * 16)
                then(tt(den, lre, lre, ALU.mult), tt(lim2, lim, lim, ALU.mult))
                then(tt(den, den, lim2, ALU.add))
                assert n_prep == S5_DEN
                pool.wait_ge(s5_dt_ready, 1)
                then(tt(are, lre, dt, ALU.mult), tt(ang, lim, dt, ALU.mult))
                then(ts(turns, ang, 1 / TWO_PI, ROUND, ALU.mult, ALU.add))
                then(ts(turns, turns, ROUND, None, ALU.subtract))
                for part in (TWO_PI_1, TWO_PI_2, TWO_PI_3):
                    then(ts(t0, turns, part, None, ALU.mult))
                    then(tt(ang, ang, t0, ALU.subtract))
                then(ts(ang, ang, PI_BELOW, -PI_BELOW, ALU.min, ALU.max))
                assert n_prep == S5_ANGLE
                pool.wait_ge(s5_trig_ready, 4)
                p = s5.pow
                then(tt(t0, sh, sh, ALU.mult))
                then(ts(t0, t0, -2.0, 1.0, ALU.mult, ALU.add))
                then(tt(p[:, 0, 1], mag, t0, ALU.mult), tt(p[:, 1, 1], mag, sn, ALU.mult),
                     pool.memset(p[:, 0, 0], 1.0), pool.memset(p[:, 1, 0], 0.0))
                for k in range(2, S5_T + 1):
                    then(tt(t0, p[:, 0, k - 1], p[:, 0, 1], ALU.mult), tt(t1, p[:, 1, k - 1], p[:, 1, 1], ALU.mult),
                         tt(t2, p[:, 0, k - 1], p[:, 1, 1], ALU.mult), tt(t3, p[:, 1, k - 1], p[:, 0, 1], ALU.mult))
                    then(tt(p[:, 0, k], t0, t1, ALU.subtract), tt(p[:, 1, k], t2, t3, ALU.add))
                then(ts(s5.rot[:, 0], p[:, 1, S5_T], -1.0, None, ALU.mult), ts(s5.rot[:, 1], p[:, 1, S5_T], 1.0, None, ALU.mult))
                then(ts(nre, p[:, 0, 1], -1.0, None, ALU.add))
                nim = p[:, 1, 1]
                then(tt(t0, nre, lre, ALU.mult), tt(t1, nim, lim, ALU.mult),
                     tt(t2, nim, lre, ALU.mult), tt(t3, nre, lim, ALU.mult))
                then(tt(mag, t0, t1, ALU.add), tt(sn, t2, t3, ALU.subtract))
                then(tt(mag, mag, den, ALU.mult), tt(sn, sn, den, ALU.mult))
                pool.wait_ge(s5_loaded, 3 * 16)
                full = [P, S5_G, S5_P]
                cre, cim = mag.unsqueeze(2).to_broadcast(full), sn.unsqueeze(2).to_broadcast(full)
                b, tb = s5.b, tmp_flat.rearrange("p (r c m) -> p r c m", r=2, c=S5_G)
                td = win_flat[:, 1024:2048].rearrange("p (c m) -> p c m", c=S5_G)
                then(tt(tb[:, 0], cre, b[:, 0], ALU.mult), tt(tb[:, 1], cim, b[:, 0], ALU.mult),
                     tt(td, cim, b[:, 1], ALU.mult))
                then(tt(b[:, 0], tb[:, 0], td, ALU.subtract))
                then(tt(td, cre, b[:, 1], ALU.mult))
                then(tt(b[:, 1], tb[:, 1], td, ALU.add), ts(s5.c[:, 1], s5.c[:, 1], -1.0, None, ALU.mult))
                assert n_prep == S5_PREP, n_prep

            def rope_angles():
                n = 0

                def then(*ins):
                    nonlocal n
                    for q in ins:
                        q.then_inc(rope_step, 1)
                        n += 1
                    pool.wait_ge(rope_step, n)

                pool.dma_start(rp_pos, A["positions"]).then_inc(pos_loaded, 16)
                pool.dma_start(rp_freq, A["rope_freq"]).then_inc(pos_loaded, 16)
                pool.wait_ge(pos_loaded, 32)
                tt, ts = pool.tensor_tensor, pool.tensor_scalar
                then(pool.tensor_copy(rp_f, rp_pos))
                then(*[ts(rp_ang[:, r], rp_f, rp_freq[:, r:r + 1], None, ALU.mult) for r in range(2)])
                then(ts(rp_n, rp_ang, 1 / TWO_PI, ROUND, ALU.mult, ALU.add))
                then(ts(rp_n, rp_n, ROUND, None, ALU.subtract))
                for part in (TWO_PI_1, TWO_PI_2, TWO_PI_3):
                    then(ts(rope[:, 0:2], rp_n, part, None, ALU.mult))
                    then(tt(rp_ang, rp_ang, rope[:, 0:2], ALU.subtract))
                ts(rp_ang, rp_ang, PI_BELOW, -PI_BELOW, ALU.min, ALU.max).then_inc(rope_angle, 1)

            def rope_cosines():
                pool.wait_ge(rope_sin, 4)
                pool.tensor_tensor(rp_n, rp_ang, rp_ang, ALU.mult).then_inc(rope_squared, 1)
                pool.wait_ge(rope_squared, 1)
                pool.tensor_scalar(rope[:, 0:3:2], rp_n, -2.0, 1.0, ALU.mult, ALU.add).then_inc(rope_ready, 1)

            def mix_loads(st):
                pool.wait_ge(x_ready, st["xr"])
                i = st["i"]
                pool.dma_start(mx.col, A["mix_col"][i]).then_inc(mix_loaded, 16)
                pool.dma_start(mx.tri, A["mask_tri"]).then_inc(mix_loaded, 16)
                pool.dma_start(mx.causal, A["mask_causal"]).then_inc(mix_loaded, 16)
                pool.dma_start(mx.turn_i, A["turn_i"]).then_inc(mix_loaded, 16)
                pool.memset(mx.small, 0.0).then_inc(small_set, 1)
                pool.memset(mx.raw[:, :, 0:CONV - 1], 0.0).then_inc(small_set, 1)

            n_turn = 0

            def turn_heads(st):
                nonlocal n_turn
                i = st["i"]
                pool.wait_ge(rope_ready, 1)
                pool.wait_ge(conv_ready, CONV_T * (i + 1))
                for r in range(KT):
                    part = (mx.q if r < 4 else mx.k)[0:ROPE_D, 2 * (r % 4):2 * (r % 4) + 2, :]
                    swap = mx.swap[:, r % 4]
                    pool.wait_ge(mix_copied, OUT_SSD * i + Q + r + 1)
                    if r >= 4:
                        pool.wait_ge(heads_turned, KT * i + r - 3)
                    for half in range(2):
                        rows = [slice(m * ROPE_D // 2, (m + 1) * ROPE_D // 2) for m in (half, 1 - half)]
                        pool.dma_start(swap[rows[0]], part[rows[1]]).then_inc(halves_swapped, 16)
                    cos, sin = (rope[0:ROPE_D, m, :].unsqueeze(1).to_broadcast([ROPE_D, 2, S]) for m in range(2))
                    pool.wait_ge(halves_swapped, 32 * (KT * i + r + 1))
                    for o, f in ((swap, sin), (part, cos)):
                        pool.tensor_tensor(o, o, f, ALU.mult).then_inc(turn_step, 1)
                        n_turn += 1
                    pool.wait_ge(turn_step, n_turn)
                    pool.tensor_tensor(part, part, swap, ALU.add).then_inc(heads_turned, 1)

            def s5_mixer(st):
                def spread_c(f):
                    if f >= 2:
                        pool.wait_ge(s5_k_ready, f - 1)
                    for r in range(2):
                        for e in range(2):
                            half = slice(e * S5_N, (e + 1) * S5_N)
                            pool.tensor_copy(s5.cbd[half, f % 2, r, :, e * S5_P:(e + 1) * S5_P],
                                             s5.c[half, r, f * NC:(f + 1) * NC, :]).then_inc(s5_cbd_ready, 1)
                    pool.wait_ge(s5_cbd_ready, 1 + 4 * (f + 1))

                pool.memset(s5.cbd, 0.0).then_inc(s5_cbd_ready, 1)
                pool.wait_ge(s5_cbd_ready, 1)
                spread_c(0)
                spread_c(1)
                pool.wait_ge(s5_hperm_ready, KT)
                s5_store_u(pool, range(U_POOL), s5_u_stored["pool"])
                pool.wait_ge(s5_u_stored["pool"], 16 * U_POOL)
                pool.wait_ge(s5_u_stored["act"], 16 * (KT - U_POOL))
                pool.dma_start(s5.u.rearrange("p g c -> p (g c)"), u_dram.rearrange("r m f g c -> (r m) (f g c)")
                               ).then_inc(s5_u_loaded, 16)
                for f in range(2, KT // 2 + 2):
                    spread_c(f)
                pool.wait_ge(s5_in_copied, KT // 2)
                l8, rot = s5.pow[:, 0, S5_T, z_pool].unsqueeze(1).to_broadcast([P, 2, S5_G // 2]), s5.rot[:, :, z_pool]
                for k in range(1, S5_C - 1):
                    z0, z1 = s5.z[:, :, z_pool, k - 1], s5.z[:, :, z_pool, k]
                    then(pool.tensor_tensor(s5.zp[:, 0], z0, l8, ALU.mult),
                         pool.tensor_tensor(s5.zp[:, 1], z0[:, ::-1, :], rot, ALU.mult))
                    then(pool.tensor_tensor(z1, z1, s5.zp[:, 0], ALU.add))
                    then(pool.tensor_tensor(z1, z1, s5.zp[:, 1], ALU.add))
                    if k % (KT - 1) == 0 and KT // 2 + 1 + k // (KT - 1) < KT:
                        spread_c(KT // 2 + 1 + k // (KT - 1))
                pool.wait_ge(s5_intra_ready, KT)
                pool.memset(s5.zbd, 0.0).then_inc(s5_cbd_ready, 1)
                for n, f in enumerate(W_POOL):
                    if f >= 4:
                        pool.wait_ge(s5_out_ready, f - 3)
                    for d in range(2):
                        tab = [s5_table(r, 1, d, f) for r in range(2)]
                        cc = [s5_over_rows(s5.c[:, r], d, f) for r in range(2)]
                        w, tmp = s5.w[f % 4], s5.wtmp.rearrange("p r c (k m) -> p r c k m", k=S5_T)
                        w_re, w_im = s5_part(w[:, 0], d), s5_part(w[:, 1], d)
                        pool.tensor_tensor(w_re, tab[0], cc[0], ALU.mult)
                        pool.tensor_tensor(w_im, tab[0], cc[1], ALU.mult)
                        pool.tensor_tensor(tmp[:, 0], tab[1], cc[1], ALU.mult)
                        pool.tensor_tensor(tmp[:, 1], tab[1], cc[0], ALU.mult).then_inc(s5_wp_part, 1)
                        pool.wait_ge(s5_wp_part, 3 * n + 2 * d + 1)
                        pool.tensor_tensor(w_re, w_re, tmp[:, 0], ALU.add)
                        ins = pool.tensor_tensor(w_im, w_im, tmp[:, 1], ALU.subtract)
                        ins.then_inc(s5_wp_part if d == 0 else s5_wp_ready, 1)
                        if d == 0:
                            pool.wait_ge(s5_wp_part, 3 * n + 2)
                    pool.wait_ge(s5_wp_ready, n + 1)
                pool.wait_ge(s5_y_ready, KT)
                s5_store_y(pool, 1, range(Y_POOL), s5_y_stored["pool1"])
                pool.wait_ge(s5_y_stored["act1"], 16 * (S5_T - Y_POOL))
                pool.wait_ge(s5_y_stored["pool1"], 16 * Y_POOL)
                s5_load_y(pool, 1)

            s5_prepare()
            pool.wait_ge(e_masked, 1)
            pool.dma_start(e_dram, da.e).then_inc(e_stored, 16)
            for st in stages:
                if st["kind"] == "s5":
                    s5_mixer(st)
                if st["kind"] == "dilated":
                    dilated_mixer(st)
                if st["kind"] == "mix":
                    mix_loads(st)
                    turn_heads(st)

        @block.scalar
        def _(a):
            def split(n, i=None, per=0):
                def at(v, m=1):
                    return v if i is None else i * (m * per) + v
                if i is None and n > n_panels:
                    return
                s = n % SLOTS
                a.wait_ge(panel_loaded[s], 16 * (n // SLOTS + 1) if i is None
                          else i * (16 * per // SLOTS) + 16 * (n // SLOTS + 1))
                if n >= SLOTS:
                    a.wait_ge(panel_done, at(n - SLOTS + 1))
                a.activation(w_hi[:, s, :], raw[:, s, :], ACT.Copy).then_inc(hi_ready, 1)

            def load_dft():
                a.dma_start(dft_ch, A["dft_ch"]).then_inc(dft_loaded, 16)
                a.dma_start(dft_sq, A["dft_sq"].rearrange("(t p) (f s) -> p t f s", p=P, f=2)).then_inc(dft_loaded, 16)

            def norm(st):
                n = st["norm"]
                a.wait_ge(x_loaded, 16)
                if st["late"]:
                    a.wait_ge(const_loaded, 48)
                    a.wait_ge(panel_done, st["n0"] - st["after_ffn"])
                    for b in range(4):
                        a.wait_ge(x_ready, st["xr"] - 3 + b)
                        for c in (2 * b, 2 * b + 1):
                            ins = a.activation(h_hi[:, c], x[:, c], ACT.Copy, scale=gains[:, n * KT + c:n * KT + c + 1])
                        ins.then_inc(h_hi_ready, 1)
                for b in range(4):
                    if st["xr"]:
                        a.wait_ge(x_ready, st["xr"] - 3 + b)
                    a.activation(h[:, 2 * b:2 * b + 2, :], x[:, 2 * b:2 * b + 2, :],
                                 ACT.Square).then_inc(sq_ready, 1)
                if st["late"]:
                    split(st["n0"] + 2)
                if st["dft"] and st["xr"]:
                    load_dft()
                a.wait_ge(const_set, 3)
                a.activation(warm[:, :], eps[:, :], ACT.Sqrt)
                a.wait_ge(ss_ready, n + 1)
                a.activation(rstd[:, :], bank[SUMS_BANK[st["late"]]][:, 0:S], ACT.Sqrt, bias=eps[:, 0:1],
                             scale=1.0 / D).then_inc(rms_ready, 1)
                if st["late"]:
                    return
                if st["split"]:
                    for b in range(4):
                        a.wait_ge(h_ready, 4 * st["whole"] + b + 1)
                        a.activation(h_hi[:, 2 * b:2 * b + 2, :], h[:, 2 * b:2 * b + 2, :],
                                     ACT.Copy).then_inc(h_hi_ready, 1)

            def ffn(st):
                n0, f = st["n0"], st["ffn"]

                def silu(c, p, i=None):
                    def at(v, per):
                        return v if i is None else i * per + v
                    a.wait_ge(scaled, at(2 * (f * FFC + c) + 1, 4))
                    a.activation(gate[:, c % 2], gate[:, c % 2], ACT.Silu).then_inc(gate_ready, 1)

                split(n0 + 3)
                silu(0, n0)
                with a.Fori(0, (FFC - 1) // 2) as i:
                    for c in (1, 2):
                        p = hidden_panel(n0, c)
                        split(p + 2, i, 6)
                        split(p + 3, i, 6)
                        silu(c, p, i)
                        split(p + 4, i, 6)
                split(n0 + 34)

            def fourier(st):
                f = st["fourier"] = sum(q["kind"] == "fourier" for q in stages[:stages.index(st)])
                for g in range(KT):
                    k = f * KT + g
                    a.wait_ge(dft_tok_ready, k + 1)
                    a.activation(dft_tok[:, g % 2], bank[4 + g % 2][:, :].rearrange("p (t n) -> p t n", t=2),
                                 ACT.Copy).then_inc(dft_tok_copied, 1)
                    if g:
                        a.wait_ge(dft_ready, k)
                        a.activation(h_hi[:, g - 1], bank[6 + (g - 1) % 2][:, 0:S], ACT.Copy).then_inc(dft_hi_ready, 1)
                a.wait_ge(dft_ready, f * KT + KT)
                a.activation(h_hi[:, KT - 1], bank[6 + (KT - 1) % 2][:, 0:S], ACT.Copy).then_inc(dft_hi_ready, 1)
                for p in range(4):
                    split(st["n0"] + p + 2)

            def s5_prepare():
                dt, are, ang, turns, mag, sn, sh = s5.t[:7]
                a.wait_ge(s5_prep, S5_ANGLE)
                a.activation(mag, are, ACT.Exp).then_inc(s5_trig_ready, 1)
                a.activation(sn, ang, ACT.Sin).then_inc(s5_trig_ready, 1)
                a.activation(sh, ang, ACT.Sin, scale=0.5).then_inc(s5_trig_ready, 1)

            def s5_mixer(st):
                hn = st["hn"]
                for f in range(KT):
                    a.wait_ge(h_ready, 4 * st["whole"] + f // 2 + 1)
                    a.activation(s5.hperm[:, f], h[:, f, :].rearrange("p (c r) -> p r c", r=S5_T)[:, ::-1, :],
                                 ACT.Copy).then_inc(s5_hperm_ready, 1)
                a.wait_ge(s5_hperm_ready, KT)
                s5_store_u(a, range(U_POOL, KT), s5_u_stored["act"])

                def factors(f):
                    for q in range(4):
                        a.wait_ge(s5_vt_ready, 4 * f + q + 1)
                        if f and q == 0:
                            a.wait_ge(s5_in_ready, f)
                        a.activation(s5.win[:, 4 * q:4 * q + 4, :], bank[4 + q % 2][:, :].rearrange(
                            "p (m q) -> p m q", m=4), ACT.Copy).then_inc(s5_win_ready, 1)
                    a.wait_ge(s5_k_ready, f + 1)
                    a.activation(s5.kc, bank[0][:, 0:LAGS * S5_P], ACT.Copy).then_inc(s5_k_copied, 1)

                factors(0)
                for f in range(KT):
                    a.wait_ge(s5_t_ready, f + 1)
                    for q in range(2):
                        a.activation(s5.tc[:, :, 4 * q:4 * q + 4, :].rearrange("p g i m -> p i g m"), bank[7 - q][:, :].rearrange(
                            "p (i g m) -> p i g m", i=4, g=KT), ACT.Copy).then_inc(s5_t_copied, 1)
                    a.wait_ge(s5_in_ready, f + 1)
                    a.activation(s5.z[:, :, f * NC:(f + 1) * NC, :], bank[2 + f % 2][:, :].rearrange(
                        "p (r c k) -> p r c k", r=2, c=NC), ACT.Copy).then_inc(s5_in_copied, 1)
                    if f + 1 < KT:
                        factors(f + 1)
                    a.wait_ge(s5_intra_ready, f + 1)
                    a.activation(s5.y[:, f * KT:(f + 1) * KT, :], bank[1][:, 0:S].rearrange(
                        "p (g c) -> p g c", g=KT), ACT.Copy).then_inc(s5_intra_copied, 1)
                def spread_z(f):
                    if f >= 2:
                        a.wait_ge(s5_out_ready, f - 1)
                    for d in range(2):
                        for e in range(2):
                            half = slice(e * S5_N, (e + 1) * S5_N)
                            z = s5.z[half, :, f * NC + 4 * d:f * NC + 4 * d + 4, :]
                            at = e * S5_C + 1 - d
                            a.activation(s5.zbd[half, f % 2, :, 4 * d:4 * d + 4, at:at + S5_C - 1],
                                         z[:, :, :, 0:S5_C - 1] if d == 0 else z[:, :, :, S5_C - 2::-1],
                                         ACT.Copy).then_inc(s5_zbd_ready, 1)

                a.wait_ge(s5_cbd_ready, 2 + 4 * KT)
                a.wait_ge(s5_prep, S5_PREP + 4 * (S5_C - 2))
                spread_z(0)
                spread_z(1)
                for f in range(KT):
                    for n in (2 * f, 2 * f + 1):
                        a.wait_ge(s5_back_ready, KT + n + 1)
                        if n >= 3:
                            a.wait_ge(s5_out_ready, (n - 3) // 2 + 1)
                        a.activation(s5.back[n % 3], bank[2 + n % 2][0:2 * S5_C, 0:2 * P], ACT.Copy).then_inc(s5_back_copied, 1)
                    if f + 2 < KT:
                        if f + 2 == KT // 2:
                            a.wait_ge(s5_step, 4 * (S5_C - 2))
                        spread_z(f + 2)
                    if f in (KT - 3, KT - 2):
                        a.wait_ge(s5_y_ready, KT // 2)
                        s5_store_y(a, 0, range(S5_T // 2) if f == KT - 3 else range(S5_T // 2, S5_T), s5_y_stored["act0"])
                a.wait_ge(s5_y_stored["act0"], 16 * S5_T)
                s5_load_y(a, 0)
                a.wait_ge(s5_y_ready, KT)
                s5_store_y(a, 1, range(Y_POOL, S5_T), s5_y_stored["act1"])
                a.activation(warm[:, :], eps[:, :], ACT.Gelu_apprx_tanh)
                for f in range(KT):
                    a.wait_ge(s5_skip_ready, f + 1)
                    a.activation(h[:, f], h[:, f], ACT.Gelu_apprx_tanh).then_inc(s5_gelu_ready, 1)
                    if f % 2:
                        a.wait_ge(s5_gelu_ready, f + 1)
                        a.activation(h_hi[:, f - 1:f + 1, :], h[:, f - 1:f + 1, :], ACT.Copy).then_inc(s5_g_hi_ready, 1)
                for k in range(4):
                    split(st["n0"] + 2 * k + 2)
                    split(st["n0"] + 2 * k + 3)
                    a.wait_ge(panel_done, st["n0"] + 2 * k + 2)
                    if k >= 2:
                        a.wait_ge(glu_mul_ready, k - 1)
                    a.activation(gate[:, k % 2], bank[(2 * k + 1) % PROJ_BANKS][:, :].rearrange("p (t s) -> p t s", t=2),
                                 ACT.Sigmoid).then_inc(glu_sig_ready, 1)

            def dilated_mixer(st):
                n0 = st["n0"]

                def evacuate(p):
                    hb, i, c = da_panel(p)
                    b = bank[p % 3]
                    a.wait_ge(panel_done, n0 + p + 1)
                    if i < QK:
                        if c >= 2:
                            a.wait_ge(qk_ss_ready, c - 1)
                        a.activation(da.sq[:, c % 2], b[:, :], ACT.Square).then_inc(qk_sq_ready, 1)
                        if hb >= 2:
                            a.wait_ge(sc_ready, UNITS * (hb - 1))
                        g, which = i // 2, i % 2
                        a.activation(da.qk[:, hb % 2, which, g], b[:, :].rearrange("p (m n) -> p m n", m=2), ACT.Copy,
                                     scale=da.gain[:, which * NG + g:which * NG + g + 1]).then_inc(qk_copied, 1)
                    else:
                        if hb >= 2:
                            a.wait_ge(o_ready, UNITS * (hb - 1))
                        a.activation(da.v[:, hb % 2, i - QK], b[:, :].rearrange("p (m n) -> p m n", m=2),
                                     ACT.Copy).then_inc(v_copied, 1)
                    if i % 2 == 0 and 2 <= i <= QK:
                        c, g = hb * QK + i - 2, i // 2 - 1
                        a.wait_ge(qk_ss_ready, c + 2)
                        if hb >= 2:
                            a.wait_ge(sc_biased, UNITS * (hb - 1))
                        a.activation(da.rq[:, hb % 2, g].rearrange("p m t e -> p (m t e)"), bank[3][:, 0:UNITS], ACT.Sqrt,
                                     bias=eps_head[:, 0:1]).then_inc(qk_rms_ready, 1)
                        if c >= 4:
                            a.wait_ge(qk_ready, c - 2)
                        a.activation(da.rs[:, c // 2 % 2], bank[5][:, :], ACT.Sqrt, bias=eps[:, 0:1],
                                     scale=1.0 / E).then_inc(qk_rms_ready, 1)

                def exp(u):
                    a.wait_ge(neg_ready, u + 1)
                    a.activation(da.sc[:, u % 3], da.sc[:, u % 3], ACT.Exp, bias=da.stat[:, 1, u:u + 1],
                                 accum_out=da.stat[:, 2, u:u + 1]).then_inc(p_ready, 1)

                def copy_p(u):
                    a.wait_ge(pt_ready, u + 1)
                    if u >= 2:
                        a.wait_ge(o_ready, u - 1)
                    a.activation(da.pt[:, u % 2], bank[6][:, :], ACT.Copy).then_inc(pt_copied, 1)

                def copy_o(u):
                    head, qt = u // 2, u % 2
                    rows = slice(head % 2 * E, head % 2 * E + E)
                    a.wait_ge(o_ready, u + 1)
                    a.activation(h[rows, head // 2, qt::2], bank[7][rows, 0:P], ACT.Copy).then_inc(o_copied, 1)

                def upper(b):
                    a.wait_ge(o_copied, UNITS * (b + 1))
                    a.activation(h_hi[:, 2 * b:2 * b + 2, :], h[:, 2 * b:2 * b + 2, :], ACT.Copy).then_inc(o_hi_ready, 1)

                a.wait_ge(e_loaded, 16 * 5)
                for p in range(PANELS):
                    split(n0 + p + 2)
                    evacuate(p)
                last = n_units - UNITS
                for u in range(last):
                    panels = da_panels(u)
                    if u:
                        copy_p(u - 1)
                    split(n0 + panels[0] + 2)
                    exp(u)
                    evacuate(panels[0])
                    for p in panels[1:]:
                        split(n0 + p + 2)
                        evacuate(p)
                    if u:
                        copy_o(u - 1)
                copy_p(last - 1)
                split(n0 + 38)
                exp(last)
                copy_o(last - 1)
                for b in range(BLOCKS - 1):
                    upper(b)
                for u in range(last + 1, n_units + 2):
                    if u < n_units:
                        exp(u)
                    if u - 1 < n_units:
                        copy_p(u - 1)
                    if u - 2 >= last:
                        copy_o(u - 2)
                upper(BLOCKS - 1)
                rope_sines()
                for p in range(37, 40):
                    split(n0 + p + 2)

            def rope_sines():
                a.wait_ge(rope_angle, 1)
                for r in range(2):
                    a.activation(rope[:, 2 * r + 1], rp_ang[:, r], ACT.Sin).then_inc(rope_sin, 1)
                a.wait_ge(rope_sin, 2)
                for r in range(2):
                    a.activation(rp_ang[:, r], rp_ang[:, r], ACT.Sin, scale=0.5).then_inc(rope_sin, 1)

            def mixer(st):
                i, n0 = st["i"], st["n0"]
                units = 2 * ATT_H

                def landed(p):
                    a.wait_ge(panel_done, n0 + p + 1)
                    return bank[p % PROJ_BANKS]

                def halves(b):
                    return b[:, :].rearrange("p (m s) -> p m s", m=2)

                def keep(dst, p, func=ACT.Copy):
                    a.activation(dst, halves(landed(p)), func).then_inc(mix_copied, 1)

                def conv_silu(pair):
                    for c in (2 * pair, 2 * pair + 1):
                        a.wait_ge(conv_ready, CONV_T * i + c + 1)
                        a.activation(mx.conv[:, c], mx.conv[:, c], ACT.Silu).then_inc(conv_act, 1)

                def relus(us):
                    for u in us:
                        keys = (u // IDX_H + 1) * P
                        n = 2 * IDX_H * i + u
                        a.wait_ge(idx_ready, n + 1)
                        if u >= RELUS:
                            a.wait_ge(idx_added, n - RELUS + 1)
                        a.activation(mx.relu[:, u % RELUS, 0:keys], bank[4 + u % 4][:, 0:keys], ACT.Relu,
                                     scale=E ** -0.5).then_inc(relu_ready, 1)

                def copy_xt(qs):
                    for q in qs:
                        a.wait_ge(xt_ready, 4 * i + q + 1)
                        a.activation(mx.xt[:, :, q * 2 * P:(q + 1) * 2 * P], bank[5 + q % 2][:, :].rearrange(
                            "p (t n) -> p t n", t=2), ACT.Copy).then_inc(xt_copied, 1)

                def exp_unit(u):
                    keys = (u % 2 + 1) * P
                    a.wait_ge(att_neg, units * i + u + 1)
                    a.activation(mx.sc[:, u % 3, 0:keys], mx.sc[:, u % 3, 0:keys], ACT.Exp, bias=mx.stat[:, 1, u:u + 1],
                                 accum_out=mx.stat[:, 2, u:u + 1]).then_inc(att_p_ready, 1)

                def copy_p(u):
                    n, keys = units * i + u, (u % 2 + 1) * P
                    a.wait_ge(att_pt_ready, n + 1)
                    if u >= 2:
                        a.wait_ge(att_o_ready, n - 1)
                    a.activation(mx.pt[:, u % 2, 0:keys], bank[6][:, 0:keys], ACT.Copy).then_inc(att_pt_copied, 1)

                def copy_o(u):
                    head, qt = u // 2, u % 2
                    a.wait_ge(att_o_ready, units * i + u + 1)
                    a.activation(mx.yatt[:, head, qt * P:(qt + 1) * P], bank[7][:, u % 2 * P:(u % 2 + 1) * P],
                                 ACT.Copy).then_inc(att_o_copied, 1)


                def upper_ssd(bs):
                    for b in bs:
                        a.wait_ge(y_normed, 4 * i + b + 1)
                        a.activation(out_pair((h_hi, act_hi), False, b), mx.y[:, 2 * b:2 * b + 2, :],
                                     ACT.Copy).then_inc(y_hi_ready, 1)

                def upper_att(bs):
                    for b in bs:
                        a.wait_ge(att_o_copied, units * i + 4 * (b + 1))
                        a.activation(out_pair((h_hi, act_hi), True, b), mx.yatt[:, 2 * b:2 * b + 2, :],
                                     ACT.Copy).then_inc(att_hi_ready, 1)

                split(n0 + 2)
                a.wait_ge(small_set, 2 * (i + 1))
                a.wait_ge(mix_loaded, 64 * (i + 1))
                a.activation(mx.alog, mx.alog, ACT.Exp).then_inc(dt_exp_ready, 1)
                b = landed(MISC)
                a.activation(mx.ki, b[:, 0:S], ACT.Copy)
                a.activation(mx.small[32:32 + IDX_H, :], b[32:32 + IDX_H, S:2 * S], ACT.Copy)
                a.activation(mx.dt[0], b[0:SSD_H, S:2 * S], ACT.Copy).then_inc(mix_copied, 1)
                a.wait_ge(dt_arg_ready, i + 1)
                a.activation(mx.dt[2], mx.dt[1], ACT.Exp).then_inc(dt_exp_ready, 1)
                for p in range(QI, XBC):
                    split(n0 + p + 2)
                    keep(mx.qi[:, 2 * (p - QI):2 * (p - QI) + 2, :], p)
                for p in range(XBC, Q):
                    split(n0 + p + 2)
                    keep(mx.raw[:, 2 * (p - XBC):2 * (p - XBC) + 2, CONV - 1:], p)
                    a.wait_ge(mix_copied, OUT_SSD * i + p + 1)
                    for c in (2 * (p - XBC), 2 * (p - XBC) + 1):
                        a.activation(mx.conv[:, c], mx.raw[:, c, 0:S], ACT.Identity, bias=mx.convb[:, c:c + 1],
                                     scale=mx.convw[:, c, 0:1]).then_inc(conv_first, 1)
                    if p == XBC:
                        a.wait_ge(tok_ready, i + 1)
                        a.activation(mx.tok, bank[7][:, 0:2 * P].rearrange("p (t n) -> p t n", t=2), ACT.Copy).then_inc(tok_copied, 1)
                        a.activation(pick_head, ident[0:SSD_H, 0:SSD_H], ACT.Copy)
                        a.activation(cs_hi, mx.small[0:SSD_H, :], ACT.Copy).then_inc(cs_hi_ready, 1)
                    if p >= Q - 4:
                        relus(range(4 * (p - Q + 4), 4 * (p - Q + 5)))
                    if p > XBC + 1:
                        conv_silu(p - XBC - 2)
                for p in range(Q, Z + 3):
                    split(n0 + p + 2)
                    j = p - SSD_0
                    if j >= 0:
                        for e in range(2):
                            a.wait_ge(decay_arg, SSD_H * i + 2 * j + e + 1)
                            d = mx.dec[:, e]
                            a.activation(d[:, 0], d[:, 0], ACT.Exp)
                            a.activation(d[:, 1, P:], d[:, 1, P:], ACT.Exp).then_inc(decay_ready, 1)
                    if p < Z:
                        keep((mx.q if p < K_ else mx.k)[:, 2 * (p - Q) % KT:2 * (p - Q) % KT + 2, :], p)
                    else:
                        if p == Z:
                            a.wait_ge(idx_added, 2 * IDX_H * (i + 1))
                        keep(mx.z[:, 2 * (p - Z):2 * (p - Z) + 2, :], p, ACT.Silu)
                    if p == Q:
                        conv_silu(4)
                        copy_xt((0, 1))
                    if p == Q + 1:
                        conv_silu(5)
                        copy_xt((2, 3))
                        for g in range(SSD_G):
                            a.wait_ge(cb_ready, 2 * i + g + 1)
                            b = bank[7 if g == 0 else 4]
                            a.activation(mx.cb[:, g, 0], b[:, 0:S], ACT.Copy)
                            a.activation(mx.cb[:, g, 1, P:], b[:, S + P:2 * S], ACT.Copy).then_inc(cb_copied, 1)
                for p in range(Z + 3, OUT_ATT):
                    split(n0 + p + 2)
                    if p == Z + 3:
                        exp_unit(0)
                        exp_unit(1)
                    if p in (Z + 3, V):
                        g = p - Z - 3
                        a.wait_ge(y_gated, 8 * i + 4 * g + 4)
                        a.activation(mx.z[:, 4 * g:4 * g + 4], mx.y[:, 4 * g:4 * g + 4], ACT.Square).then_inc(ysq_ready, 1)
                    if p == V + 1:
                        a.wait_ge(yss_ready, i + 1)
                        a.activation(mx.rms, bank[(Z + 2) % PROJ_BANKS][:, :].rearrange("p (g s) -> p g s", g=2), ACT.Sqrt,
                                     bias=eps[:, 0:1], scale=SSD_G / D).then_inc(yrms_ready, 1)
                    if p == V + 2:
                        upper_ssd((0, 1))
                    if p == OUT_SSD:
                        upper_att((0, 1))
                    if p == Z + 3:
                        a.wait_ge(heads_turned, KT * (i + 1))
                        a.wait_ge(sel_ready, 2 * (i + 1))
                        keep(mx.z[:, 6:8, :], p, ACT.Silu)
                    elif p < OUT_SSD:
                        keep(mx.v[:, :, (p - V) * COLS:(p - V + 1) * COLS], p)
                    for u in UNITS_AFTER[p]:
                        copy_p(u)
                        if u:
                            copy_o(u - 1)
                    if p == V + 3:
                        upper_ssd((2, 3))
                    for u in UNITS_AFTER[p]:
                        if u + 2 < units:
                            exp_unit(u + 2)
                landed(OUT_SSD + 3)
                upper_att((2,))
                copy_o(units - 1)
                upper_att((3,))
                for p in range(OUT_ATT, MIX_END):
                    split(n0 + p + 2)

            load_dft()
            todo = {"norm": norm, "final": norm, "ffn": ffn, "fourier": fourier, "s5": s5_mixer,
                    "dilated": dilated_mixer, "mix": mixer}
            for n, st in enumerate(stages):
                todo[st["kind"]](st)
                if n == 0:
                    a.wait_ge(const_loaded, 3 * 16)
                    a.activation(s5.t[0], s5.par[:, 2], ACT.Exp).then_inc(s5_dt_ready, 1)
                    split(0)
                    split(1)
                    s5_prepare()

        @block.vector
        def _(v):
            def split(n, i=None, per=0):
                if i is None and n > n_panels:
                    return
                v.wait_ge(hi_ready, n + 1 if i is None else i * per + n + 1)
                s = n % SLOTS
                v.tensor_tensor(w_lo[:, s, :], raw[:, s, :], w_hi[:, s, :].bitcast(F32),
                                ALU.subtract).then_inc(lo_ready, 1)

            def norm(st):
                n = st["norm"]
                v.wait_ge(const_loaded, 48)
                if st["late"]:
                    for b in range(4):
                        v.wait_ge(h_hi_ready, 4 * st["hs"] + b + 1)
                        for c in (2 * b, 2 * b + 1):
                            ins = v.scalar_tensor_tensor(h_lo[:, c], x[:, c], gains[:, n * KT + c:n * KT + c + 1],
                                                         h_hi[:, c].bitcast(F32), ALU.mult, ALU.subtract)
                        ins.then_inc(h_lo_ready, 1)
                    v.wait_ge(sq_ready, 4 * n + 4)
                    done = 3 * (n - st["whole"])
                    for m in (4, 2, 1):
                        v.tensor_tensor(h[:, 0:m], h[:, 0:m], h[:, m:2 * m], ALU.add).then_inc(sq_added, 1)
                        done += 1
                        if m > 1:
                            v.wait_ge(sq_added, done)
                    split(st["n0"] + 2)
                v.wait_ge(rms_ready, n + 1)
                v.reciprocal(rstd[:, :], rstd[:, :]).then_inc(rstd_ready, 1)
                v.wait_ge(rstd_ready, n + 1)
                if st["late"]:
                    return
                for b in range(5):
                    if b < 4:
                        for c in (2 * b, 2 * b + 1):
                            ins = v.scalar_tensor_tensor(h[:, c, :], x[:, c, :], gains[:, n * KT + c:n * KT + c + 1],
                                                         rstd[:, :], ALU.mult, ALU.mult)
                        ins.then_inc(h_ready, 1)
                    if b and st["split"]:
                        v.wait_ge(h_hi_ready, 4 * st["hs"] + b)
                        v.tensor_tensor(h_lo[:, 2 * b - 2:2 * b, :], h[:, 2 * b - 2:2 * b, :],
                                        h_hi[:, 2 * b - 2:2 * b, :].bitcast(F32),
                                        ALU.subtract).then_inc(h_lo_ready, 1)

            def ffn(st):
                n0, f = st["n0"], st["ffn"]
                scale = 1.0 if st["i"] < BLOCK1 else 0.5

                rstd_2 = rstd[:, :].unsqueeze(1).to_broadcast([P, 2, S])

                def tiles(b):
                    return bank[b % PROJ_BANKS][:, :].rearrange("p (t s) -> p t s", t=2)

                def scale_gate(c, p, i=None):
                    v.wait_ge(panel_done, p + 1 if i is None else i * 6 + p + 1)
                    v.tensor_tensor(gate[:, c % 2], tiles(2 * c), rstd_2, ALU.mult).then_inc(scaled, 1)

                def hidden(c, p, i=None):
                    def at(val, per):
                        return val if i is None else i * per + val
                    b = c % 2
                    v.wait_ge(panel_done, at(p + 2, 6))
                    v.tensor_tensor(act[:, b], tiles(2 * c + 1), rstd_2, ALU.mult).then_inc(scaled, 1)
                    v.wait_ge(scaled, at(2 * (f * FFC + c) + 2, 4))
                    v.wait_ge(gate_ready, at(f * FFC + c + 1, 2))
                    v.tensor_tensor(act[:, b], gate[:, b], act[:, b], ALU.mult).then_inc(act_ready, 1)
                    v.wait_ge(act_ready, at(f * FFC + c + 1, 2))
                    v.tensor_copy(act_hi[:, b], act[:, b]).then_inc(act_hi_ready, 1)
                    v.wait_ge(act_hi_ready, at(f * FFC + c + 1, 2))
                    v.tensor_tensor(act_lo[:, b], act[:, b], act_hi[:, b].bitcast(F32),
                                    ALU.subtract).then_inc(act_lo_ready, 1)

                scale_gate(0, n0)
                split(n0 + 3)
                if st["s5_follows"]:
                    s5_first()
                hidden(0, n0)
                with v.Fori(0, (FFC - 1) // 2) as i:
                    for c in (1, 2):
                        p = hidden_panel(n0, c)
                        split(p + 2, i, 6)
                        scale_gate(c, p, i)
                        split(p + 3, i, 6)
                        hidden(c, p, i)
                        split(p + 4, i, 6)
                for b in range(4):
                    if b < 3:
                        v.wait_ge(sums_ready, 3 * f + b + 1)
                    else:
                        v.wait_ge(panel_done, n0 + 33)
                    v.scalar_tensor_tensor(x[:, 2 * b:2 * b + 2, :], bank[4 + b][:, :].rearrange(
                        "p (t s) -> p t s", t=2), scale, x[:, 2 * b:2 * b + 2, :],
                        ALU.mult, ALU.add).then_inc(x_ready, 1)
                split(n0 + 34)

            def add_panel(st, k, first=0):
                v.wait_ge(panel_done, st["n0"] + first + k + 1)
                v.tensor_tensor(x[:, 2 * k:2 * k + 2, :], bank[k % PROJ_BANKS][:, :].rearrange(
                    "p (t s) -> p t s", t=2), x[:, 2 * k:2 * k + 2, :], ALU.add).then_inc(x_ready, 1)

            def fourier(st):
                f = st["fourier"]
                for g in range(KT):
                    k = f * KT + g
                    v.wait_ge(dft_hi_ready, k + 1)
                    v.tensor_tensor(h_lo[:, g], bank[6 + g % 2][:, 0:S], h_hi[:, g].bitcast(F32),
                                    ALU.subtract).then_inc(dft_lo_ready, 1)
                for p in range(4):
                    split(st["n0"] + p + 2)
                    add_panel(st, p)

            def s5_prepare():
                den = s5.t[12]
                v.wait_ge(s5_prep, S5_DEN)
                v.reciprocal(den, den).then_inc(s5_trig_ready, 1)

            def s5_product(out_, m, k, f, ahead, sem_part, sem_done, n):
                for d in range(2):
                    tab = [s5_table(r, ahead, d, f) for r in range(2)]
                    mm = [s5_over_rows(m[:, r], d, f) for r in range(2)]
                    re, im = s5_part(out_[:, 0], d), s5_part(out_[:, 1], d)
                    tmp = s5.tmp.rearrange("p r c (k m) -> p r c k m", k=S5_T)
                    v.tensor_tensor(re, tab[0], mm[0], ALU.mult)
                    v.tensor_tensor(im, tab[0], mm[1], ALU.mult)
                    v.tensor_tensor(tmp[:, 0], tab[1], mm[1], ALU.mult)
                    v.tensor_tensor(tmp[:, 1], tab[1], mm[0], ALU.mult).then_inc(sem_part, 1)
                    v.wait_ge(sem_part, 3 * n + 2 * d + 1)
                    v.tensor_tensor(re, re, tmp[:, 0], ALU.subtract if k > 0 else ALU.add)
                    ins = v.tensor_tensor(im, im, tmp[:, 1], ALU.add if k > 0 else ALU.subtract)
                    ins.then_inc(sem_part if d == 0 else sem_done, 1)
                    if d == 0:
                        v.wait_ge(sem_part, 3 * n + 2)

            def s5_first():
                v.wait_ge(s5_prep, S5_PREP)
                s5_product(s5.buf[0], s5.b, 1, 0, 0, s5_v_part, s5_v_ready, 0)

            def s5_mixer(st):
                for f in range(1, KT):
                    if f >= 2:
                        v.wait_ge(s5_k_ready, f - 1)
                    v.wait_ge(s5_v_ready, f)
                    s5_product(s5.buf[f % 2], s5.b, 1, f, 0, s5_v_part, s5_v_ready, f)
                w_dve = [f for f in range(KT) if f not in W_POOL]
                assert w_dve[0] == 0
                v.wait_ge(s5_k_ready, KT - 1)
                v.wait_ge(s5_v_ready, KT)
                s5_product(s5.w[0], s5.c, -1, 0, 1, s5_w_part, s5_w_ready, 0)
                v.wait_ge(s5_in_copied, KT)
                n = 0
                l8, rot = s5.pow[:, 0, S5_T, z_dve].unsqueeze(1).to_broadcast([P, 2, S5_G // 2]), s5.rot[:, :, z_dve]
                m1, m2 = (tmp_flat[:, i * S5_G:(i + 1) * S5_G].rearrange("p (r c) -> p r c", r=2) for i in range(2))
                for k in range(1, S5_C - 1):
                    z0, z1 = s5.z[:, :, z_dve, k - 1], s5.z[:, :, z_dve, k]
                    v.tensor_tensor(m1, z0, l8, ALU.mult).then_inc(s5_step, 1)
                    v.tensor_tensor(m2, z0[:, ::-1, :], rot, ALU.mult).then_inc(s5_step, 1)
                    v.wait_ge(s5_step, n + 1)
                    v.tensor_tensor(z1, z1, m1, ALU.add).then_inc(s5_step, 1)
                    v.wait_ge(s5_step, n + 3)
                    v.tensor_tensor(z1, z1, m2, ALU.add).then_inc(s5_step, 1)
                    n += 4
                    v.wait_ge(s5_step, n)

                v.wait_ge(s5_intra_copied, KT)
                added = 0
                for n, f in enumerate(w_dve[1:] + [KT], 1):
                    if f < KT:
                        if f >= 4:
                            v.wait_ge(s5_out_ready, f - 3)
                        v.wait_ge(s5_w_ready, n)
                        s5_product(s5.w[f % 4], s5.c, -1, f, 1, s5_w_part, s5_w_ready, n)
                    while added < (f - 2 if f < KT else KT):
                        v.wait_ge(s5_out_ready, added + 1)
                        yf = s5.y[:, added * KT:(added + 1) * KT, :]
                        v.tensor_tensor(yf, bank[4 + added % 4][:, 0:S].rearrange("p (g c) -> p g c", g=KT), yf,
                                        ALU.add).then_inc(s5_y_ready, 1)
                        added += 1
                for f in range(KT):
                    if f % (KT // 2) == 0:
                        v.wait_ge(s5_y_loaded[f // (KT // 2)], 16)
                    hf = h[:, f, :].rearrange("p (c i) -> p c i", i=S5_T)
                    v.scalar_tensor_tensor(hf, hf, s5.d[:, f:f + 1], s5.yt[:, f].rearrange("p i c -> p c i"),
                                           ALU.mult, ALU.add).then_inc(s5_skip_ready, 1)
                    for b in {3: (0,), 5: (1,), 7: (2, 3)}.get(f, ()):
                        v.wait_ge(s5_g_hi_ready, b + 1)
                        v.tensor_tensor(h_lo[:, 2 * b:2 * b + 2, :], h[:, 2 * b:2 * b + 2, :],
                                        h_hi[:, 2 * b:2 * b + 2, :].bitcast(F32), ALU.subtract).then_inc(s5_g_lo_ready, 1)
                for k in range(4):
                    split(st["n0"] + 2 * k + 2)
                    split(st["n0"] + 2 * k + 3)
                    v.wait_ge(glu_sig_ready, k + 1)
                    v.tensor_tensor(act[:, k % 2], gate[:, k % 2], bank[(2 * k) % PROJ_BANKS][:, :].rearrange(
                        "p (t s) -> p t s", t=2), ALU.mult).then_inc(glu_mul_ready, 1)
                    v.wait_ge(glu_mul_ready, k + 1)
                    xq = x[:, 2 * k:2 * k + 2, :]
                    v.tensor_tensor(xq, act[:, k % 2], xq, ALU.add).then_inc(x_ready, 1)

            def dilated_mixer(st):
                n0 = st["n0"]

                def scale_due(p):
                    hb, i, _ = da_panel(p)
                    if i % 2 == 0 or not 3 <= i <= QK + 1:
                        return
                    g, c = (i - 3) // 2, hb * QK + i - 3
                    rq, rs, k = da.rq[:, hb % 2, g], da.rs[:, c // 2 % 2], da.qk[:, hb % 2, 1, g]
                    v.wait_ge(qk_rms_ready, c + 2)
                    v.reciprocal(rq, rq).then_inc(qk_ready, 1)
                    v.reciprocal(rs, rs).then_inc(qk_rstd_ready, 1)
                    v.wait_ge(qk_rstd_ready, c // 2 + 1)
                    v.wait_ge(qk_copied, c + 2)
                    v.tensor_tensor(k, k, rs.rearrange("p (m n) -> p m n", m=2), ALU.mult).then_inc(qk_ready, 1)

                def bias(u):
                    qt = u % 2
                    v.wait_ge(sc_ready, u + 1)
                    v.wait_ge(bias_loaded[u % 3], 16 * (u // 3 + 1))
                    if u >= 3:
                        v.wait_ge(pt_ready, u - 2)
                    if u % UNITS == 0:
                        v.wait_ge(qk_ready, QK * (u // UNITS + 1))
                    hb, m, e = u // UNITS, u // 4 % 2, u // 2 % 2
                    tiles = [da.bias[:, u % 3, 0, ::-1].rearrange("p (j z) -> p z j", z=2)]
                    tiles += [da.bias[:, u % 3, g:g + 1, S - 1 - qt::-2] for g in range(1, NG)]
                    at = 0
                    for g, tile in enumerate(tiles):
                        cols = slice(at, at + tile.shape[1] * P)
                        at = cols.stop
                        ins = v.scalar_tensor_tensor(da.sc[:, u % 3, cols].rearrange("p (z j) -> p z j", j=P),
                                                     da_bank(u)[:, cols].rearrange("p (z j) -> p z j", j=P),
                                                     da.rq[:, hb % 2, g, m, qt, e:e + 1], tile, ALU.mult, ALU.add)
                    ins.then_inc(sc_biased, 1)
                    v.wait_ge(sc_biased, u + 1)
                    v.reduce_max(da.stat[:, 0, u:u + 1], da.sc[:, u % 3], AX.X).then_inc(max_ready, 1)
                    v.wait_ge(max_ready, u + 1)
                    v.tensor_scalar(da.stat[:, 1, u:u + 1], da.stat[:, 0, u:u + 1], -1.0, None,
                                    ALU.mult).then_inc(neg_ready, 1)

                def scale_p(u):
                    v.wait_ge(p_ready, u + 1)
                    v.reciprocal(da.stat[:, 3, u:u + 1], da.stat[:, 2, u:u + 1]).then_inc(rden_ready, 1)
                    v.wait_ge(rden_ready, u + 1)
                    v.tensor_scalar(da.sc[:, u % 3], da.sc[:, u % 3], da.stat[:, 3, u:u + 1], None,
                                    ALU.mult).then_inc(p_scaled, 1)

                def lower(b):
                    v.wait_ge(o_hi_ready, b + 1)
                    v.tensor_tensor(h_lo[:, 2 * b:2 * b + 2, :], h[:, 2 * b:2 * b + 2, :],
                                    h_hi[:, 2 * b:2 * b + 2, :].bitcast(F32), ALU.subtract).then_inc(o_lo_ready, 1)

                for p in range(PANELS):
                    split(n0 + p + 2)
                    scale_due(p)
                last = n_units - UNITS
                for u in range(last):
                    bias(u)
                    panels = da_panels(u)
                    split(n0 + panels[0] + 2)
                    scale_p(u)
                    scale_due(panels[0])
                    for p in panels[1:]:
                        split(n0 + p + 2)
                        scale_due(p)
                bias(last)
                split(n0 + 38)
                for u in range(last + 1, n_units + 1):
                    if u < n_units:
                        bias(u)
                    scale_p(u - 1)
                    if u - last <= BLOCKS - 1:
                        lower(u - last - 1)
                lower(BLOCKS - 1)
                for k in range(4):
                    if k:
                        split(n0 + 36 + k + 2)
                    add_panel(st, k, 36)

            def mixer(st):
                nonlocal n_steps
                i, n0 = st["i"], st["n0"]

                def then(*ins):
                    nonlocal n_steps
                    for q in ins:
                        q.then_inc(mix_step, 1)
                        n_steps += 1
                    v.wait_ge(mix_step, n_steps)

                tt, ts, stt = v.tensor_tensor, v.tensor_scalar, v.scalar_tensor_tensor
                v.wait_ge(mix_loaded, 64 * (i + 1))

                units = 2 * ATT_H

                def conv(pair):
                    v.wait_ge(conv_first, CONV_T * i + 2 * pair + 2)
                    pair = (2 * pair, 2 * pair + 1)
                    for k in range(1, CONV):
                        ops = [stt(mx.conv[:, c], mx.raw[:, c, k:k + S], mx.convw[:, c, k:k + 1], mx.conv[:, c],
                                   ALU.mult, ALU.add) for c in pair]
                        if k < CONV - 1:
                            then(*ops)
                        else:
                            for q in ops:
                                q.then_inc(conv_ready, 1)

                def turn(r):
                    n = ROTS * i + r
                    part = mx.qi[:, 2 * (r - 1):2 * (r - 1) + 2, :] if r else mx.ki.unsqueeze(1)
                    heads = part.shape[1]
                    cos, sin = (rope[:, m, :].unsqueeze(1).to_broadcast([P, heads, S]) for m in (2, 3))
                    tmp = mx.rot[:, r, 0:heads * S].rearrange("p (h s) -> p h s", h=heads)
                    v.wait_ge(rot_ready, n + 1)
                    tt(tmp, bank[4 + r][:, 0:heads * S].rearrange("p (h s) -> p h s", h=heads), sin,
                       ALU.mult).then_inc(rope_used, 1)
                    then(tt(part, part, cos, ALU.mult))
                    v.wait_ge(rope_used, n + 1)
                    tt(part, part, tmp, ALU.add).then_inc(rope_done, 1)

                def add_scores(us):
                    for u in us:
                        qt, hd = divmod(u, IDX_H)
                        n, keys = 2 * IDX_H * i + u, (qt + 1) * P
                        sco = mx.score[:, qt, 0:keys]
                        v.wait_ge(relu_ready, n + 1)
                        if hd == 0:
                            v.wait_ge(mix_step, n_steps)
                            ins = ts(sco, mx.relu[:, u % RELUS, 0:keys], mx.wi[:, qt, hd:hd + 1], None, ALU.mult)
                        else:
                            v.wait_ge(idx_added, n)
                            ins = stt(sco, mx.relu[:, u % RELUS, 0:keys], mx.wi[:, qt, hd:hd + 1], sco, ALU.mult, ALU.add)
                        ins.then_inc(idx_added, 1)

                def pick(qt, first, last):
                    keys = (qt + 1) * P
                    sco = mx.score[:, qt, 0:keys]
                    if first == 0:
                        v.wait_ge(idx_added, 2 * IDX_H * i + (qt + 1) * IDX_H)
                        then(tt(sco, sco, mx.causal[:, qt, 0:keys], ALU.add))
                    for _ in range(first, last):
                        then(v.max(mx.top8[:, qt], sco))
                        then(v.match_replace(sco, mx.top8[:, qt], sco, TAKEN))
                    if last == TOPK // 8:
                        then(ts(sco, sco, TAKEN / 2, MASKED, ALU.is_gt, ALU.mult))
                        tt(mx.sel[:, qt, 0:keys], sco, mx.causal[:, qt, 0:keys], ALU.add).then_inc(sel_ready, 1)

                def decay_args(j):
                    for e in range(2):
                        hd = 2 * j + e
                        n = SSD_H * i + hd
                        v.wait_ge(cs_ready, n + 1)
                        if j:
                            v.wait_ge(decay_used, n - 1)
                        stt(mx.dec[:, e, 0], bank[4 + e][:, 0:S], mx.tok[:, 0, hd:hd + 1], mx.tri[:, 0], ALU.subtract, ALU.add)
                        stt(mx.dec[:, e, 1, P:], bank[4 + e][:, P:S], mx.tok[:, 1, hd:hd + 1], mx.tri[:, 1, P:],
                            ALU.subtract, ALU.add).then_inc(decay_arg, 1)

                def decay_times(j):
                    for e in range(2):
                        hd = 2 * j + e
                        g = hd // (SSD_H // SSD_G)
                        v.wait_ge(decay_ready, SSD_H * i + hd + 1)
                        if j:
                            v.wait_ge(yp_ready, 8 * i + j)
                        stt(mx.m[:, e, 0], mx.dec[:, e, 0], mx.tok[:, 0, 64 + hd:65 + hd], mx.cb[:, g, 0], ALU.mult, ALU.mult)
                        stt(mx.m[:, e, 1, P:], mx.dec[:, e, 1, P:], mx.tok[:, 1, 64 + hd:65 + hd], mx.cb[:, g, 1, P:],
                            ALU.mult, ALU.mult).then_inc(decay_used, 1)

                def y_tile(j):
                    v.wait_ge(yp_ready, 8 * i + j + 1)
                    stt(mx.y[:, j], mx.conv[:, j], mx.dskip[:, j:j + 1], bank[6][:, 0:S],
                        ALU.mult, ALU.add).then_inc(y_raw, 1)

                def y_gate(g):
                    v.wait_ge(mix_copied, OUT_SSD * i + Z + 2 * g + 2)
                    for j in range(4 * g, 4 * g + 4):
                        v.wait_ge(y_raw, 8 * i + j + 1)
                        tt(mx.y[:, j], mx.y[:, j], mx.z[:, j], ALU.mult).then_inc(y_gated, 1)

                def y_norm(g):
                    v.wait_ge(mix_step, n_steps)
                    for c in range(4 * g, 4 * g + 4):
                        q = stt(mx.y[:, c], mx.y[:, c], mx.ygain[:, c:c + 1], mx.rms[:, g], ALU.mult, ALU.mult)
                        if c % 2:
                            q.then_inc(y_normed, 1)

                def lower_ssd(bs):
                    for b in bs:
                        v.wait_ge(y_hi_ready, 4 * i + b + 1)
                        tt(out_pair((h_lo, act_lo), False, b), mx.y[:, 2 * b:2 * b + 2, :],
                           out_pair((h_hi, act_hi), False, b).bitcast(F32), ALU.subtract).then_inc(y_lo_ready, 1)

                def lower_att(bs):
                    for b in bs:
                        v.wait_ge(att_hi_ready, 4 * i + b + 1)
                        tt(out_pair((h_lo, act_lo), True, b), mx.yatt[:, 2 * b:2 * b + 2, :],
                           out_pair((h_hi, act_hi), True, b).bitcast(F32), ALU.subtract).then_inc(att_lo_ready, 1)

                def bias_unit(u):
                    n, keys = units * i + u, (u % 2 + 1) * P
                    sc = mx.sc[:, u % 3, 0:keys]
                    v.wait_ge(att_sc_ready, n + 1)
                    if u >= 3:
                        v.wait_ge(att_pt_ready, n - 2)
                    stt(sc, bank[4 + u % 2][:, 0:keys], P ** -0.5, mx.sel[:, u % 2, 0:keys],
                        ALU.mult, ALU.add).then_inc(att_biased, 1)
                    v.wait_ge(att_biased, n + 1)
                    then(v.reduce_max(mx.stat[:, 0, u:u + 1], sc, AX.X))
                    ts(mx.stat[:, 1, u:u + 1], mx.stat[:, 0, u:u + 1], -1.0, None, ALU.mult).then_inc(att_neg, 1)

                def scale_unit(u):
                    sc = mx.sc[:, u % 3, 0:(u % 2 + 1) * P]
                    v.wait_ge(att_p_ready, units * i + u + 1)
                    then(v.reciprocal(mx.stat[:, 3, u:u + 1], mx.stat[:, 2, u:u + 1]))
                    ts(sc, sc, mx.stat[:, 3, u:u + 1], None, ALU.mult).then_inc(att_scaled, 1)

                split(n0 + 2)
                d = mx.dt
                v.wait_ge(mix_copied, OUT_SSD * i + MISC + 1)
                then(ts(d[0], d[0], mx.dtb, None, ALU.add))
                then(ts(d[1], d[0], -1.0, None, ALU.mult))
                tt(d[1], d[0], d[1], ALU.min).then_inc(dt_arg_ready, 1)
                split(n0 + QI + 2)
                v.wait_ge(dt_exp_ready, 2 * (i + 1))
                then(ts(d[3], d[2], 2.0, None, ALU.add))
                then(v.reciprocal(d[3], d[3]))
                then(tt(d[2], d[2], d[3], ALU.mult))
                then(tt(d[3], d[2], d[2], ALU.mult))
                then(ts(d[4], d[3], 1.0 / (2 * LOG_TERMS + 1), None, ALU.mult))
                for k in range(LOG_TERMS - 1, 0, -1):
                    then(stt(d[4], d[4], 1.0 / (2 * k + 1), d[3], ALU.add, ALU.mult))
                then(stt(d[4], d[4], 1.0, d[2], ALU.add, ALU.mult), ts(d[0], d[0], 0.0, None, ALU.max))
                then(stt(d[0], d[4], 2.0, d[0], ALU.mult, ALU.add))
                v.wait_ge(small_set, 2 * (i + 1))
                then(ts(d[5], d[0], mx.alog, -1.0, ALU.mult, ALU.mult),
                     v.tensor_copy(mx.small[64:64 + SSD_H, :], d[0]))
                v.tensor_tensor_scan(mx.small[0:SSD_H, :], ones[0:SSD_H, 0:1].to_broadcast([SSD_H, S]), d[5], 0.0,
                                     ALU.mult, ALU.add).then_inc(small_ready, 1)
                split(n0 + QI + 3)
                split(n0 + XBC + 2)
                v.wait_ge(rope_ready, 1)
                v.wait_ge(mix_copied, OUT_SSD * i + XBC)
                for r in range(3):
                    turn(r)
                v.wait_ge(tok_copied, i + 1)
                ts(mx.wi, mx.tok[:, :, 32:32 + IDX_H], IDX_H ** -0.5, None, ALU.mult).then_inc(mix_step, 1)
                n_steps += 1
                v.wait_ge(cs_hi_ready, i + 1)
                tt(cs_lo, mx.small[0:SSD_H, :], cs_hi.bitcast(F32), ALU.subtract).then_inc(cs_lo_ready, 1)
                for p in range(XBC + 1, Q + 1):
                    split(n0 + p + 2)
                    if p > Q - 4:
                        add_scores(range(4 * (p - Q + 3), 4 * (p - Q + 4)))
                    conv(p - XBC - 1)
                for half in range(2):
                    split(n0 + Q + half + 3)
                    pick(0, half * TOPK // 16, (half + 1) * TOPK // 16)
                v.wait_ge(cb_copied, 2 * i + 2)
                for j in range(SSD_H // 2):
                    decay_args(j)
                    if j:
                        y_tile(j - 1)
                    pick(1, j * TOPK // 64, (j + 1) * TOPK // 64)
                    decay_times(j)
                    split(n0 + SSD_0 + j + 2)
                y_tile(SSD_H // 2 - 1)
                v.wait_ge(sel_ready, 2 * i + 2)
                for p in range(Z + 3, OUT_ATT):
                    if p == Z + 3:
                        bias_unit(0)
                        bias_unit(1)
                    if p in (Z + 3, V):
                        y_gate(p - Z - 3)
                    for u in UNITS_AFTER[p]:
                        scale_unit(u)
                    split(n0 + p + 2)
                    if p == V + 1:
                        v.wait_ge(yrms_ready, i + 1)
                        then(v.reciprocal(mx.rms, mx.rms))
                        y_norm(0)
                    if p == V + 2:
                        y_norm(1)
                        lower_ssd((0, 1))
                    if p == V + 3:
                        lower_ssd((2, 3))
                    if p == OUT_SSD + 1:
                        lower_att((0, 1))
                    for u in UNITS_AFTER[p]:
                        if u + 2 < units:
                            bias_unit(u + 2)
                lower_att((2, 3))
                for k in range(4):
                    split(n0 + OUT_ATT + k + 2)
                    add_panel(st, k, OUT_ATT)

            n_steps = 0
            v.memset(zeros[:, :].bitcast(F32), 0.0).then_inc(zeros_set, 1)
            todo = {"norm": norm, "final": norm, "ffn": ffn, "fourier": fourier, "s5": s5_mixer,
                    "dilated": dilated_mixer, "mix": mixer}
            for n, st in enumerate(stages):
                st["s5_follows"] = [q["kind"] for q in stages[n + 1:n + 3]] == ["norm", "s5"]
                todo[st["kind"]](st)
                if n == 0:
                    v.wait_ge(e_ready, 1)
                    v.tensor_tensor(da.e, bank[0][0:NG * HEADS, :], da.mask, ALU.add).then_inc(e_masked, 1)
                    split(0)
                    split(1)
                    s5_prepare()

        @block.tensor
        def _(t):
            def mm3(o, w, xin, start, stop):
                t.matmul(o, w[0], xin[0], start=start, stop=False, skip_group_check=True)
                t.matmul(o, w[0], xin[1], start=False, stop=False, skip_group_check=True)
                return t.matmul(o, w[1], xin[0], start=False, stop=stop, skip_group_check=True)

            def weights(n, lo, width=P):
                s = n % SLOTS
                return w_hi[:, s, lo:lo + width], w_lo[:, s, lo:lo + width]

            def project(n, j, i=None, per=0, parts=None, o=None):
                t.wait_ge(lo_ready, n + 1 if i is None else i * per + n + 1)
                o = bank[j % PROJ_BANKS] if o is None else o
                for k, m in [(k, m) for k in range(KT) for m in range(2)] if parts else \
                        [(k, m) for m in range(2) for k in range(KT)]:
                    if parts and m == 0 and k % 2 == 0:
                        t.wait_ge(parts[0], parts[1] + k // 2 + 1)
                    last = mm3(o[:, m * S:(m + 1) * S], weights(n, k * COLS + m * P), (h_hi[:, k], h_lo[:, k]),
                               k == 0 and (m == 0 or parts is None), k == KT - 1)
                last.then_inc(panel_done, 1)

            def norm(st):
                if st["late"]:
                    return
                n = st["norm"]
                t.wait_ge(const_set, 3)
                for b in range(4):
                    t.wait_ge(sq_ready, 4 * n + b + 1)
                    for c in (2 * b, 2 * b + 1):
                        last = t.matmul(bank[SUMS_BANK[False]][:, 0:S], ones[:, :], h[:, c, :],
                                        start=(c == 0), stop=(c == KT - 1))
                last.then_inc(ss_ready, 1)

            def ffn(st):
                n0, f = st["n0"], st["ffn"]

                def down(c, p, i=None):
                    def at(val, per):
                        return val if i is None else i * per + val
                    t.wait_ge(lo_ready, at(p + 1, 6))
                    t.wait_ge(act_lo_ready, at(f * FFC + c + 1, 2))
                    for k in range(2):
                        for o in range(KT):
                            last = mm3(y_of[o], weights(p, k * D + o * P),
                                       (act_hi[:, c % 2, k], act_lo[:, c % 2, k]), False, True)
                            if c == FFC - 1 and k == 1 and o % 2 and o < KT - 1:
                                last.then_inc(sums_ready, 1)
                    last.then_inc(panel_done, 1)

                project(n0, 0, parts=(h_lo_ready, 4 * st["hs"]))
                t.wait_ge(zeros_set, 1)
                for b in range(4):
                    t.matmul(bank[4 + b][:, :].rearrange("p (a m) -> p a m", m=P), zeros[:, :],
                             zeros[:, :].unsqueeze(1).to_broadcast([P, 4, P]), start=True, stop=True)
                t.wait_ge(sq_added, 3 * (st["hn"] - st["whole"]))
                t.matmul(bank[SUMS_BANK[True]][:, 0:S], ones[:, :], h[:, 0], start=True, stop=True).then_inc(ss_ready, 1)
                project(n0 + 1, 1)
                t.wait_ge(rms_ready, st["hn"] + 1)
                with t.Fori(0, (FFC - 1) // 2) as i:
                    for c in (1, 2):
                        p = hidden_panel(n0, c)
                        t.wait_ge(act_ready, i * 2 + (f * FFC + c - 1))
                        project(p, 2 * c, i, 6)
                        project(p + 1, 2 * c + 1, i, 6)
                        down(c - 1, p + 2, i)
                down(FFC - 1, n0 + 32)

            def fourier(st):
                f = st["fourier"]
                t.wait_ge(dft_loaded, 32 * (f + 1))

                def over_channels(g):
                    k = f * KT + g
                    t.wait_ge(h_ready, 4 * st["whole"] + g // 2 + 1)
                    if g >= 2:
                        t.wait_ge(dft_tok_copied, k - 1)
                    for m in range(2):
                        last = t.matmul(bank[4 + g % 2][:, m * S:(m + 1) * S], h[:, g, m * P:(m + 1) * P],
                                        dft_ch, start=True, stop=True)
                    last.then_inc(dft_tok_ready, 1)

                over_channels(0)
                for g in range(KT):
                    k = f * KT + g
                    if g + 1 < KT:
                        over_channels(g + 1)
                    t.wait_ge(dft_tok_copied, k + 1)
                    if g >= 2:
                        t.wait_ge(dft_lo_ready, k - 1)
                    for m in range(2):
                        for c in range(2):
                            last = t.matmul(bank[6 + g % 2][:, 0:S], dft_tok[:, g % 2, m, c * P:(c + 1) * P],
                                            dft_sq[:, m, c, :], start=(m + c == 0), stop=(m + c == 2))
                    last.then_inc(dft_ready, 1)
                t.wait_ge(dft_lo_ready, (f + 1) * KT)
                for p in range(4):
                    project(st["n0"] + p, p)

            def s5_mixer(st):
                half = [slice(0, S5_N), slice(S5_N, P)]

                def factors(f):
                    vb = s5.buf[f % 2]
                    t.wait_ge(s5_v_ready, f + 1)
                    for q in range(4):
                        if 4 * f + q >= 2:
                            t.wait_ge(s5_win_ready, 4 * f + q - 1)
                        for m in range(4):
                            r, c = divmod(4 * q + m, NC)
                            last = t.transpose(bank[4 + q % 2][:, m * P:(m + 1) * P], vb[:, r, c, :], ident[:, :])
                        last.then_inc(s5_vt_ready, 1)
                    if f:
                        t.wait_ge(s5_k_copied, f)
                    t.wait_ge(s5_cbd_ready, 1 + 4 * (f + 1))
                    for pair in range(4):
                        rows = slice(pair * 2 * S5_P, (pair + 1) * 2 * S5_P)
                        for d in (1, 0):
                            at = 0 if d else (S5_T - 1) * S5_P
                            for r in range(2):
                                c = d * 4 + pair
                                last = t.matmul(bank[0][rows, at:at + P], s5.cbd[:, f % 2, r, c, :], vb[:, r, c, :],
                                                start=(d == 1 and r == 0), stop=(d == 0 and r == 1),
                                                skip_group_check=True)
                    last.then_inc(s5_k_ready, 1)

                t.wait_ge(rms_ready, st["hn"] + 1)
                factors(0)
                for f in range(KT):
                    t.wait_ge(s5_k_copied, f + 1)
                    if f:
                        t.wait_ge(s5_t_copied, 2 * f)
                    for i in range(S5_T):
                        last = t.transpose(bank[7 - i // 4][:, (i % 4) * P:(i % 4 + 1) * P],
                                           s5.kc[:, i * S5_P:i * S5_P + P], ident[:, :])
                    last.then_inc(s5_t_ready, 1)
                    if f == 0:
                        t.wait_ge(s5_u_loaded, 16)
                    t.wait_ge(s5_win_ready, 4 * f + 4)
                    if f >= 2:
                        t.wait_ge(s5_in_copied, f - 1)
                    for r in range(2):
                        for c in range(NC):
                            for e in range(2):
                                g = f * KT + (c % 4) * 2 + e
                                o = bank[2 + f % 2][half[e], (r * NC + c) * S5_C:(r * NC + c + 1) * S5_C]
                                rhs = s5.u[:, g, :] if c < 4 else s5.u[:, g, ::-1]
                                last = t.matmul(o, s5.win[:, r * NC + c, half[e]], rhs, start=True, stop=True)
                    last.then_inc(s5_in_ready, 1)
                    if f + 1 < KT:
                        factors(f + 1)
                    t.wait_ge(s5_t_copied, 2 * f + 2)
                    if f:
                        t.wait_ge(s5_intra_copied, f)
                    for g in range(KT):
                        last = t.matmul(bank[1][:, g * S5_C:(g + 1) * S5_C], s5.tc[:, g].rearrange("p i m -> p (i m)"),
                                        s5.u[:, f * KT + g, :], start=True, stop=True)
                    last.then_inc(s5_intra_ready, 1)
                w_dve = [f for f in range(KT) if f not in W_POOL]

                def bring(n):
                    f, h2 = divmod(n, 2)
                    if h2 == 0:
                        if f in W_POOL:
                            t.wait_ge(s5_wp_ready, W_POOL.index(f) + 1)
                        else:
                            t.wait_ge(s5_w_ready, w_dve.index(f) + 1)
                        t.wait_ge(s5_zbd_ready, 4 * f + 4)
                    if n >= 2:
                        t.wait_ge(s5_back_copied, 2 * KT + n - 1)
                    for k in range(2):
                        pair = 2 * h2 + k
                        for d in range(2):
                            for r in range(2):
                                last = t.matmul(bank[2 + n % 2][0:2 * S5_C, k * P:(k + 1) * P],
                                                s5.zbd[:, f % 2, r, 4 * d + pair, :], s5.w[f % 4][:, r, 4 * d + pair, :],
                                                start=(d + r == 0), stop=(d + r == 2))
                    last.then_inc(s5_back_ready, 1)

                def turn_back(n):
                    f, h2 = divmod(n, 2)
                    t.wait_ge(s5_back_copied, 2 * KT + n + 1)
                    if h2 == 0 and f >= 4:
                        t.wait_ge(s5_y_ready, f - 3)
                    for k in range(2):
                        at = (2 * h2 + k) * 2 * S5_C
                        last = t.transpose(bank[4 + f % 4][:, at:at + 2 * S5_C], s5.back[n % 3][:, k * P:(k + 1) * P],
                                           ident[0:2 * S5_C, 0:2 * S5_C])
                    if h2:
                        last.then_inc(s5_out_ready, 1)

                for n in range(2 * KT):
                    bring(n)
                    if n:
                        turn_back(n - 1)
                turn_back(2 * KT - 1)
                for p in range(8):
                    if p >= PROJ_BANKS:
                        t.wait_ge(x_ready, st["xr"] + p // 2 - 1)
                    project(st["n0"] + p, p, parts=None if p else (s5_g_lo_ready, 0))

            def project_tokens(n, o, tokens):
                t.wait_ge(lo_ready, n + 1)
                for m in range(2):
                    for k in range(KT):
                        last = mm3(o[:, m * COLS:(m + 1) * COLS], (h_hi[:, k, tokens[m]], h_lo[:, k, tokens[m]]),
                                   weights(n, k * COLS, COLS), k == 0, k == KT - 1)
                last.then_inc(panel_done, 1)

            def dilated_mixer(st):
                n0 = st["n0"]
                alone = n_units - UNITS

                def sums(c):
                    t.wait_ge(qk_sq_ready, c + 1)
                    if c >= 2:
                        t.wait_ge(qk_rms_ready, c - 1)
                    if c % 2 == 0:
                        for m in range(2):
                            for qt in range(2):
                                at = (2 * m + qt) * 2
                                last = t.matmul(bank[3][:, at:at + 2], da.sq[:, 0, m * S + qt:(m + 1) * S:2],
                                                da.pair_ones[:, 0:P:E], start=True, stop=True)
                    else:
                        last = t.matmul(bank[5][:, :], da.pair_ones, da.sq[:, 1], start=True, stop=True)
                    last.then_inc(qk_ss_ready, 1)

                def panel(p):
                    hb, i, _ = da_panel(p)
                    if p >= 3:
                        _, i3, c3 = da_panel(p - 3)
                        t.wait_ge(qk_copied if i3 < QK else v_copied, c3 + 1)
                    o = bank[p % 3]
                    if i < QK:
                        project(n0 + p, 0, o=o, parts=None if p else (h_lo_ready, 4 * st["hs"]))
                    else:
                        project_tokens(n0 + p, o, (slice(0, S, 2), slice(1, S, 2)))
                    if 1 <= i <= QK:
                        sums(hb * QK + i - 1)

                def scores(u):
                    hb, head, qt = u // UNITS, u // 2, u % 2
                    m, rows = head // 2 % 2, slice(head % 2 * E, head % 2 * E + E)
                    t.wait_ge(qk_ready, QK * (hb + 1))
                    if u:
                        t.wait_ge(sc_biased, u if u <= alone + 1 else u - 1)
                    q, k = da.qk[rows, hb % 2, 0, :, m], da.qk[rows, hb % 2, 1, :, m]
                    t.matmul(da_bank(u)[:, 0:S].rearrange("p (z j) -> p z j", z=2), q[:, 0, qt::2],
                             k[:, 0, :].rearrange("p (j z) -> p z j", z=2), start=True, stop=True)
                    for g in range(1, NG):
                        last = t.matmul(da_bank(u)[:, S + (g - 1) * P:S + g * P], q[:, g, qt::2], k[:, g, qt::2],
                                        start=True, stop=True)
                    last.then_inc(sc_ready, 1)

                def values(u):
                    t.wait_ge(p_scaled, u + 1)
                    if u:
                        t.wait_ge(pt_copied, u)
                    for i in range(4):
                        last = t.transpose(bank[6][:, i * P:(i + 1) * P], da.sc[:, u % 3, i * P:(i + 1) * P], ident[:, :])
                    last.then_inc(pt_ready, 1)

                def out_(u):
                    hb, head, qt = u // UNITS, u // 2, u % 2
                    rows = slice(head % 2 * E, head % 2 * E + E)
                    cols = slice(head % HB * E, head % HB * E + E)
                    t.wait_ge(pt_copied, u + 1)
                    t.wait_ge(v_copied, NG * (hb + 1))
                    if u:
                        t.wait_ge(o_copied, u)
                    for i, (g, parity) in enumerate(((0, 0), (0, 1), (1, qt), (2, qt))):
                        last = t.matmul(bank[7][rows, 0:P], da.v[:, hb % 2, g, parity, cols],
                                        da.pt[:, u % 2, i * P:(i + 1) * P], start=(i == 0), stop=(i == 3))
                    last.then_inc(o_ready, 1)

                def output(k, tiles):
                    t.wait_ge(lo_ready, n0 + 36 + k + 1)
                    t.wait_ge(o_lo_ready, (tiles[-1] + 2) // 2)
                    for c in tiles:
                        for m in range(2):
                            last = mm3(bank[k][:, m * S:(m + 1) * S], weights(n0 + 36 + k, c * COLS + m * P),
                                       (h_hi[:, c], h_lo[:, c]), c + m == 0, c == KT - 1)
                    if tiles[-1] == KT - 1:
                        last.then_inc(panel_done, 1)

                t.wait_ge(rms_ready, st["hn"] + 1)
                t.wait_ge(e_loaded, 16 * 5)
                for p in range(PANELS):
                    panel(p)
                for u in range(alone):
                    scores(u)
                    for p in da_panels(u):
                        panel(p)
                    if u:
                        out_(u - 1)
                    values(u)
                scores(alone)
                out_(alone - 1)
                scores(alone + 1)
                early = list(range(KT - 2))
                for u in range(alone, n_units):
                    if u + 2 < n_units:
                        scores(u + 2)
                    values(u)
                    if u > alone:
                        out_(u - 1)
                    if u - alone in (2, 4, 6):
                        output((u - alone) // 2 - 1, early)
                out_(n_units - 1)
                for k in range(3):
                    output(k, [KT - 2, KT - 1])
                output(3, early + [KT - 2, KT - 1])

            def mixer(st):
                i, n0 = st["i"], st["n0"]
                units = 2 * ATT_H

                def arrive(p):
                    if p >= PROJ_BANKS:
                        t.wait_ge(mix_copied, OUT_SSD * i + p - PROJ_BANKS + 1)
                    if p >= V:
                        project_tokens(n0 + p, bank[p % PROJ_BANKS], (slice(0, P), slice(P, S)))
                    else:
                        project(n0 + p, p, parts=(h_lo_ready, 4 * st["hs"]) if p == 0 else None)

                def accumulate(p, k, tile, tiles=range(KT)):
                    t.wait_ge(lo_ready, n0 + p + 1)
                    for c in tiles:
                        for m in range(2):
                            last = mm3(bank[k][:, m * S:(m + 1) * S], weights(n0 + p, c * COLS + m * P), tile(c),
                                       p < OUT_ATT and m == 0 and c == 0, c == KT - 1)
                    if KT - 1 in tiles:
                        last.then_inc(panel_done, 1)

                def turned(r):
                    src = mx.qi[:, 2 * (r - 1):2 * (r - 1) + 2, :].rearrange("p h s -> p (h s)") if r else mx.ki
                    t.matmul(bank[4 + r][:, 0:src.shape[1]], mx.turn_i, src, start=True, stop=True).then_inc(rot_ready, 1)

                def sums(j):
                    for e in range(2):
                        n = SSD_H * i + 2 * j + e
                        if j:
                            t.wait_ge(decay_arg, n - 1)
                        head = pick_head[:, 2 * j + e:2 * j + e + 1].to_broadcast([SSD_H, P])
                        t.matmul(bank[4 + e][:, 0:S], head, cs_hi, start=True, stop=False)
                        t.matmul(bank[4 + e][:, 0:S], head, cs_lo, start=False, stop=True).then_inc(cs_ready, 1)

                def ssd_pair(j):
                    if j:
                        t.wait_ge(y_raw, 8 * i + j)
                    for e in range(2):
                        hd = 2 * j + e
                        t.wait_ge(decay_used, SSD_H * i + hd + 1)
                        o = bank[6][e * SSD_P:(e + 1) * SSD_P, :]
                        heads = slice(hd * SSD_P, (hd + 1) * SSD_P)
                        t.matmul(o[:, 0:P], mx.xt[:, 0, heads], mx.m[:, e, 0, 0:P], start=True, stop=True)
                        t.matmul(o[:, P:S], mx.xt[:, 0, heads], mx.m[:, e, 0, P:], start=True, stop=False)
                        last = t.matmul(o[:, P:S], mx.xt[:, 1, heads], mx.m[:, e, 1, P:], start=False, stop=True)
                    last.then_inc(yp_ready, 1)

                def scores(u):
                    hd, qt = divmod(u, 2)
                    t.wait_ge(heads_turned, KT * i + 4 + hd // 2 + 1)
                    if u >= 2:
                        t.wait_ge(att_biased, units * i + u - 1)
                    t.matmul(bank[4 + u % 2][:, 0:(qt + 1) * P], mx.q[:, hd, qt * P:(qt + 1) * P],
                             mx.k[:, hd, 0:(qt + 1) * P], start=True, stop=True).then_inc(att_sc_ready, 1)

                def values(u):
                    qt = u % 2
                    t.wait_ge(att_scaled, units * i + u + 1)
                    if u:
                        t.wait_ge(att_pt_copied, units * i + u)
                    for k in range(qt + 1):
                        last = t.transpose(bank[6][:, k * P:(k + 1) * P], mx.sc[:, u % 3, k * P:(k + 1) * P], ident[:, :])
                    last.then_inc(att_pt_ready, 1)

                def out_(u):
                    hd, qt = divmod(u, 2)
                    t.wait_ge(mix_copied, OUT_SSD * i + V + hd // 2 + 1)
                    t.wait_ge(att_pt_copied, units * i + u + 1)
                    if u:
                        t.wait_ge(att_o_copied, units * i + u)
                    for k in range(qt + 1):
                        last = t.matmul(bank[7][:, u % 2 * P:(u % 2 + 1) * P], mx.v[:, k, hd * P:(hd + 1) * P],
                                        mx.pt[:, u % 2, k * P:(k + 1) * P], start=(k == 0), stop=(k == qt))
                    last.then_inc(att_o_ready, 1)

                for p in range(XBC + 1):
                    arrive(p)
                t.wait_ge(small_ready, i + 1)
                for tt_ in range(2):
                    last = t.transpose(bank[7][:, tt_ * P:(tt_ + 1) * P], mx.small[:, tt_ * P:(tt_ + 1) * P], ident[:, :])
                last.then_inc(tok_ready, 1)
                t.wait_ge(mix_copied, OUT_SSD * i + XBC)
                for r in range(3):
                    turned(r)
                for p in range(XBC + 1, Q):
                    arrive(p)
                    if p == Q - 4:
                        t.wait_ge(rope_done, ROTS * (i + 1))
                        t.wait_ge(tok_copied, i + 1)
                    for u in range(4 * (p - Q + 4), 4 * (p - Q + 5)) if p >= Q - 4 else ():
                        qt, hd = divmod(u, IDX_H)
                        rows = slice(hd % 2 * E, hd % 2 * E + E)
                        if u >= 4:
                            t.wait_ge(relu_ready, 2 * IDX_H * i + u - 3)
                        t.matmul(bank[4 + u % 4][:, 0:(qt + 1) * P], mx.qi[rows, hd // 2, qt * P:(qt + 1) * P],
                                 mx.ki[rows, 0:(qt + 1) * P], start=True, stop=True).then_inc(idx_ready, 1)
                for half in range(2):
                    arrive(Q + half)
                    if half == 0:
                        t.wait_ge(relu_ready, 2 * IDX_H * (i + 1))
                    for q in (2 * half, 2 * half + 1):
                        t.wait_ge(conv_act, CONV_T * i + 2 * q + 2)
                        if q >= 2:
                            t.wait_ge(xt_copied, 4 * i + q - 1)
                        for tt_ in range(2):
                            for c in range(2):
                                last = t.transpose(bank[5 + q % 2][:, (tt_ * 2 + c) * P:(tt_ * 2 + c + 1) * P],
                                                   mx.conv[:, 2 * q + c, tt_ * P:(tt_ + 1) * P], ident[:, :])
                        last.then_inc(xt_ready, 1)
                t.wait_ge(conv_act, CONV_T * (i + 1))
                for g in range(SSD_G):
                    o = bank[7 if g == 0 else 4]
                    for tt_ in range(2):
                        last = t.matmul(o[:, tt_ * (S + P):2 * S if tt_ else S], mx.conv[:, 8 + g, tt_ * P:(tt_ + 1) * P],
                                        mx.conv[:, 8 + SSD_G + g, tt_ * P:], start=True, stop=True)
                    last.then_inc(cb_ready, 1)
                arrive(SSD_0 - 1)
                t.wait_ge(cb_copied, 2 * i + 2)
                t.wait_ge(xt_copied, 4 * i + 4)
                t.wait_ge(cs_lo_ready, i + 1)
                sums(0)
                for j in range(SSD_H // 2):
                    arrive(SSD_0 + j)
                    if j + 1 < SSD_H // 2:
                        sums(j + 1)
                    ssd_pair(j)
                t.wait_ge(decay_arg, SSD_H * (i + 1))
                scores(0)
                scores(1)
                t.wait_ge(y_raw, 8 * (i + 1))
                for p in range(Z + 3, OUT_ATT):
                    if p == V + 2:
                        t.wait_ge(yrms_ready, i + 1)
                    if p < OUT_SSD:
                        arrive(p)
                    elif p == OUT_SSD:
                        for b in range(4):
                            t.wait_ge(y_lo_ready, 4 * i + b + 1)
                            accumulate(p, 0, ssd_out_tile, (2 * b, 2 * b + 1))
                    else:
                        accumulate(p, p - OUT_SSD, ssd_out_tile)
                    for u in UNITS_AFTER[p]:
                        if u + 2 < units:
                            scores(u + 2)
                        values(u)
                        if u:
                            out_(u - 1)
                    if p == V:
                        for g in range(SSD_G):
                            t.wait_ge(ysq_ready, 2 * i + g + 1)
                            t.wait_ge(mix_copied, OUT_SSD * i + Z + 3)
                            for c in range(4):
                                last = t.matmul(bank[(Z + 2) % PROJ_BANKS][:, g * S:(g + 1) * S], ones[:, :],
                                                mx.z[:, 4 * g + c], start=(c == 0), stop=(c == 3))
                        last.then_inc(yss_ready, 1)
                for b in range(4):
                    if b == 2:
                        out_(units - 1)
                    t.wait_ge(att_lo_ready, 4 * i + b + 1)
                    accumulate(OUT_ATT, 0, att_out_tile, (2 * b, 2 * b + 1))
                for k in range(1, 4):
                    accumulate(OUT_ATT + k, k, att_out_tile)

            todo = {"norm": norm, "final": norm, "ffn": ffn, "fourier": fourier, "s5": s5_mixer,
                    "dilated": dilated_mixer, "mix": mixer}
            for n, st in enumerate(stages):
                todo[st["kind"]](st)
                if n == 0:
                    t.wait_ge(e_loaded, 16 * 3)
                    t.matmul(bank[0][0:NG * HEADS, :], da.rel, da.onehot, start=True, stop=True).then_inc(e_ready, 1)
                    t.wait_ge(e_masked, 1)


def panel_of(w, c0):
    return w[:, c0:c0 + COLS].reshape(KT, P, COLS).transpose(1, 0, 2).reshape(P, PANEL)


def rows_panel(w, c):
    return w[c * COLS:(c + 1) * COLS].reshape(2, P, D).transpose(1, 0, 2).reshape(P, PANEL)


def ffn_panels(w_in, w_out):
    yield panel_of(w_in, 0)
    yield panel_of(w_in, FF)
    for c in range(1, FFC):
        yield panel_of(w_in, c * COLS)
        yield panel_of(w_in, FF + c * COLS)
        yield rows_panel(w_out, c - 1)
    yield rows_panel(w_out, FFC - 1)


def gain_columns(g):
    return g.reshape(-1, KT, P).transpose(2, 0, 1).reshape(P, -1)


def lay_out(inp):
    x = np.asarray(inp["x"])[0]
    a = {"x": np.ascontiguousarray(x.T)}
    panels = []
    rows = []
    for i in range(BLOCK1):
        rows += [inp["norm_mix_g"][i], inp["norm_ffn_g"][i]]
        if i % 3 == 0:
            panels += [panel_of(inp["fnet_w_out"][i // 3], c * COLS) for c in range(4)]
        if i % 3 == 1:
            w = inp["s5_w_glu"][i // 3]
            panels += [panel_of(w, c * COLS + m * D) for c in range(4) for m in range(2)]
        if i % 3 == 2:
            w = inp["attn_w_qkv"][i // 3]
            for b in range(HEADS // HB):
                panels += [panel_of(w, (g * 3 + m) * D + b * COLS) for ms in ((0, 1), (2,)) for g in range(NG) for m in ms]
            panels += [panel_of(inp["attn_w_o"][i // 3], c * COLS) for c in range(4)]
        panels += ffn_panels(inp["ffn_w_gate_up"][i], inp["ffn_w_down"][i])
    cols = []
    for i in range(BLOCK2):
        rows += [inp["norm_ffn1_2"][i], inp["norm_mix_2"][i], inp["norm_ffn2_2"][i]]
        panels += ffn_panels(inp["w_ffn1_in_2"][i], inp["w_ffn1_out_2"][i])
        w = inp["w_mix_in_2"][i]
        sizes = (D, CONV_T * P, SSD_H, D, D, D, IDX_H * E, E, IDX_H)
        z, xbc, dt, q, k, v, qi, ki, wi = np.split(w, np.cumsum(sizes)[:-1], 1)
        misc = np.zeros((D, COLS), np.float32)
        misc[:, 0:E], misc[:, E:2 * E] = ki, ki
        misc[:, P:P + SSD_H], misc[:, P + 32:P + 32 + IDX_H] = dt, wi
        for part in (misc, qi, xbc, q, k, z, v, inp["w_mix_out_2"][i][:D], inp["w_mix_out_2"][i][D:]):
            panels += [panel_of(part, c) for c in range(0, part.shape[1], COLS)]
        panels += ffn_panels(inp["w_ffn2_in_2"][i], inp["w_ffn2_out_2"][i])
        tail = np.zeros((P, 3), np.float32)
        tail[:SSD_H, 0], tail[:SSD_H, 1] = inp["dt_bias_2"][i], inp["a_log_2"][i]
        cols.append(np.concatenate([
            inp["conv_w_2"][i].reshape(CONV, CONV_T, P).transpose(2, 1, 0).reshape(P, -1),
            inp["conv_b_2"][i].reshape(CONV_T, P).T,
            np.repeat(inp["d_skip_2"][i], SSD_P).reshape(KT, P).T,
            inp["ssd_norm_2"][i].reshape(KT, P).T, tail], 1))
    a["mix_col"] = np.stack(cols)
    rows.append(inp["final_norm_2"])
    a["gains"] = gain_columns(np.stack(rows))
    tok = np.arange(S).reshape(2, P).T[:, :, None]
    along = np.arange(S)[None, None, :]
    a["mask_tri"] = np.where(along >= tok, 0.0, MASKED).astype(np.float32)
    a["mask_causal"] = np.where(along <= tok, 0.0, MASKED).astype(np.float32)
    a["positions"] = np.broadcast_to(inp["positions_2"], (P, S)).astype(np.int32)

    def freqs(rot):
        return np.float32(ROPE_THETA) ** (-np.arange(0, rot, 2, dtype=np.float32) / np.float32(rot))

    def turned(rot):
        half = rot // 2
        m = np.zeros((rot, rot), np.float32)
        m[np.arange(half) + half, np.arange(half)] = -1
        m[np.arange(half), np.arange(half) + half] = 1
        return m

    a["turn_i"] = np.zeros((P, P), np.float32)
    freq = np.zeros((P, 2), np.float32)
    freq[:ROPE_D, 0] = np.concatenate([-freqs(ROPE_D), freqs(ROPE_D)])
    for half in (0, E):
        a["turn_i"][half:half + ROPE_I, half:half + ROPE_I] = turned(ROPE_I)
        freq[half:half + ROPE_I, 1] = np.tile(freqs(ROPE_I), 2)
    a["rope_freq"] = freq
    k = np.arange(P)
    ang = 2 * np.pi * (np.outer(k, k) % P) / P
    a["dft_ch"] = np.concatenate([np.cos(ang), -np.sin(ang)], 1).astype(np.float32)
    k = np.arange(S)
    ang = 2 * np.pi * (np.outer(k, k) % S) / S
    scale = 1.0 / np.sqrt(S * P)
    a["dft_sq"] = (np.concatenate([np.cos(ang), np.sin(ang)], 1) * scale).astype(np.float32)
    a["rel_bias"] = inp["rel_bias"]
    rel = S - 1 - np.arange(2 * S)
    half = BUCKETS // 2
    exact = half // 2
    n = np.abs(rel)
    large = exact + (np.log(np.maximum(n, 1) / exact) / np.log(MAX_DISTANCE / exact) * (half - exact)).astype(np.int32)
    bucket = (rel > 0) * half + np.where(n < exact, n, np.minimum(large, half - 1))
    a["bucket_onehot"] = (bucket[None] == np.arange(BUCKETS)[:, None]).astype(np.float32)
    allowed = np.stack([(n % dil == 0) & (n // dil <= window // 2 // dil) for window, dil in GROUPS])
    a["group_mask"] = np.repeat(np.where(allowed, 0.0, MASKED).astype(np.float32), HEADS, 0)
    a["pair_ones"] = np.kron(np.eye(2), np.ones((E, E))).astype(np.float32)
    gains = np.concatenate([inp["attn_q_gain"][0], inp["attn_k_gain"][0]])
    a["qk_gain"] = np.tile(gains, (1, 2)).T
    a["ident"] = np.eye(P, dtype=np.float32)

    def s5_columns(w):
        w = w.reshape((2, KT, 4, 2, S5_N) + w.shape[3:])
        w = w.transpose((3, 4, 1, 0, 2) + tuple(range(5, w.ndim)))
        return w.reshape(P, -1)

    lam = [inp["s5_lambda_re"][0], inp["s5_lambda_im"][0],
           np.broadcast_to(inp["s5_log_dt"][0][:, :, None], (2, S5_G, S5_N))]
    a["s5_lam"] = np.concatenate([s5_columns(w) for w in lam], 1)
    a["s5_b"] = np.concatenate([s5_columns(inp["s5_b_" + r][0]) for r in ("re", "im")], 1)
    a["s5_c"] = np.concatenate([s5_columns(inp["s5_c_" + r][0].transpose(0, 1, 3, 2)) for r in ("re", "im")], 1)
    a["s5_d"] = gain_columns(inp["s5_d"])
    return a, panels


def kernel(**inputs):
    import concourse.bacc as bacc
    from concourse.bass_utils import run_bass_kernel_spmd

    data, panels = lay_out({name: np.asarray(value) for name, value in inputs.items()})
    data["panels"] = np.stack(panels + [panels[-1]])
    nc = bacc.Bacc("TRN2", target_bir_lowering=False, num_devices=1)
    arrays = {"in_" + name: np.ascontiguousarray(value) for name, value in data.items()}
    dram = {name: nc.dram_tensor("in_" + name, value.shape, mybir.dt.from_np(value.dtype), kind="ExternalInput").ap()
            for name, value in data.items()}
    out = nc.dram_tensor("out", (D, S), F32, kind="ExternalOutput").ap()
    build(nc, dram, out)
    got = run_bass_kernel_spmd(nc, [arrays], core_ids=[0]).results[0]["out"]
    return np.ascontiguousarray(np.asarray(got).T)[None]
```
